# Optimizing a Trainium2 kernel written in Bass

```python
import math
import jax
import jax.numpy as jnp
from jax import lax
import numpy as np

'''Two layers of a hybrid decoder trunk with parallel head groups (Hymba-style).

Each layer:  x += W_out . concat[FoX heads | Gated-DeltaNet heads | GLA heads](RMSNorm(x))
             x += HierarchicalMoE(RMSNorm(x))
All three token mixers read one combined input projection of the same normalised input,
are strictly causal, and their per-head outputs are concatenated into one output projection.
Input  x: (BATCH, SEQ, D_MODEL) float32.  Output: (BATCH, SEQ, D_MODEL).
'''

D_MODEL = 1024
BATCH = 1
SEQ = 1024
DEPTH = 1

HEAD_DIM = 64
N_HEADS = D_MODEL // HEAD_DIM
D_MIX = N_HEADS * HEAD_DIM
H_FOX = 3 * N_HEADS // 8
H_GDN = 3 * N_HEADS // 8
H_GLA = N_HEADS - H_FOX - H_GDN
FOX_DIM = H_FOX * HEAD_DIM
GDN_DIM = H_GDN * HEAD_DIM
GLA_DK = HEAD_DIM // 2
GLA_DV = HEAD_DIM
GLA_K_DIM = H_GLA * GLA_DK
GLA_V_DIM = H_GLA * GLA_DV
GLA_RANK = 16
GLA_TAU = 16.0
CONV_K = 4
Q_BLOCK = 128
CHUNK = 64
N_GROUPS = 4
EXPERTS_PER_GROUP = 8
N_EXPERTS = N_GROUPS * EXPERTS_PER_GROUP
TOP_K = 2
D_EXPERT = D_MODEL // 2
MOE_BLOCK = 128
RMS_EPS = 1e-6
N_IN = 3 * FOX_DIM + H_FOX + 4 * GDN_DIM + 2 * H_GDN + 2 * GLA_K_DIM + 2 * GLA_V_DIM + GLA_RANK
F32 = jnp.float32

kernel_name = 'hybrid_fox_gdn_gla_hier_moe'

def rms_norm(x, gain):
    xf = x.astype(F32)
    y = xf * lax.rsqrt(jnp.mean(xf * xf, axis=-1, keepdims=True) + RMS_EPS)
    return (y * gain.astype(F32)).astype(x.dtype)

def l2_normalize(x):
    xf = x.astype(F32)
    return (xf * lax.rsqrt(jnp.sum(xf * xf, axis=-1, keepdims=True) + RMS_EPS)).astype(x.dtype)

def causal_depthwise_conv(x, w):
    c = x.shape[-1]
    return lax.conv_general_dilated(x, w[:, None, :].astype(x.dtype), window_strides=(1,),
                                    padding=[(CONV_K - 1, 0)],
                                    dimension_numbers=('NWC', 'WIO', 'NWC'),
                                    feature_group_count=c)

def split_columns(proj):
    sizes = [FOX_DIM, FOX_DIM, FOX_DIM, H_FOX,
             3 * GDN_DIM, GDN_DIM, H_GDN, H_GDN,
             GLA_K_DIM, GLA_K_DIM, GLA_V_DIM, GLA_V_DIM, GLA_RANK]
    idx = np.cumsum(sizes)[:-1].tolist()
    return jnp.split(proj, idx, axis=-1)

def fox_branch(q, k, v, f_logit, q_gain, k_gain, f_bias, o_gain):
    b, s, _ = q.shape
    q = rms_norm(q.reshape(b, s, H_FOX, HEAD_DIM), q_gain)
    k = rms_norm(k.reshape(b, s, H_FOX, HEAD_DIM), k_gain)
    v = v.reshape(b, s, H_FOX, HEAD_DIM)
    log_f = jax.nn.log_sigmoid(f_logit.astype(F32) + f_bias.astype(F32))
    cum = jnp.cumsum(log_f, axis=1).transpose(0, 2, 1)
    nq = s // Q_BLOCK
    q_blocks = q.reshape(b, nq, Q_BLOCK, H_FOX, HEAD_DIM).transpose(1, 0, 2, 3, 4)
    c_blocks = cum.reshape(b, H_FOX, nq, Q_BLOCK).transpose(2, 0, 1, 3)
    key_pos = jnp.arange(s)
    scale = HEAD_DIM ** -0.5

    def attend(args):
        q_i, c_i, blk = args
        logits = (jnp.einsum('bqhd,bkhd->bhqk', q_i, k).astype(F32) * scale
                  + (c_i[..., :, None] - cum[..., None, :]))
        query_pos = blk * Q_BLOCK + jnp.arange(Q_BLOCK)
        logits = jnp.where(key_pos[None, :] <= query_pos[:, None], logits, -jnp.inf)
        p = jax.nn.softmax(logits, axis=-1).astype(v.dtype)
        return jnp.einsum('bhqk,bkhd->bqhd', p, v)

    o = lax.map(attend, (q_blocks, c_blocks, jnp.arange(nq)))
    o = o.transpose(1, 0, 2, 3, 4).reshape(b, s, H_FOX, HEAD_DIM)
    return rms_norm(o, o_gain).reshape(b, s, FOX_DIM)

def gated_delta_rule(q, k, v, g, beta):
    b, s, h, dk = q.shape
    dv = v.shape[-1]
    n = s // CHUNK

    def chunks(t):
        return t.astype(F32).reshape(b, n, CHUNK, h, t.shape[-1]).transpose(0, 3, 1, 2, 4)

    qc, kc, vc = chunks(q), chunks(k), chunks(v)
    gc = g.reshape(b, n, CHUNK, h).transpose(0, 3, 1, 2)
    bc = beta.reshape(b, n, CHUNK, h).transpose(0, 3, 1, 2)
    decay = jnp.cumsum(gc, axis=-1)
    causal = jnp.tril(jnp.ones((CHUNK, CHUNK), bool))
    strict = jnp.tril(jnp.ones((CHUNK, CHUNK), bool), k=-1)
    diff = decay[..., :, None] - decay[..., None, :]
    gamma = jnp.where(causal, jnp.exp(jnp.where(causal, diff, 0.0)), 0.0)
    kb = kc * bc[..., None]
    a_strict = jnp.where(strict, jnp.einsum('bhnid,bhnjd->bhnij', kb, kc) * gamma, 0.0)
    lhs = a_strict + jnp.eye(CHUNK, dtype=F32)
    rhs = jnp.concatenate([vc * bc[..., None], kb * jnp.exp(decay)[..., None]], axis=-1)
    sol = lax.linalg.triangular_solve(lhs, rhs, left_side=True, lower=True)
    u, w = sol[..., :dv], sol[..., dv:]
    intra = jnp.einsum('bhnid,bhnjd->bhnij', qc, kc) * gamma
    q_dec = qc * jnp.exp(decay)[..., None]
    k_dec = kc * jnp.exp(decay[..., -1:] - decay)[..., None]
    last = jnp.exp(decay[..., -1])

    def step(state, xs):
        u_i, w_i, qd_i, kd_i, a_i, last_i = xs
        v_new = u_i - jnp.einsum('bhcd,bhde->bhce', w_i, state)
        o = jnp.einsum('bhcd,bhde->bhce', qd_i, state) + jnp.einsum('bhij,bhje->bhie', a_i, v_new)
        state = state * last_i[..., None, None] + jnp.einsum('bhcd,bhce->bhde', kd_i, v_new)
        return state, o

    xs = tuple(jnp.moveaxis(t, 2, 0) for t in (u, w, q_dec, k_dec, intra, last))
    _, o = lax.scan(step, jnp.zeros((b, h, dk, dv), F32), xs)
    return o.transpose(1, 0, 3, 2, 4).reshape(b, s, h, dv)

def gdn_branch(qkv, gate, a, beta_logit, conv_w, a_log, dt_bias, o_gain):
    b, s, _ = qkv.shape
    qkv = jax.nn.silu(causal_depthwise_conv(qkv, conv_w))
    q, k, v = jnp.split(qkv, 3, axis=-1)
    q = l2_normalize(q.reshape(b, s, H_GDN, HEAD_DIM)) * (HEAD_DIM ** -0.5)
    k = l2_normalize(k.reshape(b, s, H_GDN, HEAD_DIM))
    v = v.reshape(b, s, H_GDN, HEAD_DIM)
    g = -jnp.exp(a_log.astype(F32)) * jax.nn.softplus(a.astype(F32) + dt_bias.astype(F32))
    beta = jax.nn.sigmoid(beta_logit.astype(F32))
    o = gated_delta_rule(q, k, v, g, beta).astype(qkv.dtype)
    o = rms_norm(o, o_gain) * jax.nn.silu(gate.reshape(b, s, H_GDN, HEAD_DIM))
    return o.reshape(b, s, GDN_DIM)

def gla_chunked(q, k, v, log_a):
    b, s, h, dk = q.shape
    dv = v.shape[-1]
    n = s // CHUNK

    def chunks(t):
        return t.astype(F32).reshape(b, n, CHUNK, h, t.shape[-1]).transpose(1, 0, 3, 2, 4)

    qc, kc, vc = chunks(q), chunks(k), chunks(v)
    bcum = jnp.cumsum(chunks(log_a), axis=3)
    causal = jnp.tril(jnp.ones((CHUNK, CHUNK), bool))[..., None]

    def step(state, xs):
        q_i, k_i, v_i, b_i = xs
        diff = b_i[:, :, :, None, :] - b_i[:, :, None, :, :]
        dec = jnp.where(causal, jnp.exp(jnp.where(causal, diff, 0.0)), 0.0)
        scores = jnp.einsum('bhid,bhjd,bhijd->bhij', q_i, k_i, dec)
        o = (jnp.einsum('bhid,bhde->bhie', q_i * jnp.exp(b_i), state)
             + jnp.einsum('bhij,bhje->bhie', scores, v_i))
        b_last = b_i[:, :, -1:, :]
        state = (state * jnp.exp(b_last[:, :, 0, :, None])
                 + jnp.einsum('bhjd,bhje->bhde', k_i * jnp.exp(b_last - b_i), v_i))
        return state, o

    _, o = lax.scan(step, jnp.zeros((b, h, dk, dv), F32), (qc, kc, vc, bcum))
    return o.transpose(1, 0, 3, 2, 4).reshape(b, s, h, dv)

def gla_branch(q, k, v, r, a1, w_a2, b_a, o_gain):
    b, s, _ = q.shape
    q = q.reshape(b, s, H_GLA, GLA_DK) * (GLA_DK ** -0.5)
    k = k.reshape(b, s, H_GLA, GLA_DK)
    v = v.reshape(b, s, H_GLA, GLA_DV)
    log_a = jax.nn.log_sigmoid((a1 @ w_a2 + b_a).astype(F32)) / GLA_TAU
    log_a = log_a.reshape(b, s, H_GLA, GLA_DK)
    o = gla_chunked(q, k, v, log_a).astype(q.dtype)
    o = rms_norm(o, o_gain) * jax.nn.silu(r.reshape(b, s, H_GLA, GLA_DV))
    return o.reshape(b, s, GLA_V_DIM)

def token_mixer(h, w_in, fox_q_norm, fox_k_norm, fox_f_bias, fox_o_norm,
                gdn_conv, gdn_a_log, gdn_dt_bias, gdn_o_norm,
                gla_w_a2, gla_b_a, gla_o_norm, w_out):
    proj = h @ w_in
    (fq, fk, fv, ff, gqkv, ggate, ga, gb, lq, lk, lv, lr, la1) = split_columns(proj)
    o_fox = fox_branch(fq, fk, fv, ff, fox_q_norm, fox_k_norm, fox_f_bias, fox_o_norm)
    o_gdn = gdn_branch(gqkv, ggate, ga, gb, gdn_conv, gdn_a_log, gdn_dt_bias, gdn_o_norm)
    o_gla = gla_branch(lq, lk, lv, lr, la1, gla_w_a2, gla_b_a, gla_o_norm)
    return jnp.concatenate([o_fox, o_gdn, o_gla], axis=-1) @ w_out

def expert_dispatch(hf, expert_id, gate, w_g, w_u, w_d):
    n, d = hf.shape
    nk = n * TOP_K
    flat_e = expert_id.reshape(-1)
    flat_tok = jnp.repeat(jnp.arange(n, dtype=jnp.int32), TOP_K)
    flat_g = gate.reshape(-1).astype(hf.dtype)
    order = jnp.argsort(flat_e)
    e_sorted, tok_sorted, g_sorted = flat_e[order], flat_tok[order], flat_g[order]
    counts = jnp.bincount(flat_e, length=N_EXPERTS)
    starts = jnp.cumsum(counts) - counts
    padded = (counts + MOE_BLOCK - 1) // MOE_BLOCK * MOE_BLOCK
    pends = jnp.cumsum(padded)
    pstarts = pends - padded
    dest = pstarts[e_sorted] + (jnp.arange(nk) - starts[e_sorted])
    n_rows = -(-nk // MOE_BLOCK) * MOE_BLOCK + N_EXPERTS * MOE_BLOCK
    n_blocks = n_rows // MOE_BLOCK
    row_tok = jnp.full((n_rows,), n, jnp.int32).at[dest].set(tok_sorted)
    row_gate = jnp.zeros((n_rows,), hf.dtype).at[dest].set(g_sorted)
    block_e = jnp.minimum(jnp.searchsorted(pends, jnp.arange(n_blocks) * MOE_BLOCK, side='right'),
                          N_EXPERTS - 1)
    h_pad = jnp.concatenate([hf, jnp.zeros((1, d), hf.dtype)], axis=0)
    xb = h_pad[row_tok].reshape(n_blocks, MOE_BLOCK, d)

    def run_block(args):
        x_blk, e = args
        return (jax.nn.silu(x_blk @ w_g[e]) * (x_blk @ w_u[e])) @ w_d[e]

    yb = lax.map(run_block, (xb, block_e)).reshape(n_rows, d)
    y = jnp.zeros((n + 1, d), hf.dtype).at[row_tok].add(yb * row_gate[:, None])
    return y[:n]

def hierarchical_moe(h, w_rg, b_rg, w_re, b_re, w_g, w_u, w_d):
    b, s, d = h.shape
    n = b * s
    hf = h.reshape(n, d)
    group_prob = jax.nn.softmax((hf @ w_rg).astype(F32) + b_rg.astype(F32), axis=-1)
    group_p, group_idx = lax.top_k(group_prob, 1)
    expert_logits = ((hf @ w_re).astype(F32) + b_re.astype(F32)).reshape(n, N_GROUPS, EXPERTS_PER_GROUP)
    sel = jnp.broadcast_to(group_idx[:, :, None], (n, 1, EXPERTS_PER_GROUP))
    in_group = jnp.take_along_axis(expert_logits, sel, axis=1)[:, 0]
    top_p, top_idx = lax.top_k(jax.nn.softmax(in_group, axis=-1), TOP_K)
    gate = group_p * top_p / jnp.sum(top_p, axis=-1, keepdims=True)
    expert_id = group_idx * EXPERTS_PER_GROUP + top_idx
    return expert_dispatch(hf, expert_id, gate, w_g, w_u, w_d).reshape(b, s, d)

def setup_inputs(seed: int = 0) -> dict:
    key = jax.random.key(seed)
    ks = jax.random.split(key, 24)
    L = DEPTH

    def normal(k, shape, scale):
        return jax.random.normal(k, shape, F32) * scale

    def gain(k, shape):
        return 1.0 + 0.1 * jax.random.normal(k, shape, F32)

    dt = jnp.exp(jax.random.uniform(ks[9], (L, H_GDN), F32, math.log(1e-3), math.log(1e-1)))
    return {
        'x': normal(ks[0], (BATCH, SEQ, D_MODEL), 1.0),
        'attn_norm': gain(ks[1], (L, D_MODEL)),
        'w_in': normal(ks[2], (L, D_MODEL, N_IN), D_MODEL ** -0.5),
        'fox_q_norm': gain(ks[3], (L, HEAD_DIM)),
        'fox_k_norm': gain(ks[4], (L, HEAD_DIM)),
        'fox_f_bias': jax.random.uniform(ks[5], (L, H_FOX), F32, 1.0, 4.0),
        'fox_o_norm': gain(ks[6], (L, HEAD_DIM)),
        'gdn_conv': normal(ks[7], (L, CONV_K, 3 * GDN_DIM), CONV_K ** -0.5),
        'gdn_a_log': jnp.log(jax.random.uniform(ks[8], (L, H_GDN), F32, 1.0, 16.0)),
        'gdn_dt_bias': dt + jnp.log(-jnp.expm1(-dt)),
        'gdn_o_norm': gain(ks[10], (L, HEAD_DIM)),
        'gla_w_a2': normal(ks[11], (L, GLA_RANK, GLA_K_DIM), GLA_RANK ** -0.5),
        'gla_b_a': normal(ks[12], (L, GLA_K_DIM), 0.1),
        'gla_o_norm': gain(ks[13], (L, GLA_DV)),
        'w_out': normal(ks[14], (L, D_MIX, D_MODEL), D_MIX ** -0.5),
        'ffn_norm': gain(ks[15], (L, D_MODEL)),
        'w_router_group': normal(ks[16], (L, D_MODEL, N_GROUPS), D_MODEL ** -0.5),
        'b_router_group': normal(ks[17], (L, N_GROUPS), 0.01),
        'w_router_expert': normal(ks[18], (L, D_MODEL, N_EXPERTS), D_MODEL ** -0.5),
        'b_router_expert': normal(ks[19], (L, N_EXPERTS), 0.01),
        'w_expert_gate': normal(ks[20], (L, N_EXPERTS, D_MODEL, D_EXPERT), D_MODEL ** -0.5),
        'w_expert_up': normal(ks[21], (L, N_EXPERTS, D_MODEL, D_EXPERT), D_MODEL ** -0.5),
        'w_expert_down': normal(ks[22], (L, N_EXPERTS, D_EXPERT, D_MODEL), D_EXPERT ** -0.5),
    }

def reference(x, attn_norm, w_in, fox_q_norm, fox_k_norm, fox_f_bias, fox_o_norm,
              gdn_conv, gdn_a_log, gdn_dt_bias, gdn_o_norm,
              gla_w_a2, gla_b_a, gla_o_norm, w_out,
              ffn_norm, w_router_group, b_router_group, w_router_expert, b_router_expert,
              w_expert_gate, w_expert_up, w_expert_down):
    for layer in range(DEPTH):
        h = rms_norm(x, attn_norm[layer])
        x = x + token_mixer(h, w_in[layer], fox_q_norm[layer], fox_k_norm[layer],
                            fox_f_bias[layer], fox_o_norm[layer],
                            gdn_conv[layer], gdn_a_log[layer], gdn_dt_bias[layer], gdn_o_norm[layer],
                            gla_w_a2[layer], gla_b_a[layer], gla_o_norm[layer], w_out[layer])
        h = rms_norm(x, ffn_norm[layer])
        x = x + hierarchical_moe(h, w_router_group[layer], b_router_group[layer],
                                 w_router_expert[layer], b_router_expert[layer],
                                 w_expert_gate[layer], w_expert_up[layer], w_expert_down[layer])
    return x


_drawn_inputs = setup_inputs


def setup_inputs(seed=0):
    import zlib

    import numpy as np

    out = dict(_drawn_inputs(seed))
    spreads = {}
    factors = {'gla_b_a': 2.997, 'b_router_group': 5.972, 'b_router_expert': 4.442}
    for name, (base, spread) in spreads.items():
        noise = np.random.default_rng([zlib.crc32(name.encode()), seed]).standard_normal(out[name].shape)
        drawn = base * np.exp(spread * noise) if base else spread * noise
        out[name] = jnp.asarray(drawn.astype(out[name].dtype))
    for name, factor in factors.items():
        out[name] = (out[name] * factor).astype(out[name].dtype)
    return out
```

```python
import math
from contextlib import ExitStack

import concourse.bass as bass
from concourse import mybir

P = 128
S = 1024
D = 1024
KD = D // P
NT = S // P
HD = 64
H_FOX, H_GDN, H_GLA = 6, 6, 4
FOX, GDN = H_FOX * HD, H_GDN * HD
DK, GK, GV = 32, 128, 256
RANK = 16
NG, EPG, NE = 4, 8, 32
DE = 512
EPS = 1e-6
NEG = -1e30
MAXB = NE + 2 * S // P - 1
LST = 48

F32 = mybir.dt.float32
BF16 = mybir.dt.bfloat16
I32 = mybir.dt.int32
U32 = mybir.dt.uint32
ALU = mybir.AluOpType
ACT = mybir.ActivationFunctionType
AX = mybir.AxisListType

C_FQ, C_FK, C_FV = 0, FOX, 2 * FOX
C_GQKV = 3 * FOX + H_FOX
C_GATE = C_GQKV + 3 * GDN
C_LQ = C_GATE + GDN + 2 * H_GDN
C_LV = C_LQ + 2 * GK
C_LA = C_LV + 2 * GV
N_IN = C_LA + RANK
W_VF = FOX + H_FOX
W_GAB = GDN + 2 * H_GDN

(K_ID, K_U, K_L, K_ONE, K_LM) = (0, 1, 2, 3, 4)
K_BD = 11
K_HO = 13
K_IOTA = 14
NKC = 15
PC = {}
_at = 0
for _n, _w in (("attn_gain", KD), ("ffn_gain", KD), ("fox_q", HD), ("fox_k", HD), ("fox_o", HD), ("gdn_o", HD),
               ("gla_o", HD), ("f_bias", H_FOX), ("dt_bias", H_GDN), ("a_log", H_GDN), ("conv", 36),
               ("b_rg", NG), ("b_re", NE), ("b_a", GK)):
    PC[_n] = (_at, _at + _w)
    _at += _w
NPC = _at


class Steps:

    def __init__(self, eng, sem):
        self.eng, self.sem, self.n = eng, sem, 0

    def done(self, ins):
        self.n += 1
        ins.then_inc(self.sem, 1)
        self.eng.wait_ge(self.sem, self.n)


def trunk_kernel(nc, x, w_in, w_out, w_router, w_a2, w_g, w_u, w_d, params, consts, masks, out):
    ctx = ExitStack()

    names = {}

    def sb(name, shape, dt=F32, c=None):
        names[name] = names.get(name, -1) + 1
        name += f"_{names[name]}" if names[name] else ""
        return (c or ctx).enter_context(nc.sbuf_tensor(name, shape, dt))

    phase_sems = [None]

    def sem(name):
        handle = nc.alloc_semaphore(name)
        if phase_sems[0] is not None:
            phase_sems[0].append(handle)
        return handle

    def new_phase(c):
        phase_sems[0] = []
        c.callback(end_phase)

    def end_phase():
        nc.clear_and_free_semaphores(phase_sems[0])
        nc.all_engine_barrier()
        phase_sems[0] = None

    with ctx:
        PS = ctx.enter_context(nc.psum_tensor("PS", [P, 8, 512], F32))
        kc = sb("kc", [P, NKC, P])
        km = sb("km", [P, 5, P], BF16)
        prm = sb("prm", [P, NPC])
        eps = sb("eps", [P, 1])
        wring = [sb(f"wring{i}", [P, KD, 512]) for i in range(3)]
        hT = sb("hT", [P, KD, S])
        mix = sb("mix", [P, NT, D])
        h2_dram = nc.dram_tensor("h2_scratch", (S, D), F32, kind="Internal").ap()
        y_dram = nc.dram_tensor("y_scratch", (MAXB * P, D), F32, kind="Internal").ap()
        list_dram = nc.dram_tensor("list_scratch", (LST * P, 1), F32, kind="Internal").ap()

        ident, U, L, ones = (kc[:, i, :] for i in (K_ID, K_U, K_L, K_ONE))
        identb, mask_q, mask_incl, mask_strict, before = (km[:, i, :] for i in range(5))

        def par(name):
            a, b = PC[name]
            return prm[:, a:b]

        w_loaded = [sem(f"w_loaded{i}") for i in range(3)]
        w_used = sem("w_used")
        const_loaded = sem("const_loaded")

        w_in_v = w_in.rearrange("(k p) n -> p k n", p=P)
        w_out_v = w_out.rearrange("(k p) n -> p k n", p=P)
        chunks = [[(w_in_v[:, :, a:b], 0)] for a, b in
                  ((C_FV, C_FV + W_VF), (C_FQ, C_FK), (C_FK, C_FV),
                   (C_GQKV, C_GQKV + 512), (C_GQKV + 512, C_GQKV + 1024), (C_GQKV + 1024, C_GATE),
                   (C_GATE, C_LQ), (C_LQ, C_LV), (C_LV, C_LA))]
        chunks[7].append((w_in_v[:, :, C_LA:N_IN], 2 * GK))
        chunks += [[(w_out_v[:, :, a:a + 512], 0)] for a in (0, 512)]
        CH_VF, CH_Q, CH_K, CH_T0, CH_T1, CH_T2, CH_GAB, CH_L, CH_LVR, CH_O0, CH_O1 = range(11)
        n_loads, seen = [], [0, 0, 0]
        for c, parts in enumerate(chunks):
            seen[c % 3] += 16 * len(parts)
            n_loads.append(seen[c % 3])

        def load_chunk(eng, c):
            if c >= 3:
                eng.wait_ge(w_used, c - 2)
            for src, at in chunks[c]:
                eng.dma_start(wring[c % 3][:, :, at:at + src.shape[2]], src).then_inc(w_loaded[c % 3], 16)

        def chunk_ready(eng, c):
            eng.wait_ge(w_loaded[c % 3], n_loads[c])

        def project_tile(pe, c, n, bank, cols):
            for k in range(KD):
                mm = pe.matmul(PS[:, bank, 0:cols], hT[:, k, n * P:(n + 1) * P], wring[c % 3][:, k, 0:cols],
                               start=(k == 0), stop=(k == KD - 1))
            return mm

        with ExitStack() as c, nc.Block() as block:
            new_phase(c)
            xin = sb("xin", [P, 2, D], c=c)
            junk = sb("junk", [P, D], c=c)
            ss = sb("ss", [P, NT], c=c)
            lnss = sb("lnss", [P, NT], c=c)
            rstd = sb("rstd", [P, NT], c=c)
            x_loaded = [sem("x_loaded0"), sem("x_loaded1")]
            rstd_ready, act_step = sem("rstd_ready"), sem("act_step")
            h_ready, h_turned, hT_ready, eps_ready = sem("h_ready"), sem("h_turned"), sem("hT_ready"), sem("eps_ready")

            @block.sync
            def _(sp):
                sp.dma_start(xin[:, 0, :], x[0:P, :]).then_inc(x_loaded[0], 16)
                sp.dma_start(xin[:, 1, :], x[P:2 * P, :]).then_inc(x_loaded[1], 16)
                sp.dma_start(prm[:, :], params).then_inc(const_loaded, 16)
                sp.dma_start(kc[:, :, :], consts).then_inc(const_loaded, 16)
                sp.dma_start(km[:, :, :], masks).then_inc(const_loaded, 16)
                for k in range(3):
                    load_chunk(sp, k)
                for n in range(2, NT):
                    sp.wait_ge(h_turned, 2 * (n - 1))
                    sp.dma_start(xin[:, n % 2, :], x[n * P:(n + 1) * P, :]).then_inc(x_loaded[n % 2], 16)

            @block.gpsimd
            def _(pool):
                pool.memset(eps[:, :], EPS).then_inc(eps_ready, 1)

            @block.scalar
            def _(act):
                st = Steps(act, act_step)
                act.wait_ge(eps_ready, 1)
                act.preload_act_table_set("natural_log_exp_and_others")
                for n in range(NT):
                    act.wait_ge(x_loaded[n % 2], 16 * (n // 2 + 1))
                    st.done(act.activation(junk[:, :], xin[:, n % 2, :], ACT.Square, accum_out=ss[:, n:n + 1]))
                    st.done(act.activation(lnss[:, n:n + 1], ss[:, n:n + 1], ACT.Ln, bias=eps[:, :], scale=1.0 / D))
                    act.activation(rstd[:, n:n + 1], lnss[:, n:n + 1], ACT.Exp, scale=-0.5).then_inc(rstd_ready, 1)

            @block.vector
            def _(dve):
                dve.wait_ge(const_loaded, 48)
                for n in range(NT):
                    dve.wait_ge(rstd_ready, n + 1)
                    dve.tensor_scalar(xin[:, n % 2, :], xin[:, n % 2, :], rstd[:, n:n + 1], None, ALU.mult).then_inc(h_ready, 1)
                    for b in range(2):
                        dve.wait_ge(h_turned, 2 * n + b + 1)
                        bank = 2 * (n % 2) + b
                        g = par("attn_gain")[:, 4 * b:4 * b + 4].unsqueeze(2).to_broadcast([P, 4, P])
                        dve.tensor_tensor(hT[:, 4 * b:4 * b + 4, n * P:(n + 1) * P],
                                          PS[:, bank, :].rearrange("p (k t) -> p k t", k=4), g, ALU.mult).then_inc(hT_ready, 1)

            @block.tensor
            def _(pe):
                pe.wait_ge(const_loaded, 48)
                for n in range(NT):
                    pe.wait_ge(h_ready, n + 1)
                    for b in range(2):
                        if n >= 2:
                            pe.wait_ge(hT_ready, 2 * (n - 2) + b + 1)
                        for k in range(4):
                            kk = 4 * b + k
                            t = pe.transpose(PS[:, 2 * (n % 2) + b, k * P:(k + 1) * P],
                                             xin[:, n % 2, kk * P:(kk + 1) * P], ident)
                        t.then_inc(h_turned, 1)

        with ExitStack() as fc:
            vf = sb("vf", [P, NT, W_VF], c=fc)
            qT = sb("qT", [HD + 1, H_FOX, S], c=fc)
            kT = sb("kT", [HD + 1, H_FOX, S], c=fc)
            with ExitStack() as c, nc.Block() as block:
                new_phase(c)
                fx = sb("fx", [P, NT, H_FOX], c=c)
                fmin = sb("fmin", [P, NT, H_FOX], c=c)
                fexp = sb("fexp", [P, NT, H_FOX], c=c)
                carry = sb("carry", [P, NT, H_FOX], c=c)
                cum8 = sb("cum8", [P, NT, H_FOX], c=c)
                sq = sb("sq", [P, 2, FOX], c=c)
                qn = sb("qn", [P, 2, H_FOX, HD + 1], c=c)
                ss = sb("ss", [P, 2, H_FOX], c=c)
                lns = sb("lns", [P, 2, H_FOX], c=c)
                rq = sb("rq", [P, 2, H_FOX], c=c)
                proj_ready, vf_ready, sq_ready, ss_ready = sem("fproj"), sem("vf_ready"), sem("fsq"), sem("fss")
                r_ready, qn_ready, qn_turned, qT_ready = sem("fr"), sem("fqn"), sem("fqnt"), sem("fqT")
                fx_ready, lf_act, lf_ready, cs_ready, cum_ready = (sem("ffx"), sem("lf_act"), sem("lf_ready"),
                                                                   sem("cs_ready"), sem("cum_ready"))
                dstep, astep = sem("f_dve_step"), sem("f_act_step")
                UNITS = [(c_, n) for c_ in (CH_Q, CH_K) for n in range(NT)]

                @block.sync
                def _(sp):
                    for k in range(3, 6):
                        load_chunk(sp, k)

                @block.tensor
                def _(pe):
                    chunk_ready(pe, CH_VF)
                    for n in range(NT):
                        if n >= 2:
                            pe.wait_ge(vf_ready, n - 1)
                        mm = project_tile(pe, CH_VF, n, n % 2, W_VF)
                        mm.then_inc(proj_ready, 1)
                        if n == NT - 1:
                            pe.wait_ge(proj_ready, NT)
                            pe.nop().then_inc(w_used, 1)

                    def turn(u):
                        pe.wait_ge(qn_ready, u + 1)
                        for b in range(2):
                            if u >= 1:
                                pe.wait_ge(qT_ready, 2 * (u - 1) + b + 1)
                            for j in range(3):
                                t = pe.transpose(PS[0:HD + 1, 4 + b, j * P:(j + 1) * P], qn[:, u % 2, 3 * b + j, :], ident)
                            t.then_inc(qn_turned, 1)

                    for u, (ch, n) in enumerate(UNITS):
                        if n == 0:
                            chunk_ready(pe, ch)
                        if u >= 2:
                            pe.wait_ge(qn_ready, u - 1)
                        else:
                            pe.wait_ge(vf_ready, NT)
                        mm = project_tile(pe, ch, n, u % 2, FOX)
                        mm.then_inc(proj_ready, 1)
                        if n == NT - 1:
                            pe.wait_ge(proj_ready, NT + u + 1)
                            pe.nop().then_inc(w_used, 1)
                        if u == 1:
                            pe.wait_ge(lf_ready, 1)
                            lf = fx[:, :, :].rearrange("p n h -> p (n h)")
                            pe.matmul(PS[:, 6, 0:NT * H_FOX], U, lf, start=True, stop=True)
                            pe.matmul(PS[:, 7, 0:NT * H_FOX], ones, lf, start=True, stop=True).then_inc(cs_ready, 1)
                        if u >= 1:
                            turn(u - 1)
                    turn(len(UNITS) - 1)

                @block.scalar
                def _(act):
                    st = Steps(act, astep)
                    for n in range(NT):
                        act.wait_ge(proj_ready, n + 1)
                        act.activation(vf[:, n, :], PS[:, n % 2, 0:W_VF], ACT.Copy).then_inc(vf_ready, 1)
                    act.wait_ge(fx_ready, 1)
                    st.done(act.activation(fexp[:, :, :], fx[:, :, :], ACT.Abs))
                    st.done(act.activation(fexp[:, :, :], fexp[:, :, :], ACT.Exp, scale=-1.0))
                    act.activation(fexp[:, :, :], fexp[:, :, :], ACT.Ln, bias=1.0).then_inc(lf_act, 1)

                    def evac(u):
                        ch, n = UNITS[u]
                        dst = qT if ch == CH_Q else kT
                        for b in range(2):
                            act.wait_ge(qn_turned, 2 * u + b + 1)
                            act.activation(dst[:, 3 * b:3 * b + 3, n * P:(n + 1) * P],
                                           PS[0:HD + 1, 4 + b, 0:3 * P].rearrange("p (h t) -> p h t", h=3),
                                           ACT.Copy).then_inc(qT_ready, 1)

                    for u, (ch, n) in enumerate(UNITS):
                        i = u % 2
                        act.wait_ge(proj_ready, NT + u + 1)
                        if u >= 2:
                            act.wait_ge(ss_ready, u - 1)
                        act.activation(sq[:, i, :], PS[:, i, 0:FOX], ACT.Square).then_inc(sq_ready, 1)
                        act.wait_ge(ss_ready, u + 1)
                        st.done(act.activation(lns[:, i, :], ss[:, i, :], ACT.Ln, bias=eps[:, :], scale=1.0 / HD))
                        if u >= 2:
                            act.wait_ge(qn_ready, u - 1)
                        act.activation(rq[:, i, :], lns[:, i, :], ACT.Exp, scale=-0.5).then_inc(r_ready, 1)
                        if u >= 1:
                            evac(u - 1)
                    evac(len(UNITS) - 1)

                @block.vector
                def _(dve):
                    st = Steps(dve, dstep)
                    st.done(dve.memset(qn[:, :, :, :], 1.0))
                    dve.wait_ge(vf_ready, NT)
                    fb = par("f_bias").unsqueeze(1).to_broadcast([P, NT, H_FOX])
                    dve.tensor_tensor(fx[:, :, :], vf[:, :, FOX:W_VF], fb, ALU.add).then_inc(fx_ready, 1)
                    dve.wait_ge(fx_ready, 1)
                    st.done(dve.tensor_scalar(fmin[:, :, :], fx[:, :, :], 0.0, None, ALU.min))
                    dve.wait_ge(lf_act, 1)
                    dve.tensor_tensor(fx[:, :, :], fmin[:, :, :], fexp[:, :, :], ALU.subtract).then_inc(lf_ready, 1)

                    def cumulate():
                        dve.wait_ge(cs_ready, 1)
                        st.done(dve.memset(carry[:, 0, :], 0.0))
                        tot = PS[:, 7, 0:NT * H_FOX].rearrange("p (n h) -> p n h", h=H_FOX)
                        for n in range(1, NT):
                            st.done(dve.tensor_tensor(carry[:, n, :], carry[:, n - 1, :], tot[:, n - 1, :], ALU.add))
                        st.done(dve.tensor_tensor(cum8[:, :, :], carry[:, :, :],
                                                  PS[:, 6, 0:NT * H_FOX].rearrange("p (n h) -> p n h", h=H_FOX), ALU.add))
                        st.done(dve.tensor_scalar(cum8[:, :, :], cum8[:, :, :], -float(HD) ** 0.5, None, ALU.mult))

                    for u, (ch, n) in enumerate(UNITS):
                        i = u % 2
                        dve.wait_ge(sq_ready, u + 1)
                        dve.tensor_reduce(ss[:, i, :], sq[:, i, :].rearrange("p (h d) -> p h d", h=H_FOX), AX.X,
                                          ALU.add).then_inc(ss_ready, 1)
                        if u == 1:
                            cumulate()
                        dve.wait_ge(r_ready, u + 1)
                        if u >= 2:
                            dve.wait_ge(qn_turned, 2 * (u - 1))
                        rows = qn[:, i, :, 0:HD]
                        st.done(dve.tensor_tensor(rows, PS[:, i, 0:FOX].rearrange("p (h d) -> p h d", h=H_FOX),
                                                  rq[:, i, :].unsqueeze(2).to_broadcast([P, H_FOX, HD]), ALU.mult))
                        if ch == CH_K:
                            st.done(dve.tensor_copy(qn[:, i, :, HD], cum8[:, n, :]))
                        g = par("fox_q" if ch == CH_Q else "fox_k").unsqueeze(1).to_broadcast([P, H_FOX, HD])
                        dve.tensor_tensor(rows, rows, g, ALU.mult).then_inc(qn_ready, 1)

            with ExitStack() as c, nc.Block() as block:
                new_phase(c)
                pr = sb("pr", [P, 2, S], c=c)
                prT = sb("prT", [P, 2, 4, P], c=c)
                mx = sb("mx", [P, 2], c=c)
                den = sb("den", [P, 2], c=c)
                rden = sb("rden", [P, 2], c=c)
                sq = sb("sq2", [P, FOX], c=c)
                ss = sb("ss2", [P, H_FOX], c=c)
                rr = sb("rr2", [P, H_FOX], c=c)
                logits, mx_ready, p_ready = sem("logits"), sem("mx_ready"), sem("p_ready")
                p_turned, pT_ready, pv_ready, o_ready = sem("p_turned"), sem("pT_ready"), sem("pv_ready"), sem("o_ready")
                osq_ready, oss_ready, orr_ready, on_ready = sem("osq"), sem("oss"), sem("orr"), sem("on")
                dstep, astep = sem("a_dve_step"), sem("a_act_step")
                ATT = [(n, h) for n in range(NT) for h in range(H_FOX)]
                GR = [(u, g) for u, (n, h) in enumerate(ATT) for g in range((n + 4) // 4)]
                G0 = [sum(1 for x_ in GR if x_[0] < u) for u in range(len(ATT) + 1)]

                @block.sync
                def _(sp):
                    pass

                @block.tensor
                def _(pe):
                    def qk(u):
                        n, h = ATT[u]
                        i = u % 2
                        if u >= 2:
                            pe.wait_ge(p_ready, u - 1)
                        keys = (n + 1) * P
                        for a in range(0, keys, 512):
                            w = min(512, keys - a)
                            last = a + w == keys
                            mm = pe.matmul(PS[:, 2 * i + a // 512, 0:w], qT[:, h, n * P:(n + 1) * P], kT[:, h, a:a + w],
                                           start=True, stop=not last)
                        pe.matmul(PS[:, 2 * i + (keys - 1) // 512, w - P:w], identb, mask_q, start=False, stop=True)\
                          .then_inc(logits, 1)

                    def turn_pv(u):
                        n, h = ATT[u]
                        i = u % 2
                        for g in range((n + 4) // 4):
                            G = G0[u] + g
                            if g == 0:
                                pe.wait_ge(p_ready, u + 1)
                            if G >= 2:
                                pe.wait_ge(pT_ready, G - 1)
                            k0, k1 = 4 * g, min(4 * g + 4, n + 1)
                            for k in range(k0, k1):
                                t = pe.transpose(PS[:, 4 + G % 2, (k - k0) * P:(k - k0 + 1) * P], pr[:, i, k * P:(k + 1) * P], ident)
                            t.then_inc(p_turned, 1)

                    def pv(u):
                        n, h = ATT[u]
                        i = u % 2
                        if u >= 2:
                            pe.wait_ge(o_ready, u - 1)
                        for g in range((n + 4) // 4):
                            G = G0[u] + g
                            pe.wait_ge(pT_ready, G + 1)
                            k0, k1 = 4 * g, min(4 * g + 4, n + 1)
                            for k in range(k0, k1):
                                mm = pe.matmul(PS[:, 6 + i, 0:HD], prT[:, G % 2, k - k0, :], vf[:, k, h * HD:(h + 1) * HD],
                                               start=(k == 0), stop=(k == n))
                        mm.then_inc(pv_ready, 1)

                    for u in range(len(ATT)):
                        qk(u)
                        if u >= 1:
                            turn_pv(u - 1)
                            pv(u - 1)
                    turn_pv(len(ATT) - 1)
                    pv(len(ATT) - 1)

                def norm_act(act, st, n):
                    act.wait_ge(o_ready, H_FOX * (n + 1))
                    if n >= 1:
                        act.wait_ge(on_ready, n)
                    act.activation(sq[:, :], mix[:, n, 0:FOX], ACT.Square).then_inc(osq_ready, 1)
                    act.wait_ge(oss_ready, n + 1)
                    st.done(act.activation(rr[:, :], ss[:, :], ACT.Ln, bias=eps[:, :], scale=1.0 / HD))
                    act.activation(rr[:, :], rr[:, :], ACT.Exp, scale=-0.5).then_inc(orr_ready, 1)

                @block.scalar
                def _(act):
                    st = Steps(act, astep)
                    for u, (n, h) in enumerate(ATT):
                        i = u % 2
                        keys = (n + 1) * P
                        act.wait_ge(mx_ready, u + 1)
                        if u >= 2:
                            act.wait_ge(pv_ready, u - 1)
                            act.wait_ge(o_ready, u - 1)
                        lg = PS[:, 2 * i:2 * i + 2, :].rearrange("p b k -> p (b k)")[:, 0:keys]
                        act.activation(pr[:, i, 0:keys], lg, ACT.Exp, bias=mx[:, i:i + 1], scale=float(HD) ** -0.5,
                                       accum_out=den[:, i:i + 1]).then_inc(p_ready, 1)
                        if h == H_FOX - 1 and n >= 1:
                            norm_act(act, st, n - 1)
                    norm_act(act, st, NT - 1)

                @block.vector
                def _(dve):
                    st = Steps(dve, dstep)

                    def norm(n):
                        dve.wait_ge(osq_ready, n + 1)
                        dve.tensor_reduce(ss[:, :], sq[:, :].rearrange("p (h d) -> p h d", h=H_FOX), AX.X, ALU.add)\
                           .then_inc(oss_ready, 1)
                        dve.wait_ge(orr_ready, n + 1)
                        o = mix[:, n, 0:FOX].rearrange("p (h d) -> p h d", h=H_FOX)
                        st.done(dve.tensor_tensor(o, o, rr[:, :].unsqueeze(2).to_broadcast([P, H_FOX, HD]), ALU.mult))
                        dve.tensor_tensor(o, o, par("fox_o").unsqueeze(1).to_broadcast([P, H_FOX, HD]), ALU.mult)\
                           .then_inc(on_ready, 1)

                    def finish(u):
                        n, h = ATT[u]
                        i = u % 2
                        for g in range((n + 4) // 4):
                            G = G0[u] + g
                            w = (min(4 * g + 4, n + 1) - 4 * g) * P
                            dve.wait_ge(p_turned, G + 1)
                            if G >= 2:
                                dve.wait_ge(pv_ready, GR[G - 2][0] + 1) if GR[G - 2][0] < u else None
                            dve.tensor_copy(prT[:, G % 2, :, :].rearrange("p k q -> p (k q)")[:, 0:w],
                                            PS[:, 4 + G % 2, 0:w]).then_inc(pT_ready, 1)
                        st.done(dve.reciprocal(rden[:, i:i + 1], den[:, i:i + 1]))
                        dve.wait_ge(pv_ready, u + 1)
                        dve.tensor_scalar(mix[:, n, h * HD:(h + 1) * HD], PS[:, 6 + i, 0:HD], rden[:, i:i + 1], None,
                                          ALU.mult).then_inc(o_ready, 1)

                    for u, (n, h) in enumerate(ATT):
                        i = u % 2
                        keys = (n + 1) * P
                        dve.wait_ge(logits, u + 1)
                        lg = PS[:, 2 * i:2 * i + 2, :].rearrange("p b k -> p (b k)")[:, 0:keys]
                        st.done(dve.tensor_reduce(mx[:, i:i + 1], lg, AX.X, ALU.max))
                        dve.tensor_scalar(mx[:, i:i + 1], mx[:, i:i + 1], -float(HD) ** -0.5, None, ALU.mult).then_inc(mx_ready, 1)
                        if u >= 1:
                            finish(u - 1)
                        if h == H_FOX - 1 and n >= 1:
                            norm(n - 1)
                    finish(len(ATT) - 1)
                    norm(NT - 1)
        with ExitStack() as gc:
            qkvT = sb("qkvT", [P, 9, S], c=gc)
            sgate = sb("sgate", [P, NT, GDN], c=gc)
            N6 = [P, NT, H_GDN]
            g_ = sb("g_log", N6, c=gc)
            row_a, row_q = sb("row_a", N6, c=gc), sb("row_q", N6, c=gc)
            bias_j = sb("bias_j", N6, c=gc)
            beta, s_w, s_kd, s_q = (sb(n_, N6, c=gc) for n_ in ("beta", "s_w", "s_kd", "s_q"))
            e_last = sb("e_last", [P, NT, H_GDN // 2], c=gc)
            with ExitStack() as c, nc.Block() as block:
                new_phase(c)
                raw = sb("raw", [P, 2, S + 3], c=c)
                conv = sb("conv", [P, 2, S], c=c)
                sqT = sb("sqT", [P, S], c=c)
                ab = sb("ab", [P, NT, 2 * H_GDN], c=c)
                lnr = sb("lnr", [P, NT, 2 * H_GDN], c=c)
                t1, t2, t3 = (sb(n_, [P, NT, 2 * H_GDN], c=c) for n_ in ("t1", "t2", "t3"))
                ealog = sb("ealog", [P, H_GDN], c=c)
                projT, raw_ready, conv_ready, silu_ready = sem("projT"), sem("raw_ready"), sem("conv_ready"), sem("silu_ready")
                sqT_ready, sumsq_ready, gate_proj, gate_ready = sem("sqT_ready"), sem("sumsq"), sem("gate_proj"), sem("gate_ready")
                sc_dve, sc_act, sc_pe = sem("sc_dve"), sem("sc_act"), sem("sc_pe")
                dstep, astep, pads = sem("g_dve_step"), sem("g_act_step"), sem("pads")

                @block.sync
                def _(sp):
                    for k in range(6, 9):
                        load_chunk(sp, k)

                @block.tensor
                def _(pe):
                    def sumsq(g):
                        pe.wait_ge(sqT_ready, g + 1)
                        for n in range(NT):
                            at = n * 12 + 2 * g
                            mm = pe.matmul(PS[:, 6, at:at + 2], sqT[:, n * P:(n + 1) * P], kc[:, K_HO, 0:2], start=True, stop=True)
                        mm.then_inc(sumsq_ready, 1)

                    for g in range(9):
                        ch = CH_T0 + g // 4
                        if g % 4 == 0:
                            chunk_ready(pe, ch)
                        for b in range(2):
                            if g >= 2:
                                pe.wait_ge(raw_ready, 2 * (g - 2) + b + 1)
                            for k in range(KD):
                                mm = pe.matmul(PS[:, 2 * (g % 2) + b, :], wring[ch % 3][:, k, (g % 4) * P:(g % 4 + 1) * P],
                                               hT[:, k, 512 * b:512 * b + 512], start=(k == 0), stop=(k == KD - 1))
                            mm.then_inc(projT, 1)
                        if g % 4 == 3 or g == 8:
                            pe.wait_ge(projT, 2 * g + 2)
                            pe.nop().then_inc(w_used, 1)
                        if 1 <= g <= 6:
                            sumsq(g - 1)
                    chunk_ready(pe, CH_GAB)
                    for n in range(NT):
                        if n >= 2:
                            pe.wait_ge(gate_ready, n - 1)
                        project_tile(pe, CH_GAB, n, 4 + n % 2, W_GAB).then_inc(gate_proj, 1)
                    pe.wait_ge(gate_proj, NT)
                    pe.nop().then_inc(w_used, 1)
                    pe.wait_ge(sc_dve, 2)
                    for j, m in enumerate((U, L, ones)):
                        mm = pe.matmul(PS[:, 7, 48 * j:48 * j + 48], m, g_[:, :, :].rearrange("p n h -> p (n h)"), start=True, stop=True)
                    mm.then_inc(sc_pe, 1)

                @block.scalar
                def _(act):
                    st = Steps(act, astep)

                    def silu(g):
                        act.wait_ge(conv_ready, g + 1)
                        act.activation(qkvT[:, g, :], conv[:, g % 2, :], ACT.Silu).then_inc(silu_ready, 1)
                        if g < 6:
                            act.wait_ge(silu_ready, g + 1)
                            if g >= 1:
                                act.wait_ge(sumsq_ready, g)
                            act.activation(sqT[:, :], qkvT[:, g, :], ACT.Square).then_inc(sqT_ready, 1)

                    act.preload_act_table_set("silu_and_others")
                    act.wait_ge(pads, 1)
                    for g in range(9):
                        for b in range(2):
                            act.wait_ge(projT, 2 * g + b + 1)
                            if g >= 2:
                                act.wait_ge(conv_ready, g - 1)
                            act.activation(raw[:, g % 2, 3 + 512 * b:515 + 512 * b], PS[:, 2 * (g % 2) + b, :], ACT.Copy)\
                               .then_inc(raw_ready, 1)
                        if g >= 1:
                            silu(g - 1)
                    silu(8)
                    for n in range(NT):
                        act.wait_ge(gate_proj, n + 1)
                        st.done(act.activation(sgate[:, n, :], PS[:, 4 + n % 2, 0:GDN], ACT.Silu))
                        act.activation(ab[:, n, :], PS[:, 4 + n % 2, GDN:W_GAB], ACT.Copy).then_inc(gate_ready, 1)
                    act.wait_ge(sc_dve, 1)
                    act.preload_act_table_set("natural_log_exp_and_others")
                    st.done(act.activation(t2[:, :, :], t1[:, :, :], ACT.Abs))
                    st.done(act.activation(t2[:, :, :], t2[:, :, :], ACT.Exp, scale=-1.0))
                    st.done(act.activation(t2[:, :, :], t2[:, :, :], ACT.Ln, bias=1.0))
                    act.wait_ge(sumsq_ready, 6)
                    st.done(act.activation(lnr[:, :, :], PS[:, 6, 0:96].rearrange("p (n h) -> p n h", n=NT), ACT.Ln, bias=eps[:, :]))
                    act.activation(ealog[:, :], par("a_log"), ACT.Exp).then_inc(sc_act, 1)
                    act.wait_ge(sc_dve, 3)
                    for j, t in enumerate((beta, s_w, s_kd, s_q)):
                        st.done(act.activation(t[:, :, :], t[:, :, :], ACT.Exp))
                    for h in range(2):
                        tot = PS[64 * h:64 * h + 64, 7, 96:144].rearrange("p (n a s) -> p n a s", n=NT, s=2)[:, :, :, h]
                        st.done(act.activation(e_last[64 * h:64 * h + 64, :, :], tot, ACT.Exp))

                @block.vector
                def _(dve):
                    st = Steps(dve, dstep)
                    dve.memset(raw[:, :, 0:3], 0.0).then_inc(pads, 1)
                    w = par("conv").rearrange("p (g j) -> p g j", j=4)
                    dve.wait_ge(pads, 1)
                    for g in range(9):
                        dve.wait_ge(raw_ready, 2 * g + 2)
                        if g >= 2:
                            dve.wait_ge(silu_ready, g - 1)
                        y = conv[:, g % 2, :]
                        st.done(dve.tensor_scalar(y, raw[:, g % 2, 0:S], w[:, g, 0:1], None, ALU.mult))
                        for j in range(1, 4):
                            i = dve.scalar_tensor_tensor(out=y, in0=raw[:, g % 2, j:j + S], scalar=w[:, g, j:j + 1], in1=y,
                                                         op0=ALU.mult, op1=ALU.add)
                            st.done(i) if j < 3 else i.then_inc(conv_ready, 1)
                    dve.wait_ge(gate_ready, NT)
                    a, b = ab[:, :, 0:H_GDN], ab[:, :, H_GDN:12]
                    dt = par("dt_bias").unsqueeze(1).to_broadcast([P, NT, H_GDN])
                    st.done(dve.tensor_tensor(t1[:, :, 0:H_GDN], a, dt, ALU.add))
                    dve.tensor_copy(t1[:, :, H_GDN:12], b).then_inc(sc_dve, 1)
                    dve.wait_ge(sc_dve, 1)
                    st.done(dve.tensor_scalar(t3[:, :, 0:H_GDN], t1[:, :, 0:H_GDN], 0.0, None, ALU.max))
                    st.done(dve.tensor_scalar(t3[:, :, H_GDN:12], t1[:, :, H_GDN:12], 0.0, None, ALU.min))
                    dve.wait_ge(sc_act, 1)
                    st.done(dve.tensor_tensor(t3[:, :, 0:H_GDN], t3[:, :, 0:H_GDN], t2[:, :, 0:H_GDN], ALU.add))
                    st.done(dve.tensor_tensor(t3[:, :, H_GDN:12], t3[:, :, H_GDN:12], t2[:, :, H_GDN:12], ALU.subtract))
                    st.done(dve.tensor_scalar(ealog[:, :], ealog[:, :], -1.0, None, ALU.mult))
                    dve.tensor_tensor(g_[:, :, :], t3[:, :, 0:H_GDN],
                                      ealog[:, :].unsqueeze(1).to_broadcast([P, NT, H_GDN]), ALU.mult).then_inc(sc_dve, 1)
                    lb = t3[:, :, H_GDN:12]
                    st.done(dve.tensor_scalar(row_q[:, :, :], lnr[:, :, 0:6], -0.5, -0.5 * math.log(HD), ALU.mult, ALU.add))
                    st.done(dve.tensor_scalar(t2[:, :, 0:6], lnr[:, :, 6:12], -0.5, None, ALU.mult))
                    lnrk = t2[:, :, 0:6]
                    st.done(dve.tensor_tensor(row_a[:, :, :], lb, lnrk, ALU.add))
                    dve.wait_ge(sc_pe, 1)
                    d, dl = (PS[:, 7, 48 * j:48 * j + 48].rearrange("p (n h) -> p n h", n=NT) for j in range(2))
                    st.done(dve.tensor_copy(beta[:, :, :], lb))
                    st.done(dve.tensor_tensor(bias_j[:, :, :], lnrk, d, ALU.subtract))
                    st.done(dve.tensor_tensor(s_w[:, :, :], row_a[:, :, :], d, ALU.add))
                    st.done(dve.tensor_tensor(s_kd[:, :, :], lnrk, dl, ALU.add))
                    dve.tensor_tensor(s_q[:, :, :], row_q[:, :, :], d, ALU.add).then_inc(sc_dve, 1)
                    go = par("gdn_o").unsqueeze(1).to_broadcast([P, NT * H_GDN, HD])
                    sg = sgate[:, :, :].rearrange("p n (h d) -> p (n h) d", d=HD)
                    st.done(dve.tensor_tensor(sg, sg, go, ALU.mult))

            with ExitStack() as c, nc.Block() as block:
                new_phase(c)
                kn, vn = sb("kn", [P, GDN], c=c), sb("vn", [P, GDN], c=c)
                rv, rw, kd = (sb(n_, [P, GDN], c=c) for n_ in ("rv", "rw", "kd"))
                M6 = [P, 2, 3, P]
                AT, IT, X, Y, M, T1 = (sb(n_, M6, c=c) for n_ in ("AT", "IT", "X", "Y", "M", "T1"))
                wTn = sb("wTn", [P, 3, P], c=c)
                vnew = sb("vnew", [P, 2, 3, HD], c=c)
                St = sb("St", [P, 3, HD], c=c)
                otmp = sb("otmp", [P, GDN], c=c)
                oss, orr = sb("oss", [P, H_GDN], c=c), sb("orr", [P, H_GDN], c=c)
                kv_turned, kv_ready, sc_ready = sem("kv_turned"), sem("kv_ready"), sem("sc_ready")
                dbc, gam_ready, kk, AT_ready = sem("dbc"), sem("gam_ready"), sem("kk"), sem("AT_ready")
                M_ready, XY_ready, T1_mm, T1_ready, D_mm = sem("M_ready"), sem("XY_ready"), sem("T1_mm"), sem("T1_ready"), sem("D_mm")
                M0_turned, w_mm, w_ready, v_mm, v_ready, o_mm, o_ready = (sem(n_) for n_ in (
                    "M0_turned", "w_mm", "w_ready", "v_mm", "v_ready", "o_mm", "go_ready"))
                S_ready, os_act, oss_rdy, orr_rdy, on_ready = (sem(n_) for n_ in ("S_ready", "os_act", "oss_rdy", "orr_rdy", "gon_ready"))
                dstep, astep, pstep = sem("h_dve_step"), sem("h_act_step"), sem("h_pool_step")
                LV = 7

                def slots(ap, s):
                    return ap.rearrange("p (a s) -> p s a", s=2)[:, s, :]

                def hcols(ap, s):
                    return ap.rearrange("p (a s d) -> p s a d", s=2, d=HD)[:, s, :, :]

                def bank3(b):
                    return PS[:, b, 0:3 * P].rearrange("p (a t) -> p a t", a=3)

                @block.sync
                def _(sp):
                    load_chunk(sp, 9)

                @block.tensor
                def _(pe):
                    for n in range(NT):
                        t = slice(n * P, (n + 1) * P)
                        if n >= 1:
                            pe.wait_ge(S_ready, n + 1)
                            pe.wait_ge(o_ready, n)
                        for j, b in ((0, 0), (1, 1)):
                            for a in range(3):
                                mm = pe.transpose(PS[:, b, a * P:(a + 1) * P], qkvT[:, 3 + 3 * j + a, t], ident)
                            mm.then_inc(kv_turned, 1)
                        for s in range(2):
                            for b, row, mask in ((2 + s, row_a, mask_strict), (4 + s, row_q, mask_incl)):
                                for a in range(3):
                                    h = 2 * a + s
                                    o = PS[:, b, a * P:(a + 1) * P]
                                    pe.matmul(o, g_[:, n, h:h + 1].to_broadcast([P, P]), U, start=True, stop=False)
                                    pe.matmul(o, row[:, n, h:h + 1].to_broadcast([P, P]), ident, start=False, stop=False)
                                    mm = pe.matmul(o, identb, mask, start=False, stop=True)
                                mm.then_inc(dbc, 1)
                        for j in range(2):
                            for s in range(2):
                                b = (6 + s) if j == 0 else s
                                if j == 1:
                                    pe.wait_ge(kv_ready, 2 * n + s + 1)
                                for a in range(3):
                                    hs = slice(64 * s, 64 * s + 64)
                                    rhs = qkvT[hs, 3 + a, t] if j == 0 else qkvT[hs, a, t]
                                    mm = pe.matmul(PS[:, b, a * P:(a + 1) * P], qkvT[hs, 3 + a, t], rhs, start=True, stop=True)
                                mm.then_inc(kk, 1)
                        for s in range(2):
                            pe.wait_ge(M_ready, 2 * LV * n + s + 1)
                            pe.wait_ge(gam_ready, 4 * n + 2 + s)
                            for a in range(3):
                                mm = pe.transpose(PS[:, 2 + s, a * P:(a + 1) * P], M[:, s, a, :], ident)
                            mm.then_inc(M0_turned, 1)
                        for l in range(1, LV):
                            for s in range(2):
                                pe.wait_ge(M_ready, 2 * LV * n + 2 * l + s + 1)
                                pe.wait_ge(XY_ready, 2 * LV * n + 2 * (l - 1) + s + 1)
                                for a in range(3):
                                    mm = pe.matmul(PS[:, s, a * P:(a + 1) * P], M[:, s, a, :], X[:, s, a, :], start=True, stop=True)
                                mm.then_inc(T1_mm, 1)
                            for s in range(2):
                                pe.wait_ge(T1_ready, 2 * (LV - 1) * n + 2 * (l - 1) + s + 1)
                                for a in range(3):
                                    if l < LV - 1:
                                        pe.matmul(PS[:, 2 + s, a * P:(a + 1) * P], Y[:, s, a, :], T1[:, s, a, :], start=True, stop=True)
                                    mm = pe.matmul(PS[:, 4 + s, a * P:(a + 1) * P], T1[:, s, a, :], Y[:, s, a, :], start=True, stop=True)
                                mm.then_inc(D_mm, 1)
                        for s in range(2):
                            pe.wait_ge(XY_ready, 2 * LV * (n + 1) - 1 + s)
                            pe.wait_ge(sc_ready, 3 * n + 3)
                            for a in range(3):
                                h = 2 * a + s
                                mm = pe.matmul(PS[64 * s:64 * s + 64, s, a * P:(a + 1) * P], rw[:, h * HD:(h + 1) * HD], Y[:, s, a, :],
                                               start=True, stop=True)
                            mm.then_inc(w_mm, 1)
                        for s in range(2):
                            pe.wait_ge(w_ready, 2 * n + s + 1)
                            if s == 0:
                                pe.wait_ge(S_ready, n + 1)
                            for a in range(3):
                                h = 2 * a + s
                                o = PS[:, 2 + s, a * HD:(a + 1) * HD]
                                pe.matmul(o, Y[:, s, a, :], rv[:, h * HD:(h + 1) * HD], start=True, stop=False)
                                mm = pe.matmul(o, wTn[64 * s:64 * s + 64, a, :], St[64 * s:64 * s + 64, a, :], start=False, stop=True)
                            mm.then_inc(v_mm, 1)
                        for s in range(2):
                            for a in range(3):
                                hs = slice(64 * s, 64 * s + 64)
                                mm = pe.matmul(PS[:, 4 + s, a * HD:(a + 1) * HD], qkvT[hs, a, t], St[hs, a, :], start=True, stop=True)
                            mm.then_inc(o_mm, 1)
                        for s in range(2):
                            pe.wait_ge(v_ready, 2 * n + s + 1)
                            for a in range(3):
                                h = 2 * a + s
                                pe.matmul(PS[:, 6, (3 * s + a) * HD:(3 * s + a + 1) * HD], IT[:, s, a, :], vnew[:, s, a, :], start=True, stop=True)
                                mm = pe.matmul(PS[64 * s:64 * s + 64, 7, a * HD:(a + 1) * HD], kd[:, h * HD:(h + 1) * HD], vnew[:, s, a, :],
                                               start=True, stop=True)
                            mm.then_inc(o_mm, 1)

                @block.scalar
                def _(act):
                    st = Steps(act, astep)
                    for n in range(NT):
                        for j, dst in enumerate((kn, vn)):
                            act.wait_ge(kv_turned, 2 * n + j + 1)
                            if n >= 1:
                                act.wait_ge(sc_ready, 3 * n)
                            act.activation(dst[:, :], PS[:, j, 0:GDN], ACT.Copy).then_inc(kv_ready, 1)
                        for s in range(2):
                            for j, dst in enumerate((AT, IT)):
                                act.wait_ge(dbc, 4 * n + 2 * s + j + 1)
                                if n >= 1:
                                    act.wait_ge(M_ready, 2 * LV * n)
                                    act.wait_ge(o_mm, 4 * n)
                                for a in range(3):
                                    h = 2 * a + s
                                    i = act.activation(dst[:, s, a, :], PS[:, 2 + 2 * j + s, a * P:(a + 1) * P], ACT.Exp,
                                                       bias=bias_j[:, n, h:h + 1])
                                i.then_inc(gam_ready, 1)
                        for l in range(1, LV):
                            for s in range(2):
                                act.wait_ge(T1_mm, 2 * (LV - 1) * n + 2 * (l - 1) + s + 1)
                                if l > 1 or n >= 1:
                                    act.wait_ge(D_mm, 2 * (LV - 1) * n + 2 * (l - 2) + s + 1)
                                act.activation(T1[:, s, :, :], bank3(s), ACT.Copy).then_inc(T1_ready, 1)
                        for s in range(2):
                            act.wait_ge(w_mm, 2 * n + s + 1)
                            hs = slice(64 * s, 64 * s + 64)
                            act.activation(wTn[hs, :, :], PS[hs, s, 0:3 * P].rearrange("p (a t) -> p a t", a=3), ACT.Copy, scale=-1.0)\
                               .then_inc(w_ready, 1)
                        for s in range(2):
                            act.wait_ge(v_mm, 2 * n + s + 1)
                            act.activation(vnew[:, s, :, :].rearrange("p a d -> p (a d)"), PS[:, 2 + s, 0:3 * HD], ACT.Copy)\
                               .then_inc(v_ready, 1)
                        act.wait_ge(o_ready, n + 1)
                        if n >= 1:
                            act.wait_ge(on_ready, n)
                        act.activation(otmp[:, :], mix[:, n, FOX:FOX + GDN], ACT.Square).then_inc(os_act, 1)
                        act.wait_ge(oss_rdy, n + 1)
                        st.done(act.activation(orr[:, :], oss[:, :], ACT.Ln, bias=eps[:, :], scale=1.0 / HD))
                        act.activation(orr[:, :], orr[:, :], ACT.Exp, scale=-0.5).then_inc(orr_rdy, 1)

                @block.gpsimd
                def _(pool):
                    for n in range(NT):
                        def bc(t):
                            return t[:, n, :].unsqueeze(2).to_broadcast([P, H_GDN, HD])

                        def v3(t):
                            return t[:, :].rearrange("p (h d) -> p h d", d=HD)
                        pool.wait_ge(kv_ready, 2 * n + 2)
                        if n >= 1:
                            pool.wait_ge(o_mm, 4 * n)
                        pool.tensor_tensor(v3(rw), v3(kn), bc(s_w), ALU.mult).then_inc(sc_ready, 1)
                        pool.tensor_tensor(v3(kd), v3(kn), bc(s_kd), ALU.mult).then_inc(sc_ready, 1)
                        pool.tensor_tensor(v3(rv), v3(vn), bc(beta), ALU.mult).then_inc(sc_ready, 1)
                        for l in range(LV):
                            for s in range(2):
                                pool.wait_ge(AT_ready, 4 * n + s + 1)
                                if l == 0 and n >= 1:
                                    pool.wait_ge(T1_mm, 2 * (LV - 1) * n)
                                if l == 1:
                                    pool.wait_ge(M0_turned, 2 * n + s + 1)
                                    pool.wait_ge(XY_ready, 2 * LV * n + s + 1)
                                if l > 1:
                                    pool.wait_ge(T1_mm, 2 * (LV - 1) * n + 2 * (l - 2) + s + 1)
                                lm = kc[:, K_LM + l, :].unsqueeze(1).to_broadcast([P, 3, P])
                                pool.tensor_tensor(M[:, s, :, :], AT[:, s, :, :], lm, ALU.mult).then_inc(M_ready, 1)

                @block.vector
                def _(dve):
                    st = Steps(dve, dstep)
                    st.done(dve.memset(St[:, :, :], 0.0))
                    idb3 = ident.unsqueeze(1).to_broadcast([P, 3, P])
                    for n in range(NT):
                        for s in range(2):
                            dve.wait_ge(gam_ready, 4 * n + 2 * s + 1)
                            dve.wait_ge(kk, 4 * n + s + 1)
                            if n >= 1:
                                dve.wait_ge(M_ready, 2 * LV * n)
                            dve.tensor_tensor(AT[:, s, :, :], bank3(6 + s), AT[:, s, :, :], ALU.mult).then_inc(AT_ready, 1)
                        for s in range(2):
                            dve.wait_ge(gam_ready, 4 * n + 2 * s + 2)
                            dve.wait_ge(kk, 4 * n + 2 + s + 1)
                            dve.tensor_tensor(IT[:, s, :, :], bank3(s), IT[:, s, :, :], ALU.mult).then_inc(AT_ready, 1)
                        for s in range(2):
                            dve.wait_ge(M_ready, 2 * LV * n + s + 1)
                            st.done(dve.tensor_tensor(Y[:, s, :, :], idb3, M[:, s, :, :], ALU.subtract))
                            dve.wait_ge(M0_turned, 2 * n + s + 1)
                            dve.tensor_tensor(X[:, s, :, :], idb3, bank3(2 + s), ALU.subtract).then_inc(XY_ready, 1)
                        for l in range(1, LV):
                            for s in range(2):
                                dve.wait_ge(D_mm, 2 * (LV - 1) * n + 2 * (l - 1) + s + 1)
                                if l < LV - 1:
                                    st.done(dve.tensor_tensor(X[:, s, :, :], X[:, s, :, :], bank3(2 + s), ALU.subtract))
                                dve.tensor_tensor(Y[:, s, :, :], Y[:, s, :, :], bank3(4 + s), ALU.subtract).then_inc(XY_ready, 1)
                        if n == 0:
                            st.done(dve.tensor_copy(otmp[:, 0:1], eps[:, :]))
                            dve.memset(St[:, :, :], 0.0).then_inc(S_ready, 1)
                        dve.wait_ge(o_mm, 4 * n + 4)
                        for s in range(2):
                            o = hcols(mix[:, n, FOX:FOX + GDN], s)
                            st.done(dve.tensor_tensor(o, PS[:, 4 + s, 0:3 * HD].rearrange("p (a d) -> p a d", a=3),
                                                      slots(s_q[:, n, :], s).unsqueeze(2).to_broadcast([P, 3, HD]), ALU.mult))
                            i = dve.tensor_tensor(o, o, PS[:, 6, 3 * s * HD:3 * (s + 1) * HD].rearrange("p (a d) -> p a d", a=3), ALU.add)
                            st.done(i) if s == 0 else i.then_inc(o_ready, 1)
                        dve.wait_ge(o_ready, n + 1)
                        st.done(dve.tensor_tensor(St[:, :, :], St[:, :, :], e_last[:, n, :].unsqueeze(2).to_broadcast([P, 3, HD]), ALU.mult))
                        dve.tensor_tensor(St[:, :, :], St[:, :, :], PS[:, 7, 0:3 * HD].rearrange("p (a d) -> p a d", a=3), ALU.add)\
                           .then_inc(S_ready, 1)
                        dve.wait_ge(os_act, n + 1)
                        dve.tensor_reduce(oss[:, :], otmp[:, :].rearrange("p (h d) -> p h d", d=HD), AX.X, ALU.add).then_inc(oss_rdy, 1)
                        dve.wait_ge(orr_rdy, n + 1)
                        o = mix[:, n, FOX:FOX + GDN].rearrange("p (h d) -> p h d", d=HD)
                        st.done(dve.tensor_tensor(o, o, orr[:, :].unsqueeze(2).to_broadcast([P, H_GDN, HD]), ALU.mult))
                        dve.tensor_tensor(mix[:, n, FOX:FOX + GDN], mix[:, n, FOX:FOX + GDN], sgate[:, n, :], ALU.mult).then_inc(on_ready, 1)

        with ExitStack() as lc:
            vl = sb("vl", [P, NT, GV], c=lc)
            slr = sb("slr", [P, NT, GV], c=lc)
            qlT, klT, bT = (sb(n_, [P, S], c=lc) for n_ in ("qlT", "klT", "bT"))
            with ExitStack() as c, nc.Block() as block:
                new_phase(c)
                wa2 = sb("wa2", [RANK, GK], c=c)
                la1T = sb("la1T", [RANK, S], c=c)
                lx, le, lm_ = (sb(n_, [P, NT, GK], c=c) for n_ in ("lx", "le", "lmin"))
                wa2_loaded, lproj, l_ready, nproj, n_ready = (sem(n_) for n_ in ("wa2_loaded", "lproj", "l_ready", "nproj", "n_ready"))
                la_mm, lx_ready, ls_act, ls_ready, b_mm, b_ready = (sem(n_) for n_ in ("la_mm", "lx_ready", "ls_act", "ls_ready", "b_mm", "b_ready"))
                dstep, astep = sem("l_dve_step"), sem("l_act_step")

                @block.sync
                def _(sp):
                    sp.dma_start(wa2[:, :], w_a2).then_inc(wa2_loaded, 16)
                    load_chunk(sp, 10)

                @block.tensor
                def _(pe):
                    chunk_ready(pe, CH_L)
                    for j, (a, w) in enumerate(((2 * GK, RANK), (0, GK), (GK, GK))):
                        for b in range(2):
                            if j == 2:
                                pe.wait_ge(l_ready, b + 1)
                            for k in range(KD):
                                mm = pe.matmul(PS[0:w, 2 * (j % 2) + b, :], wring[CH_L % 3][:, k, a:a + w],
                                               hT[:, k, 512 * b:512 * b + 512], start=(k == 0), stop=(k == KD - 1))
                            mm.then_inc(lproj, 1)
                    pe.wait_ge(lproj, 6)
                    pe.nop().then_inc(w_used, 1)
                    pe.wait_ge(wa2_loaded, 16)
                    pe.wait_ge(l_ready, 2)
                    for n in range(NT):
                        mm = pe.matmul(PS[:, 6 + n // 4, (n % 4) * P:(n % 4 + 1) * P], la1T[:, n * P:(n + 1) * P], wa2[:, :],
                                       start=True, stop=True)
                    mm.then_inc(la_mm, 1)
                    chunk_ready(pe, CH_LVR)
                    for n in range(NT):
                        if n >= 2:
                            pe.wait_ge(n_ready, n - 1)
                        project_tile(pe, CH_LVR, n, 4 + n % 2, 512).then_inc(nproj, 1)
                    pe.wait_ge(nproj, NT)
                    pe.nop().then_inc(w_used, 1)
                    pe.wait_ge(ls_ready, 1)
                    for n in range(NT):
                        mm = pe.matmul(PS[:, 6 + n // 4, (n % 4) * P:(n % 4 + 1) * P], lx[:, n, :], U, start=True, stop=True)
                    mm.then_inc(b_mm, 1)

                @block.scalar
                def _(act):
                    st = Steps(act, astep)
                    act.preload_act_table_set("silu_and_others")
                    for j, dst in enumerate((la1T, qlT, klT)):
                        for b in range(2):
                            act.wait_ge(lproj, 2 * j + b + 1)
                            w = RANK if j == 0 else P
                            act.activation(dst[:, 512 * b:512 * b + 512], PS[0:w, 2 * (j % 2) + b, :], ACT.Copy).then_inc(l_ready, 1)
                    for n in range(NT):
                        act.wait_ge(nproj, n + 1)
                        st.done(act.activation(vl[:, n, :], PS[:, 4 + n % 2, 0:GV], ACT.Copy))
                        act.activation(slr[:, n, :], PS[:, 4 + n % 2, GV:512], ACT.Silu).then_inc(n_ready, 1)
                    act.wait_ge(lx_ready, 1)
                    act.preload_act_table_set("natural_log_exp_and_others")
                    st.done(act.activation(le[:, :, :], lx[:, :, :], ACT.Abs))
                    st.done(act.activation(le[:, :, :], le[:, :, :], ACT.Exp, scale=-1.0))
                    act.activation(le[:, :, :], le[:, :, :], ACT.Ln, bias=1.0).then_inc(ls_act, 1)
                    act.wait_ge(b_mm, 1)
                    for b in range(2):
                        act.activation(bT[:, 512 * b:512 * b + 512], PS[:, 6 + b, :], ACT.Copy, scale=1.0 / 16).then_inc(b_ready, 1)

                @block.vector
                def _(dve):
                    st = Steps(dve, dstep)
                    dve.wait_ge(la_mm, 1)
                    ba = par("b_a").unsqueeze(1).to_broadcast([P, 4, GK])
                    for b in range(2):
                        i = dve.tensor_tensor(lx[:, 4 * b:4 * b + 4, :], PS[:, 6 + b, :].rearrange("p (n c) -> p n c", n=4), ba, ALU.add)
                        st.done(i) if b == 0 else i.then_inc(lx_ready, 1)
                    dve.wait_ge(lx_ready, 1)
                    st.done(dve.tensor_scalar(lm_[:, :, :], lx[:, :, :], 0.0, None, ALU.min))
                    dve.wait_ge(ls_act, 1)
                    dve.tensor_tensor(lx[:, :, :], lm_[:, :, :], le[:, :, :], ALU.subtract).then_inc(ls_ready, 1)
                    go = par("gla_o").unsqueeze(1).to_broadcast([P, NT * H_GLA, HD])
                    sg = slr[:, :, :].rearrange("p n (h d) -> p (n h) d", d=HD)
                    dve.wait_ge(n_ready, NT)
                    st.done(dve.tensor_tensor(sg, sg, go, ALU.mult))

            with ExitStack() as c, nc.Block() as block:
                new_phase(c)
                ql, kl = sb("ql", [P, S], c=c), sb("kl", [P, S], c=c)
                el_ = sb("el_", [P, S], c=c)
                sc = sb("sc", [P, NT, H_GLA, P], c=c)
                qe, kdT = sb("qe", [P, S], c=c), sb("kdT", [P, S], c=c)
                kdn = sb("kdn", [P, GK], c=c)
                e_end = sb("e_end", [P, NT], c=c)
                Sg = sb("Sg", [P, GV], c=c)
                kvm = sb("kvm", [P, GV], c=c)
                osq = sb("osq", [P, NT, GV], c=c)
                oss, orr = sb("loss", [P, NT * H_GLA], c=c), sb("lorr", [P, NT * H_GLA], c=c)
                diff_ready, e_ready, qk_ready, sc_mm, sc_done = (sem(n_) for n_ in ("diff_ready", "e_ready", "qk_ready", "sc_mm", "sc_done"))
                kd_turned, kdn_ready, o_mm, kv_mm, o_ready, S_ready = (sem(n_) for n_ in (
                    "lkd_turned", "kdn_ready", "lo_mm", "kv_mm", "lo_ready", "lS_ready"))
                sq_done, ss_done, rr_done = sem("lsq_done"), sem("lss_done"), sem("lrr_done")
                dstep = sem("m_dve_step")
                astep = sem("m_act_step")
                LV = 7

                def halves(t, l):
                    v = t[:, :].rearrange("p (b u w) -> p b u w", u=2, w=1 << l)
                    return v[:, :, 0, :], v[:, :, 1, :]

                @block.tensor
                def _(pe):
                    for l in range(LV + 1):
                        for n in range(NT):
                            pe.wait_ge(qk_ready, min(l + 1, LV + 1))
                            u = l * NT + n
                            if u >= 2:
                                pe.wait_ge(sc_done, u - 1)
                            t = slice(n * P, (n + 1) * P)
                            q_, k_ = (ql, kl) if l < LV else (qlT, klT)
                            for h in range(H_GLA):
                                hs = slice(DK * h, DK * h + DK)
                                mm = pe.matmul(PS[:, 4 * (u % 2) + h, 0:P], k_[hs, t], q_[hs, t], start=True, stop=True,
                                               tile_position=(DK * h, 0))
                            mm.then_inc(sc_mm, 1)
                    for n in range(NT):
                        t = slice(n * P, (n + 1) * P)
                        pe.wait_ge(qk_ready, LV + 2)
                        if n == 0:
                            pe.wait_ge(sc_done, (LV + 1) * NT)
                        pe.wait_ge(o_ready, n) if n else None
                        if n:
                            pe.wait_ge(kdn_ready, n)
                            pe.wait_ge(S_ready, n + 1)
                        pe.transpose(PS[:, 0, 0:P], kdT[:, t], ident).then_inc(kd_turned, 1)
                        pe.wait_ge(S_ready, n + 1)
                        pe.matmul(PS[:, 1 + n % 2, 0:GV], qe[:, t], Sg[:, :], start=True, stop=False)
                        for h in range(H_GLA):
                            mm = pe.matmul(PS[:, 1 + n % 2, h * HD:(h + 1) * HD], sc[:, n, h, :], vl[:, n, h * HD:(h + 1) * HD],
                                           start=False, stop=(h == H_GLA - 1))
                        mm.then_inc(o_mm, 1)
                        pe.wait_ge(kdn_ready, n + 1)
                        pe.matmul(PS[:, 3, 0:GV], kdn[:, :], vl[:, n, :], start=True, stop=True).then_inc(kv_mm, 1)

                @block.scalar
                def _(act):
                    st = Steps(act, astep)
                    for l in range(LV + 2):
                        act.wait_ge(diff_ready, l + 1)
                        act.activation(el_[:, :], el_[:, :], ACT.Exp).then_inc(e_ready, 1)
                    for n in range(NT):
                        act.wait_ge(kd_turned, n + 1)
                        if n:
                            act.wait_ge(kv_mm, n)
                        act.activation(kdn[:, :], PS[:, 0, 0:P], ACT.Copy).then_inc(kdn_ready, 1)
                        act.wait_ge(o_mm, n + 1)
                        act.activation(mix[:, n, FOX + GDN:D], PS[:, 1 + n % 2, 0:GV], ACT.Copy, scale=float(DK) ** -0.5)\
                           .then_inc(o_ready, 1)
                    act.wait_ge(o_ready, NT)
                    act.activation(osq[:, :, :], mix[:, :, FOX + GDN:D], ACT.Square).then_inc(sq_done, 1)
                    act.wait_ge(ss_done, 1)
                    st.done(act.activation(orr[:, :], oss[:, :], ACT.Ln, bias=eps[:, :], scale=1.0 / HD))
                    act.activation(orr[:, :], orr[:, :], ACT.Exp, scale=-0.5).then_inc(rr_done, 1)

                @block.vector
                def _(dve):
                    st = Steps(dve, dstep)
                    for t_ in (ql, kl, sc):
                        st.done(dve.memset(t_[tuple(slice(None) for _ in t_.shape)], 0.0))
                    dve.memset(Sg[:, :], 0.0).then_inc(S_ready, 1)

                    def scores(u):
                        l, n = u // NT, u % NT
                        dve.wait_ge(sc_mm, u + 1)
                        lm = (kc[:, K_LM + l, :] if l < LV else ident).bitcast(U32).unsqueeze(1).to_broadcast([P, H_GLA, P])
                        src = PS[:, 4 * (u % 2):4 * (u % 2) + 4, 0:P]
                        dve.copy_predicated(sc[:, n, :, :], lm, src).then_inc(sc_done, 1)

                    for l in range(LV):
                        w = 1 << l
                        blo, bhi = halves(bT, l)
                        elo, ehi = halves(el_, l)
                        ref = bhi[:, :, 0:1].to_broadcast([P, S // (2 * w), w])
                        if l:
                            dve.wait_ge(qk_ready, l)
                        st.done(dve.tensor_tensor(elo, ref, blo, ALU.subtract))
                        dve.tensor_tensor(ehi, bhi, ref, ALU.subtract).then_inc(diff_ready, 1)
                        if l:
                            for n in range(NT):
                                scores((l - 1) * NT + n)
                        dve.wait_ge(e_ready, l + 1)
                        dve.wait_ge(sc_mm, l * NT) if l else None
                        st.done(dve.tensor_tensor(halves(kl, l)[0], halves(klT, l)[0], elo, ALU.mult))
                        dve.tensor_tensor(halves(ql, l)[1], halves(qlT, l)[1], ehi, ALU.mult).then_inc(qk_ready, 1)
                    dve.wait_ge(qk_ready, LV)
                    dve.tensor_copy(el_[:, :], bT[:, :]).then_inc(diff_ready, 1)
                    for n in range(NT):
                        scores((LV - 1) * NT + n)
                    dve.wait_ge(e_ready, LV + 1)
                    v = el_[:, :].rearrange("p (n t) -> p n t", n=NT)
                    st.done(dve.tensor_copy(e_end[:, :], v[:, :, P - 1]))
                    dve.tensor_tensor(qe[:, :], qlT[:, :], el_[:, :], ALU.mult).then_inc(qk_ready, 1)
                    dve.wait_ge(qk_ready, LV + 1)
                    bv = bT[:, :].rearrange("p (n t) -> p n t", n=NT)
                    dve.tensor_tensor(v, bv[:, :, P - 1:P].to_broadcast([P, NT, P]), bv, ALU.subtract).then_inc(diff_ready, 1)
                    for n in range(NT):
                        scores(LV * NT + n)
                    dve.wait_ge(e_ready, LV + 2)
                    dve.tensor_tensor(kdT[:, :], klT[:, :], el_[:, :], ALU.mult).then_inc(qk_ready, 1)
                    for n in range(NT):
                        dve.wait_ge(kv_mm, n + 1)
                        st.done(dve.tensor_tensor(kvm[:, :], PS[:, 3, 0:GV], kc[:, K_BD:K_BD + 2, :].rearrange("p a b -> p (a b)"), ALU.mult))
                        dve.scalar_tensor_tensor(out=Sg[:, :], in0=Sg[:, :], scalar=e_end[:, n:n + 1], in1=kvm[:, :],
                                                 op0=ALU.mult, op1=ALU.add).then_inc(S_ready, 1)
                    dve.wait_ge(sq_done, 1)
                    dve.tensor_reduce(oss[:, :], osq[:, :, :].rearrange("p n (h d) -> p (n h) d", d=HD), AX.X, ALU.add).then_inc(ss_done, 1)
                    dve.wait_ge(rr_done, 1)
                    o = mix[:, :, FOX + GDN:D]
                    for n in range(NT):
                        o3 = o[:, n, :].rearrange("p (h d) -> p h d", d=HD)
                        st.done(dve.tensor_tensor(o3, o3, orr[:, H_GLA * n:H_GLA * n + H_GLA].unsqueeze(2).to_broadcast([P, H_GLA, HD]), ALU.mult))
                    st.done(dve.tensor_tensor(o, o, slr[:, :, :], ALU.mult))

        rl = sb("rl", [P, NT, NG + NE])
        with ExitStack() as c, nc.Block() as block:
            new_phase(c)
            xr = sb("xr", [P, 2, D], c=c)
            mT = sb("mT", [P, 2, KD, P], c=c)
            h2 = sb("h2", [P, 2, D], c=c)
            wr = sb("wr", [P, KD, NG + NE], c=c)
            junk = sb("junk2", [P, D], c=c)
            zy = sb("zy", [P, D], c=c)
            zy_ready, zy_stored = sem("zy_ready"), sem("zy_stored")
            ss, rr = sb("oss2", [P, NT], c=c), sb("orr2", [P, NT], c=c)
            xr_loaded, wr_loaded = [sem("xr_loaded0"), sem("xr_loaded1")], sem("wr_loaded")
            m_turned, mT_ready, y_mm, x1_ready = sem("m_turned"), sem("mT_ready"), sem("y_mm"), sem("x1_ready")
            r2_ready, h2_ready, h2_turned, h2T_ready, rl_mm, rl_ready = (sem(n_) for n_ in (
                "r2_ready", "h2_ready", "h2_turned", "h2T_ready", "rl_mm", "rl_ready"))
            h2_stored = [sem("h2_stored0"), sem("h2_stored1")]
            astep = sem("o_act_step")

            @block.sync
            def _(sp):
                sp.dma_start(wr[:, :, :], w_router.rearrange("(k p) n -> p k n", p=P)).then_inc(wr_loaded, 16)
                for n in range(NT):
                    if n >= 2:
                        sp.wait_ge(x1_ready, 2 * (n - 1))
                    sp.dma_start(xr[:, n % 2, :], x[n * P:(n + 1) * P, :]).then_inc(xr_loaded[n % 2], 16)
                    if n >= 1:
                        sp.wait_ge(h2_ready, n)
                        sp.dma_start(h2_dram[(n - 1) * P:n * P, :], h2[:, (n - 1) % 2, :]).then_inc(h2_stored[(n - 1) % 2], 16)
                sp.wait_ge(h2_ready, NT)
                sp.dma_start(h2_dram[(NT - 1) * P:S, :], h2[:, (NT - 1) % 2, :]).then_inc(h2_stored[(NT - 1) % 2], 16)
                for i in range(2):
                    sp.wait_ge(h2_stored[i], 16 * NT // 2)
                sp.wait_ge(zy_stored, 16)

            @block.gpsimd
            def _(pool):
                pool.memset(zy[:, :], 0.0).then_inc(zy_ready, 1)
                pool.wait_ge(zy_ready, 1)
                pool.dma_start(y_dram[NE * P:, :].rearrange("(b p) d -> p b d", p=P),
                               zy[:, :].unsqueeze(1).to_broadcast([P, MAXB - NE, D])).then_inc(zy_stored, 16)

            @block.tensor
            def _(pe):
                def project(n):
                    for b in range(2):
                        if n >= 1:
                            pe.wait_ge(mT_ready, 2 * (n - 1) + b + 1)
                        for k in range(4):
                            mm = pe.transpose(PS[:, b, k * P:(k + 1) * P], mix[:, n, (4 * b + k) * P:(4 * b + k + 1) * P], ident)
                        mm.then_inc(m_turned, 1)
                    for b in range(2):
                        if n == 0:
                            chunk_ready(pe, CH_O0 + b)
                        else:
                            pe.wait_ge(x1_ready, 2 * (n - 1) + b + 1)
                        for k in range(KD):
                            pe.wait_ge(mT_ready, 2 * n + k // 4 + 1) if b == 0 and k % 4 == 0 else None
                            mm = pe.matmul(PS[:, 2 + b, :], mT[:, n % 2, k, :], wring[(CH_O0 + b) % 3][:, k, :],
                                           start=(k == 0), stop=(k == KD - 1))
                        mm.then_inc(y_mm, 1)

                def route(n):
                    pe.wait_ge(h2_ready, n + 1)
                    for b in range(2):
                        if n >= 1:
                            pe.wait_ge(h2T_ready, 2 * (n - 1) + b + 1)
                        for k in range(4):
                            mm = pe.transpose(PS[:, 4 + b, k * P:(k + 1) * P], h2[:, n % 2, (4 * b + k) * P:(4 * b + k + 1) * P], ident)
                        mm.then_inc(h2_turned, 1)
                    pe.wait_ge(h2T_ready, 2 * n + 2)
                    if n >= 1:
                        pe.wait_ge(rl_ready, n)
                    for k in range(KD):
                        mm = pe.matmul(PS[:, 6, 0:NG + NE], hT[:, k, n * P:(n + 1) * P], wr[:, k, :], start=(k == 0), stop=(k == KD - 1))
                    mm.then_inc(rl_mm, 1)

                pe.wait_ge(wr_loaded, 16)
                for n in range(NT):
                    project(n)
                    if n >= 1:
                        route(n - 1)
                route(NT - 1)
                pe.wait_ge(y_mm, 2 * NT)
                pe.nop().then_inc(w_used, 2)

            @block.scalar
            def _(act):
                st = Steps(act, astep)
                for n in range(NT):
                    for b in range(2):
                        act.wait_ge(m_turned, 2 * n + b + 1)
                        if n >= 2:
                            act.wait_ge(y_mm, 2 * (n - 1))
                        act.activation(mT[:, n % 2, 4 * b:4 * b + 4, :], PS[:, b, :].rearrange("p (k t) -> p k t", k=4), ACT.Copy)\
                           .then_inc(mT_ready, 1)
                    act.wait_ge(x1_ready, 2 * n + 2)
                    st.done(act.activation(junk[:, :], mix[:, n, :], ACT.Square, accum_out=ss[:, n:n + 1]))
                    st.done(act.activation(rr[:, n:n + 1], ss[:, n:n + 1], ACT.Ln, bias=eps[:, :], scale=1.0 / D))
                    act.activation(rr[:, n:n + 1], rr[:, n:n + 1], ACT.Exp, scale=-0.5).then_inc(r2_ready, 1)

            @block.vector
            def _(dve):
                def residual(n):
                    dve.wait_ge(xr_loaded[n % 2], 16 * (n // 2 + 1))
                    for b in range(2):
                        dve.wait_ge(y_mm, 2 * n + b + 1)
                        if b == 0:
                            dve.wait_ge(m_turned, 2 * n + 2)
                        c_ = slice(512 * b, 512 * b + 512)
                        dve.tensor_tensor(mix[:, n, c_], PS[:, 2 + b, :], xr[:, n % 2, c_], ALU.add).then_inc(x1_ready, 1)

                def norm(n):
                    dve.wait_ge(r2_ready, n + 1)
                    if n >= 2:
                        dve.wait_ge(h2_stored[n % 2], 16 * (n // 2))
                    dve.tensor_scalar(h2[:, n % 2, :], mix[:, n, :], rr[:, n:n + 1], None, ALU.mult).then_inc(h2_ready, 1)
                    for b in range(2):
                        dve.wait_ge(h2_turned, 2 * n + b + 1)
                        g = par("ffn_gain")[:, 4 * b:4 * b + 4].unsqueeze(2).to_broadcast([P, 4, P])
                        dve.tensor_tensor(hT[:, 4 * b:4 * b + 4, n * P:(n + 1) * P],
                                          PS[:, 4 + b, :].rearrange("p (k t) -> p k t", k=4), g, ALU.mult).then_inc(h2T_ready, 1)

                def logits(n):
                    dve.wait_ge(rl_mm, n + 1)
                    dve.tensor_tensor(rl[:, n, :], PS[:, 6, 0:NG + NE], prm[:, PC["b_rg"][0]:PC["b_re"][1]], ALU.add).then_inc(rl_ready, 1)

                for n in range(NT):
                    residual(n)
                    if n >= 1:
                        norm(n - 1)
                        logits(n - 1)
                norm(NT - 1)
                logits(NT - 1)

        dest_i = sb("dest_i", [P, NT, 2], I32)
        gates = sb("gates", [P, NT, 2])
        plan = sb("plan", [1, 2 + 16], I32)
        slots_i = sb("slots_i", [P, LST], I32)
        with ExitStack() as c, nc.Block() as block:
            new_phase(c)
            def rt(name, *shape, dt=F32):
                return sb(name, [P, *shape], dt, c=c)
            glp, g8, gi8 = rt("glp", NT, 8), rt("g8", NT, 8), rt("gi8", NT, 8, dt=U32)
            gidx, oh_g, gd, gs = rt("gidx", NT), rt("oh_g", NT, NG), rt("gd", NT, NG), rt("gs", NT)
            eall, esel = rt("eall", NT, NG, EPG), rt("esel", NT, EPG)
            e8, ei8, eid, rr = rt("e8", NT, 8), rt("ei8", NT, 8, dt=U32), rt("eid", NT, 2), rt("rr3", NT)
            Mk, Mb, onesb = rt("Mk", 2, NT, NE), rt("Mb", NT, NE, dt=BF16), rt("onesb", P, dt=BF16)
            pre, rank, ov, cum, big = rt("pre", NT, NE), rt("rank", NT, NE), rt("ov", NE), rt("cum", 2, NE), rt("big", NT, NE)
            cnt, ia, ib = rt("cnt", NE), rt("ia", NE), rt("ib", NE)
            tmpd, dest_f, nb_f, cmp_, tok = rt("tmpd", NT, NE), rt("dest_f", NT, 2), rt("nb_f", 18), rt("cmp", 16, NE), rt("tok", NT)
            zl = sb("zl", [LST, P], c=c)
            lrow = sb("lrow", [LST, P], c=c)
            g_exp, g_act, Mb_ready, rank_mm, dest_ready, zl_ready = (sem(n_) for n_ in (
                "g_exp", "g_act", "Mb_ready", "rank_mm", "dest_ready", "zl_ready"))
            zl_stored, listed, lrow_loaded, l_turned = sem("zl_stored"), sem("listed"), sem("lrow_loaded"), sem("l_turned")
            dstep = sem("r_dve_step")

            @block.sync
            def _(sp):
                sp.wait_ge(zl_ready, 1)
                sp.dma_start(list_dram.rearrange("(a b) o -> a (b o)", b=P), zl[:, :]).then_inc(zl_stored, 16)
                sp.wait_ge(listed, 16 * 2 * NT)
                sp.dma_start(lrow[:, :], list_dram.rearrange("(a b) o -> a (b o)", b=P)).then_inc(lrow_loaded, 16)

            @block.gpsimd
            def _(pool):
                pool.wait_ge(zl_stored, 16)
                pool.wait_ge(dest_ready, 1)
                for n in range(NT):
                    for k in range(2):
                        pool.indirect_dma_start(list_dram, bass.IndirectOffsetOnAxis(ap=dest_i[:, n, k:k + 1], axis=0),
                                                tok[:, n:n + 1], None).then_inc(listed, 16)

            @block.tensor
            def _(pe):
                pe.wait_ge(Mb_ready, 1)
                m = Mb[:, :, :].rearrange("p n e -> p (n e)")
                pe.matmul(PS[:, 0, 0:NT * NE], before, m, start=True, stop=True)
                pe.matmul(PS[:, 1, 0:NT * NE], onesb[:, :], m, start=True, stop=True).then_inc(rank_mm, 1)
                pe.wait_ge(lrow_loaded, 16)
                pe.transpose(PS[:, 2, 0:LST], lrow[:, :], ident[0:LST, 0:LST]).then_inc(l_turned, 1)

            @block.scalar
            def _(act):
                act.wait_ge(g_exp, 1)
                act.activation(gd[:, :, :], gd[:, :, :], ACT.Exp).then_inc(g_act, 1)
                act.wait_ge(g_exp, 2)
                act.activation(rr[:, :], rr[:, :], ACT.Exp).then_inc(g_act, 1)

            @block.vector
            def _(dve):
                st = Steps(dve, dstep)
                dve.memset(zl[:, :], 0.0).then_inc(zl_ready, 1)
                st.done(dve.memset(onesb[:, :], 1.0))
                st.done(dve.memset(glp[:, :, :], NEG))
                st.done(dve.tensor_copy(glp[:, :, 0:NG], rl[:, :, 0:NG]))
                for n in range(NT):
                    st.done(dve.max(g8[:, n, :], glp[:, n, :]))
                    st.done(dve.max_index(gi8[:, n, :], g8[:, n, :], glp[:, n, :]))
                st.done(dve.tensor_copy(gidx[:, :], gi8[:, :, 0]))
                iota = kc[:, K_IOTA, :]
                st.done(dve.tensor_tensor(oh_g[:, :, :], iota[:, 0:NG].unsqueeze(1).to_broadcast([P, NT, NG]),
                                          gidx[:, :].unsqueeze(2).to_broadcast([P, NT, NG]), ALU.is_equal))
                dve.tensor_tensor(gd[:, :, :], rl[:, :, 0:NG], g8[:, :, 0:1].to_broadcast([P, NT, NG]), ALU.subtract).then_inc(g_exp, 1)
                for n in range(NT):
                    st.done(dve.tensor_tensor(eall[:, n, :, :], rl[:, n, NG:].rearrange("p (g e) -> p g e", g=NG),
                                              oh_g[:, n, :].unsqueeze(2).to_broadcast([P, NG, EPG]), ALU.mult))
                    st.done(dve.tensor_reduce(esel[:, n, :], eall[:, n, :, :].rearrange("p g e -> p e g"), AX.X, ALU.add))
                    st.done(dve.max(e8[:, n, :], esel[:, n, :]))
                    st.done(dve.max_index(ei8[:, n, :], e8[:, n, :], esel[:, n, :]))
                dve.tensor_tensor(rr[:, :], e8[:, :, 1], e8[:, :, 0], ALU.subtract).then_inc(g_exp, 1)
                st.done(dve.tensor_copy(eid[:, :, :], ei8[:, :, 0:2]))
                st.done(dve.tensor_scalar(gidx[:, :], gidx[:, :], float(EPG), None, ALU.mult))
                st.done(dve.tensor_tensor(eid[:, :, :], eid[:, :, :], gidx[:, :].unsqueeze(2).to_broadcast([P, NT, 2]), ALU.add))
                for k in range(2):
                    st.done(dve.tensor_tensor(Mk[:, k, :, :], iota[:, 0:NE].unsqueeze(1).to_broadcast([P, NT, NE]),
                                              eid[:, :, k:k + 1].to_broadcast([P, NT, NE]), ALU.is_equal))
                dve.tensor_tensor(Mb[:, :, :], Mk[:, 0, :, :], Mk[:, 1, :, :], ALU.add).then_inc(Mb_ready, 1)
                dve.wait_ge(g_act, 2)
                st.done(dve.tensor_reduce(gs[:, :], gd[:, :, :], AX.X, ALU.add))
                st.done(dve.reciprocal(gs[:, :], gs[:, :]))
                st.done(dve.tensor_scalar(gates[:, :, 1], rr[:, :], 1.0, None, ALU.add))
                st.done(dve.reciprocal(gates[:, :, 1], gates[:, :, 1]))
                st.done(dve.tensor_tensor(gates[:, :, 0], gates[:, :, 1], gs[:, :], ALU.mult))
                st.done(dve.tensor_tensor(gates[:, :, 1], gates[:, :, 0], rr[:, :], ALU.mult))
                dve.wait_ge(rank_mm, 1)
                st.done(dve.memset(pre[:, 0, :], 0.0))
                tot = PS[:, 1, 0:NT * NE].rearrange("p (n e) -> p n e", n=NT)
                for n in range(1, NT):
                    st.done(dve.tensor_tensor(pre[:, n, :], pre[:, n - 1, :], tot[:, n - 1, :], ALU.add))
                st.done(dve.tensor_tensor(cnt[:, :], pre[:, NT - 1, :], tot[:, NT - 1, :], ALU.add))
                st.done(dve.tensor_tensor(rank[:, :, :], pre[:, :, :], PS[:, 0, 0:NT * NE].rearrange("p (n e) -> p n e", n=NT), ALU.add))
                st.done(dve.tensor_scalar(ov[:, :], cnt[:, :], float(P), None, ALU.is_gt))
                for m in range(2, NT):
                    st.done(dve.scalar_tensor_tensor(out=ov[:, :], in0=cnt[:, :], scalar=float(P * m), in1=ov[:, :], op0=ALU.is_gt, op1=ALU.add))
                st.done(dve.tensor_copy(cum[:, 0, :], ov[:, :]))
                a = 0
                for sh in (1, 2, 4, 8, 16):
                    st.done(dve.tensor_copy(cum[:, 1 - a, 0:sh], cum[:, a, 0:sh]))
                    st.done(dve.tensor_tensor(cum[:, 1 - a, sh:NE], cum[:, a, sh:NE], cum[:, a, 0:NE - sh], ALU.add))
                    a = 1 - a
                incl = cum[:, a, :]
                st.done(dve.tensor_scalar(ia[:, :], iota[:, 0:NE], float(P), None, ALU.mult))
                st.done(dve.tensor_tensor(ib[:, :], incl, ov[:, :], ALU.subtract))
                st.done(dve.tensor_scalar(ib[:, :], ib[:, :], float(NE - 1), float(P), ALU.add, ALU.mult))
                st.done(dve.tensor_tensor(ib[:, :], ib[:, :], ia[:, :], ALU.subtract))
                st.done(dve.tensor_scalar(big[:, :, :], rank[:, :, :], float(P), None, ALU.is_ge))
                st.done(dve.tensor_tensor(big[:, :, :], big[:, :, :], ib[:, :].unsqueeze(1).to_broadcast([P, NT, NE]), ALU.mult))
                st.done(dve.tensor_tensor(rank[:, :, :], rank[:, :, :], big[:, :, :], ALU.add))
                st.done(dve.tensor_tensor(rank[:, :, :], rank[:, :, :], ia[:, :].unsqueeze(1).to_broadcast([P, NT, NE]), ALU.add))
                for k in range(2):
                    st.done(dve.tensor_tensor(tmpd[:, :, :], rank[:, :, :], Mk[:, k, :, :], ALU.mult))
                    st.done(dve.tensor_reduce(dest_f[:, :, k], tmpd[:, :, :], AX.X, ALU.add))
                for n in range(NT):
                    st.done(dve.tensor_scalar(tok[:, n:n + 1], kc[:, K_HO, 2:3], float(n * P), None, ALU.add))
                dve.tensor_copy(dest_i[:, :, :], dest_f[:, :, :]).then_inc(dest_ready, 1)
                st.done(dve.tensor_scalar(nb_f[:, 0:1], incl[:, NE - 1:NE], float(NE), None, ALU.add))
                st.done(dve.memset(nb_f[:, 1:2], float(NE - 1)))
                st.done(dve.tensor_tensor(cmp_[:, :, :], incl.unsqueeze(1).to_broadcast([P, 16, NE]),
                                          iota[:, 0:16].unsqueeze(2).to_broadcast([P, 16, NE]), ALU.is_le))
                st.done(dve.tensor_reduce(nb_f[:, 2:18], cmp_[:, :, :], AX.X, ALU.add))
                st.done(dve.tensor_scalar(nb_f[:, 2:18], nb_f[:, 2:18], float(NE - 1), None, ALU.min))
                st.done(dve.tensor_copy(plan[:, :], nb_f[0:1, :]))
                dve.wait_ge(l_turned, 1)
                st.done(dve.tensor_copy(slots_i[:, :], PS[:, 2, 0:LST]))

        n_chunks = len(chunks)
        SL = [(n_chunks + j) % 3 for j in range(3)]
        BASE = [seen[s] for s in SL]
        wg_s, wu_s = wring[SL[0]], wring[SL[1]]
        wd_s = wring[SL[2]][:, :, :].rearrange("p k n -> p (k n)").rearrange("p (k n) -> p k n", k=DE // P)
        KH = DE // P
        with ExitStack() as c, nc.Block() as block:
            new_phase(c)
            idxb = sb("idxb", [P, 1], I32, c=c)
            settle, settled = sb("settle", [P, 1], c=c), sb("settled", [P, 1], c=c)
            xg = sb("xg", [P, D], c=c)
            xT = sb("xT", [P, KD, P], c=c)
            sg = sb("sg", [P, DE], c=c)
            ac = sb("ac", [P, DE], c=c)
            aT = sb("aT", [P, KH, P], c=c)
            ysb = sb("ysb", [P, D], c=c)
            idx_ready, x_gathered = sem("idx_ready"), sem("x_gathered")
            x_turned, xT_ready, silu_ready, ac_ready, a_turned, aT_ready = (sem(n_) for n_ in (
                "x_turned", "xT_ready", "e_silu_ready", "ac_ready", "a_turned", "aT_ready"))
            y0_mm, ysb0_ready, ysb1_ready, y_stored = sem("y0_mm"), sem("ysb0_ready"), sem("ysb1_ready"), sem("y_stored")
            gate_done, up_done, down_done = (sem(n_) for n_ in ("gate_done", "up_done", "down_done"))

            def blocks(eng):
                return eng.value_load(plan[0:1, 0:1], min_val=NE, max_val=MAXB)

            @block.sync
            def _(sp):
                def load(j, e, i):
                    src = (w_g, w_u, w_d)[j]
                    src = src[e] if isinstance(e, int) else src[bass.ds(e, 1), :, :].rearrange("o a b -> (o a) b")
                    dst = (wg_s[:, :, :], wu_s[:, :, :], wd_s)[j]
                    sp.wait_ge((gate_done, up_done, down_done)[j], i + 1)
                    sp.dma_start(dst, src.rearrange("(k p) n -> p k n", p=P)).then_inc(w_loaded[SL[j]], 16)

                def expert(i):
                    return sp.value_load(plan[0:1, bass.ds(i - (NE - 2), 1)], min_val=0, max_val=NE - 1)

                load(0, 0, 0)
                load(1, 0, 0)
                with sp.Fori(1, NE) as i:
                    load(0, i, i)
                    load(2, i - 1, i - 1)
                    load(1, i, i)
                nb = blocks(sp)
                with sp.If(nb > NE):
                    with sp.Fori(NE, nb) as i:
                        e = expert(i)
                        load(0, e, i)
                        load(2, expert(i - 1), i - 1)
                        load(1, e, i)
                load(2, expert(nb - 1), nb - 1)

            @block.gpsimd
            def _(pool):
                nb = blocks(pool)
                with pool.Fori(0, nb) as i:
                    pool.wait_ge(x_turned, 2 * i + 1)
                    pool.tensor_copy(idxb[:, :], slots_i[:, bass.ds(i, 1)]).then_inc(idx_ready, 1)
                    pool.wait_ge(idx_ready, i + 1)
                    pool.tensor_tensor(settle[:, :], eps[:, :], eps[:, :], ALU.add)
                    pool.indirect_dma_start(xg[:, :], None, h2_dram, bass.IndirectOffsetOnAxis(ap=idxb[:, 0:1], axis=0))\
                        .then_inc(x_gathered, 16)

            @block.tensor
            def _(pe):
                def turn_x(b, i):
                    if b == 0:
                        pe.wait_ge(x_gathered, 16 * i + 16)
                    pe.wait_ge(xT_ready, 2 * i)
                    for k in range(4):
                        mm = pe.transpose(PS[:, b, k * P:(k + 1) * P], xg[:, (4 * b + k) * P:(4 * b + k + 1) * P], ident)
                    mm.then_inc(x_turned, 1)

                def gate(b, i):
                    if b == 0:
                        pe.wait_ge(w_loaded[SL[0]], 16 * i + BASE[0] + 16)
                        pe.wait_ge(silu_ready, i + 1)
                    pe.wait_ge(xT_ready, 2 * i + b + 2)
                    for k in range(4 * b, 4 * b + 4):
                        mm = pe.matmul(PS[:, 2, :], xT[:, k, :], wg_s[:, k, :], start=(k == 0), stop=(k == KD - 1))
                    if b == 1:
                        mm.then_inc(gate_done, 1)

                def up(b, i):
                    if b == 0:
                        pe.wait_ge(w_loaded[SL[1]], 16 * i + BASE[1] + 16)
                        pe.wait_ge(ac_ready, i + 1)
                    for k in range(4 * b, 4 * b + 4):
                        mm = pe.matmul(PS[:, 3, :], xT[:, k, :], wu_s[:, k, :], start=(k == 0), stop=(k == KD - 1))
                    if b == 1:
                        mm.then_inc(up_done, 1)

                def turn_a(i):
                    pe.wait_ge(ac_ready, i + 2)
                    pe.wait_ge(aT_ready, i + 1)
                    for k in range(KH):
                        mm = pe.transpose(PS[:, 4, k * P:(k + 1) * P], ac[:, k * P:(k + 1) * P], ident)
                    mm.then_inc(a_turned, 1)

                def down(i):
                    pe.wait_ge(w_loaded[SL[2]], 16 * i + BASE[2] + 16)
                    pe.wait_ge(aT_ready, i + 2)
                    for b, (s_mm, s_out) in enumerate(((y0_mm, ysb0_ready), (down_done, ysb1_ready))):
                        pe.wait_ge(s_out, i + 1)
                        for k in range(KH):
                            mm = pe.matmul(PS[:, 5 + b, :], aT[:, k, :], wd_s[:, k, 512 * b:512 * b + 512], start=(k == 0), stop=(k == KH - 1))
                        mm.then_inc(s_mm, 1)

                for s_ in (x_turned, gate_done, up_done, down_done):
                    pe.nop().then_inc(s_, 1)
                nb = blocks(pe)
                for b in range(2):
                    if b == 0:
                        pe.wait_ge(x_gathered, 16)
                    for k in range(4):
                        mm = pe.transpose(PS[:, b, k * P:(k + 1) * P], xg[:, (4 * b + k) * P:(4 * b + k + 1) * P], ident)
                    mm.then_inc(x_turned, 1)
                gate(0, 0)
                gate(1, 0)
                with pe.Fori(1, nb) as i:
                    up(0, i - 1)
                    turn_x(0, i)
                    up(1, i - 1)
                    turn_x(1, i)
                    gate(0, i)
                    turn_a(i - 1)
                    gate(1, i)
                    down(i - 1)
                up(0, nb - 1)
                up(1, nb - 1)
                turn_a(nb - 1)
                down(nb - 1)

            @block.scalar
            def _(act):
                act.preload_act_table_set("silu_and_others")
                for s_ in (silu_ready, aT_ready, ysb0_ready):
                    act.nop().then_inc(s_, 1)
                act.nop().then_inc(y_stored, 16)
                nb = blocks(act)
                with act.Fori(0, nb) as i:
                    act.wait_ge(gate_done, i + 2)
                    act.wait_ge(ac_ready, i + 1)
                    act.activation(sg[:, :], PS[:, 2, :], ACT.Silu).then_inc(silu_ready, 1)
                    act.wait_ge(a_turned, i + 1)
                    act.wait_ge(down_done, i + 1)
                    act.activation(aT[:, :, :], PS[:, 4, :].rearrange("p (k t) -> p k t", k=KH), ACT.Copy).then_inc(aT_ready, 1)
                    act.wait_ge(y0_mm, i + 1)
                    act.wait_ge(y_stored, 16 * i + 16)
                    act.activation(ysb[:, 0:512], PS[:, 5, :], ACT.Copy).then_inc(ysb0_ready, 1)
                    act.wait_ge(ysb0_ready, i + 2)
                    act.wait_ge(ysb1_ready, i + 2)
                    act.dma_start(y_dram[bass.ds(i * P, P), :], ysb[:, :]).then_inc(y_stored, 16)
                act.wait_ge(y_stored, 16 * nb + 16)
                act.activation(settled[:, :], eps[:, :], ACT.Copy)

            @block.vector
            def _(dve):
                def rows(b, i):
                    dve.wait_ge(x_turned, 2 * i + b + 2)
                    g = par("ffn_gain")[:, 4 * b:4 * b + 4].unsqueeze(2).to_broadcast([P, 4, P])
                    dve.tensor_tensor(xT[:, 4 * b:4 * b + 4, :], PS[:, b, :].rearrange("p (k t) -> p k t", k=4), g, ALU.mult)\
                       .then_inc(xT_ready, 1)

                def act_mul(i):
                    dve.wait_ge(up_done, i + 2)
                    dve.wait_ge(silu_ready, i + 2)
                    dve.tensor_tensor(ac[:, :], sg[:, :], PS[:, 3, :], ALU.mult).then_inc(ac_ready, 1)

                def y_half(i):
                    dve.wait_ge(down_done, i + 2)
                    dve.wait_ge(y_stored, 16 * i + 16)
                    dve.tensor_copy(ysb[:, 512:D], PS[:, 6, :]).then_inc(ysb1_ready, 1)

                for s_ in (xT_ready, ac_ready, ysb1_ready):
                    dve.nop().then_inc(s_, 1)
                nb = blocks(dve)
                rows(0, 0)
                rows(1, 0)
                with dve.Fori(1, nb) as i:
                    rows(0, i)
                    act_mul(i - 1)
                    rows(1, i)
                    y_half(i - 1)
                act_mul(nb - 1)
                y_half(nb - 1)

        with ExitStack() as c, nc.Block() as block:
            new_phase(c)
            yg = sb("yg", [P, 2, 2, D], c=c)
            y_gathered = [sem("y_gathered0"), sem("y_gathered1")]
            sum_ready, out_stored, cstep = sem("sum_ready"), sem("out_stored"), sem("c_step")

            @block.gpsimd
            def _(pool):
                for n in range(NT):
                    if n >= 2:
                        pool.wait_ge(sum_ready, n - 1)
                    for k in range(2):
                        pool.indirect_dma_start(yg[:, n % 2, k, :], None, y_dram,
                                                bass.IndirectOffsetOnAxis(ap=dest_i[:, n, k:k + 1], axis=0)).then_inc(y_gathered[n % 2], 16)

            @block.vector
            def _(dve):
                st = Steps(dve, cstep)
                for n in range(NT):
                    dve.wait_ge(y_gathered[n % 2], 32 * (n // 2 + 1))
                    st.done(dve.scalar_tensor_tensor(out=mix[:, n, :], in0=yg[:, n % 2, 0, :], scalar=gates[:, n, 0:1], in1=mix[:, n, :],
                                                     op0=ALU.mult, op1=ALU.add))
                    dve.scalar_tensor_tensor(out=mix[:, n, :], in0=yg[:, n % 2, 1, :], scalar=gates[:, n, 1:2], in1=mix[:, n, :],
                                             op0=ALU.mult, op1=ALU.add).then_inc(sum_ready, 1)

            @block.sync
            def _(sp):
                for n in range(NT):
                    sp.wait_ge(sum_ready, n + 1)
                    sp.dma_start(out[n * P:(n + 1) * P, :], mix[:, n, :]).then_inc(out_stored, 16)
                sp.wait_ge(out_stored, 16 * NT)
    return nc


def shape_constants(np, bf16):
    kc = np.zeros((P, NKC, P), np.float32)
    i = np.arange(P)
    kc[:, K_ID] = np.eye(P)
    kc[:, K_U] = i[:, None] <= i[None, :]
    kc[:, K_L] = i[:, None] > i[None, :]
    kc[:, K_ONE] = 1
    for l in range(7):
        same = (i[:, None] >> (l + 1)) == (i[None, :] >> (l + 1))
        kc[:, K_LM + l] = same & (((i[:, None] >> l) & 1) == 0) & (((i[None, :] >> l) & 1) == 1)
    for h in range(H_GLA):
        bd = kc[:, K_BD:K_BD + 2].reshape(P, GV)
        kc[:, K_BD + h // 2, (h % 2) * HD:(h % 2 + 1) * HD] = (i[:, None] // DK) == h
    kc[0:HD, K_HO, 0] = 1
    kc[HD:P, K_HO, 1] = 1
    kc[:, K_IOTA] = i[None, :]
    kc[:, K_HO, 2] = i
    km = np.zeros((P, 5, P), np.float32)
    km[:, 0] = np.eye(P)
    km[:, 1] = np.where(i[None, :] > i[:, None], NEG, 0)
    km[:, 2] = np.where(i[:, None] > i[None, :], NEG, 0)
    km[:, 3] = np.where(i[:, None] >= i[None, :], NEG, 0)
    km[:, 4] = i[:, None] < i[None, :]
    return kc, km.astype(bf16)


def layout(np, inputs):
    a = {k: np.asarray(v)[0] if k != "x" else np.asarray(v)[0] for k, v in inputs.items()}

    def cols(v):
        return np.ascontiguousarray(v.reshape(-1, P).T)

    def rows(v):
        return np.broadcast_to(v[None, :], (P, v.shape[0]))

    prm = np.concatenate([cols(a["attn_norm"]), cols(a["ffn_norm"]), rows(a["fox_q_norm"]), rows(a["fox_k_norm"]),
                          rows(a["fox_o_norm"]), rows(a["gdn_o_norm"]), rows(a["gla_o_norm"]), rows(a["fox_f_bias"]),
                          rows(a["gdn_dt_bias"]), rows(a["gdn_a_log"]),
                          a["gdn_conv"].reshape(4, 9, P).transpose(2, 1, 0).reshape(P, 36),
                          rows(a["b_router_group"]), rows(a["b_router_expert"]), rows(a["gla_b_a"])], axis=1)
    return {
        "x": a["x"], "w_in": a["w_in"], "w_out": a["w_out"],
        "w_router": np.concatenate([a["w_router_group"], a["w_router_expert"]], axis=1),
        "w_a2": a["gla_w_a2"], "w_g": a["w_expert_gate"], "w_u": a["w_expert_up"], "w_d": a["w_expert_down"],
        "params": np.ascontiguousarray(prm),
    }


def kernel(**inputs):
    import numpy as np
    import ml_dtypes
    import concourse.bacc as bacc
    from concourse.bass_utils import run_bass_kernel_spmd

    nc = bacc.Bacc("TRN2", target_bir_lowering=False, num_devices=1)
    data = layout(np, inputs)
    data["consts"], data["masks"] = shape_constants(np, ml_dtypes.bfloat16)
    arrays, args = {}, {}
    for name, v in data.items():
        v = np.ascontiguousarray(v)
        arrays["in_" + name] = v
        args[name] = nc.dram_tensor("in_" + name, v.shape, mybir.dt.from_np(v.dtype), kind="ExternalInput").ap()
    out = nc.dram_tensor("out_0", (S, D), F32, kind="ExternalOutput").ap()
    trunk_kernel(nc, out=out, **args)
    r = run_bass_kernel_spmd(nc, [arrays], core_ids=[0])
    return r.results[0]["out_0"].reshape(1, S, D)
```

```python
import math
from contextlib import ExitStack

import concourse.bass as bass
from concourse import mybir

P = 128
S = 1024
D = 1024
KD = D // P
NT = S // P
HD = 64
H_FOX, H_GDN, H_GLA = 6, 6, 4
FOX, GDN = H_FOX * HD, H_GDN * HD
DK, GK, GV = 32, 128, 256
RANK = 16
NG, EPG, NE = 4, 8, 32
DE = 512
EPS = 1e-6
NEG = -1e30
MAXB = NE + 2 * S // P - 1
LST = 48

F32 = mybir.dt.float32
BF16 = mybir.dt.bfloat16
I32 = mybir.dt.int32
U32 = mybir.dt.uint32
ALU = mybir.AluOpType
ACT = mybir.ActivationFunctionType
AX = mybir.AxisListType

C_FQ, C_FK, C_FV = 0, FOX, 2 * FOX
C_GQKV = 3 * FOX + H_FOX
C_GATE = C_GQKV + 3 * GDN
C_LQ = C_GATE + GDN + 2 * H_GDN
C_LV = C_LQ + 2 * GK
C_LA = C_LV + 2 * GV
N_IN = C_LA + RANK
W_VF = FOX + H_FOX
W_GAB = GDN + 2 * H_GDN

(K_ID, K_U, K_L, K_ONE, K_LM) = (0, 1, 2, 3, 4)
KR = 96
K_BD = 11
K_HO = 13
K_IOTA = 14
NKC = 15
PC = {}
_at = 0
for _n, _w in (("attn_gain", KD), ("ffn_gain", KD), ("fox_q", HD), ("fox_k", HD), ("fox_o", HD), ("gdn_o", HD),
               ("gla_o", HD), ("f_bias", H_FOX), ("dt_bias", H_GDN), ("a_log", H_GDN), ("conv", 36),
               ("b_rg", NG), ("b_re", NE), ("b_a", GK)):
    PC[_n] = (_at, _at + _w)
    _at += _w
NPC = _at


class Steps:

    def __init__(self, eng, sem):
        self.eng, self.sem, self.n = eng, sem, 0

    def done(self, ins):
        self.n += 1
        ins.then_inc(self.sem, 1)
        self.eng.wait_ge(self.sem, self.n)


def trunk_kernel(nc, x, w_in, w_out, w_router, w_a2, w_g, w_u, w_d, params, consts, masks, out):
    ctx = ExitStack()

    names = {}

    def sb(name, shape, dt=F32, c=None):
        names[name] = names.get(name, -1) + 1
        name += f"_{names[name]}" if names[name] else ""
        return (c or ctx).enter_context(nc.sbuf_tensor(name, shape, dt))

    phase_sems = [None]

    def sem(name):
        handle = nc.alloc_semaphore(name)
        if phase_sems[0] is not None:
            phase_sems[0].append(handle)
        return handle

    def new_phase(c):
        phase_sems[0] = []
        c.callback(end_phase)

    def end_phase():
        nc.clear_and_free_semaphores(phase_sems[0])
        nc.all_engine_barrier()
        phase_sems[0] = None

    with ctx:
        PS = ctx.enter_context(nc.psum_tensor("PS", [P, 8, 512], F32))
        kc = sb("kc", [P, NKC, P])
        km = sb("km", [P, 5, P], BF16)
        prm = sb("prm", [P, NPC])
        eps = sb("eps", [P, 1])
        eps_hd = sb("eps_hd", [P, 1])
        wring = [sb(f"wring{i}", [P, KD, 512]) for i in range(3)]
        hT = sb("hT", [P, KD, S])
        mix = sb("mix", [P, NT, D])
        h2_dram = nc.dram_tensor("h2_scratch", (S, D), F32, kind="Internal").ap()
        y_dram = nc.dram_tensor("y_scratch", (MAXB * P, D), F32, kind="Internal").ap()
        list_dram = nc.dram_tensor("list_scratch", (LST * P, 1), F32, kind="Internal").ap()

        ident, U, L, ones = (kc[:, i, :] for i in (K_ID, K_U, K_L, K_ONE))
        identb, mask_q, mask_incl, mask_strict, before = (km[:, i, :] for i in range(5))

        def par(name):
            a, b = PC[name]
            return prm[:, a:b]

        w_loaded = [sem(f"w_loaded{i}") for i in range(3)]
        w_used = sem("w_used")
        const_loaded = sem("const_loaded")

        w_in_v = w_in.rearrange("(k p) n -> p k n", p=P)
        w_out_v = w_out.rearrange("(k p) n -> p k n", p=P)
        chunks = [[(w_in_v[:, :, a:b], 0)] for a, b in
                  ((C_FV, C_FV + W_VF), (C_FQ, C_FK), (C_FK, C_FV),
                   (C_GQKV, C_GQKV + 512), (C_GQKV + 512, C_GQKV + 1024), (C_GQKV + 1024, C_GATE),
                   (C_GATE, C_LQ), (C_LQ, C_LV), (C_LV, C_LA))]
        chunks[7].append((w_in_v[:, :, C_LA:N_IN], 2 * GK))
        chunks += [[(w_out_v[:, :, a:a + 512], 0)] for a in (0, 512)]
        CH_VF, CH_Q, CH_K, CH_T0, CH_T1, CH_T2, CH_GAB, CH_L, CH_LVR, CH_O0, CH_O1 = range(11)
        n_loads, seen = [], [0, 0, 0]
        for c, parts in enumerate(chunks):
            seen[c % 3] += 16 * len(parts)
            n_loads.append(seen[c % 3])

        def load_chunk(eng, c):
            if c >= 3:
                eng.wait_ge(w_used, c - 2)
            for src, at in chunks[c]:
                eng.dma_start(wring[c % 3][:, :, at:at + src.shape[2]], src).then_inc(w_loaded[c % 3], 16)

        def chunk_ready(eng, c):
            eng.wait_ge(w_loaded[c % 3], n_loads[c])

        def project_tile(pe, c, n, bank, cols):
            for k in range(KD):
                mm = pe.matmul(PS[:, bank, 0:cols], hT[:, k, n * P:(n + 1) * P], wring[c % 3][:, k, 0:cols],
                               start=(k == 0), stop=(k == KD - 1))
            return mm

        with ExitStack() as c, nc.Block() as block:
            new_phase(c)
            xin = sb("xin", [P, 2, D], c=c)
            junk = sb("junk", [P, D], c=c)
            ss = sb("ss", [P, NT], c=c)
            lnss = sb("lnss", [P, NT], c=c)
            rstd = sb("rstd", [P, NT], c=c)
            x_loaded = [sem("x_loaded0"), sem("x_loaded1")]
            rstd_ready, act_step = sem("rstd_ready"), sem("act_step")
            h_ready, h_turned, hT_ready, eps_ready = sem("h_ready"), sem("h_turned"), sem("hT_ready"), sem("eps_ready")

            @block.sync
            def _(sp):
                sp.dma_start(xin[:, 0, :], x[0:P, :]).then_inc(x_loaded[0], 16)
                sp.dma_start(xin[:, 1, :], x[P:2 * P, :]).then_inc(x_loaded[1], 16)
                sp.dma_start(prm[:, :], params).then_inc(const_loaded, 16)
                sp.dma_start(kc[:, :, :], consts).then_inc(const_loaded, 16)
                sp.dma_start(km[:, :, :], masks).then_inc(const_loaded, 16)
                for k in range(3):
                    load_chunk(sp, k)
                for n in range(2, NT):
                    sp.wait_ge(h_turned, 2 * (n - 1))
                    sp.dma_start(xin[:, n % 2, :], x[n * P:(n + 1) * P, :]).then_inc(x_loaded[n % 2], 16)

            @block.gpsimd
            def _(pool):
                pool.memset(eps_hd[:, :], EPS * HD).then_inc(eps_ready, 1)
                pool.memset(eps[:, :], EPS).then_inc(eps_ready, 1)

            @block.scalar
            def _(act):
                st = Steps(act, act_step)
                act.wait_ge(eps_ready, 2)
                act.preload_act_table_set("natural_log_exp_and_others")
                for n in range(NT):
                    act.wait_ge(x_loaded[n % 2], 16 * (n // 2 + 1))
                    st.done(act.activation(junk[:, :], xin[:, n % 2, :], ACT.Square, accum_out=ss[:, n:n + 1]))
                    st.done(act.activation(lnss[:, n:n + 1], ss[:, n:n + 1], ACT.Ln, bias=eps[:, :], scale=1.0 / D))
                    act.activation(rstd[:, n:n + 1], lnss[:, n:n + 1], ACT.Exp, scale=-0.5).then_inc(rstd_ready, 1)

            @block.vector
            def _(dve):
                dve.wait_ge(const_loaded, 48)
                for n in range(NT):
                    dve.wait_ge(rstd_ready, n + 1)
                    dve.tensor_scalar(xin[:, n % 2, :], xin[:, n % 2, :], rstd[:, n:n + 1], None, ALU.mult).then_inc(h_ready, 1)
                    for b in range(2):
                        dve.wait_ge(h_turned, 2 * n + b + 1)
                        bank = 2 * (n % 2) + b
                        g = par("attn_gain")[:, 4 * b:4 * b + 4].unsqueeze(2).to_broadcast([P, 4, P])
                        dve.tensor_tensor(hT[:, 4 * b:4 * b + 4, n * P:(n + 1) * P],
                                          PS[:, bank, :].rearrange("p (k t) -> p k t", k=4), g, ALU.mult).then_inc(hT_ready, 1)

            @block.tensor
            def _(pe):
                pe.wait_ge(const_loaded, 48)
                for n in range(NT):
                    pe.wait_ge(h_ready, n + 1)
                    for b in range(2):
                        if n >= 2:
                            pe.wait_ge(hT_ready, 2 * (n - 2) + b + 1)
                        for k in range(4):
                            kk = 4 * b + k
                            t = pe.transpose(PS[:, 2 * (n % 2) + b, k * P:(k + 1) * P],
                                             xin[:, n % 2, kk * P:(kk + 1) * P], ident)
                        t.then_inc(h_turned, 1)

        with ExitStack() as fc:
            vf = sb("vf", [P, NT, W_VF], c=fc)
            qT = sb("qT", [KR, H_FOX, S], c=fc)
            kT = sb("kT", [KR, H_FOX, S], c=fc)
            with ExitStack() as c, nc.Block() as block:
                new_phase(c)
                fx = sb("fx", [P, NT, H_FOX], c=c)
                fmin = sb("fmin", [P, NT, H_FOX], c=c)
                fexp = sb("fexp", [P, NT, H_FOX], c=c)
                carry = sb("carry", [P, NT, H_FOX], c=c)
                neg_cum = sb("neg_cum", [P, NT, H_FOX], c=c)
                sq = sb("sq", [P, 2, FOX], c=c)
                qn = sb("qn", [P, 2, H_FOX, KR], c=c)
                ss = sb("ss", [P, 2, H_FOX], c=c)
                lns = sb("lns", [P, 2, H_FOX], c=c)
                rq = sb("rq", [P, 2, H_FOX], c=c)
                proj_ready, vf_ready, sq_ready, ss_ready = sem("fproj"), sem("vf_ready"), sem("fsq"), sem("fss")
                r_ready, qn_ready, qn_turned, qT_ready = sem("fr"), sem("fqn"), sem("fqnt"), sem("fqT")
                fx_ready, lf_act, lf_ready, cs_ready, cum_ready = (sem("ffx"), sem("lf_act"), sem("lf_ready"),
                                                                   sem("cs_ready"), sem("cum_ready"))
                dstep, astep = sem("f_dve_step"), sem("f_act_step")
                UNITS = [(c_, n) for c_ in (CH_Q, CH_K) for n in range(NT)]

                @block.sync
                def _(sp):
                    for k in range(3, 6):
                        load_chunk(sp, k)

                @block.tensor
                def _(pe):
                    chunk_ready(pe, CH_VF)
                    for n in range(NT):
                        if n >= 2:
                            pe.wait_ge(vf_ready, n - 1)
                        mm = project_tile(pe, CH_VF, n, n % 2, W_VF)
                        mm.then_inc(proj_ready, 1)
                        if n == NT - 1:
                            pe.wait_ge(proj_ready, NT)
                            pe.nop().then_inc(w_used, 1)

                    def turn(u):
                        pe.wait_ge(qn_ready, u + 1)
                        for b in range(2):
                            if u >= 1:
                                pe.wait_ge(qT_ready, 2 * (u - 1) + b + 1)
                            for j in range(3):
                                t = pe.transpose(PS[0:KR, 4 + b, j * P:(j + 1) * P], qn[:, u % 2, 3 * b + j, :], ident)
                            t.then_inc(qn_turned, 1)

                    for u, (ch, n) in enumerate(UNITS):
                        if n == 0:
                            chunk_ready(pe, ch)
                        if u >= 2:
                            pe.wait_ge(qn_ready, u - 1)
                        else:
                            pe.wait_ge(vf_ready, NT)
                        mm = project_tile(pe, ch, n, u % 2, FOX)
                        mm.then_inc(proj_ready, 1)
                        if n == NT - 1:
                            pe.wait_ge(proj_ready, NT + u + 1)
                            pe.nop().then_inc(w_used, 1)
                        if u == 1:
                            pe.wait_ge(lf_ready, 1)
                            lf = fx[:, :, :].rearrange("p n h -> p (n h)")
                            pe.matmul(PS[:, 6, 0:NT * H_FOX], U, lf, start=True, stop=True)
                            pe.matmul(PS[:, 7, 0:NT * H_FOX], ones, lf, start=True, stop=True).then_inc(cs_ready, 1)
                        if u >= 1:
                            turn(u - 1)
                    turn(len(UNITS) - 1)

                @block.scalar
                def _(act):
                    st = Steps(act, astep)
                    for n in range(NT):
                        act.wait_ge(proj_ready, n + 1)
                        act.activation(vf[:, n, :], PS[:, n % 2, 0:W_VF], ACT.Copy).then_inc(vf_ready, 1)
                    act.wait_ge(fx_ready, 1)
                    st.done(act.activation(fexp[:, :, :], fx[:, :, :], ACT.Abs))
                    st.done(act.activation(fexp[:, :, :], fexp[:, :, :], ACT.Exp, scale=-1.0))
                    act.activation(fexp[:, :, :], fexp[:, :, :], ACT.Ln, bias=1.0).then_inc(lf_act, 1)

                    def evac(u):
                        ch, n = UNITS[u]
                        dst = qT if ch == CH_Q else kT
                        for b in range(2):
                            act.wait_ge(qn_turned, 2 * u + b + 1)
                            act.activation(dst[:, 3 * b:3 * b + 3, n * P:(n + 1) * P],
                                           PS[0:KR, 4 + b, 0:3 * P].rearrange("p (h t) -> p h t", h=3),
                                           ACT.Copy).then_inc(qT_ready, 1)

                    for u, (ch, n) in enumerate(UNITS):
                        i = u % 2
                        act.wait_ge(proj_ready, NT + u + 1)
                        if u >= 2:
                            act.wait_ge(ss_ready, u - 1)
                        act.activation(sq[:, i, :], PS[:, i, 0:FOX], ACT.Square).then_inc(sq_ready, 1)
                        act.wait_ge(ss_ready, u + 1)
                        q_unit = ch == CH_Q
                        st.done(act.activation(lns[:, i, :], ss[:, i, :], ACT.Ln, bias=eps_hd[:, :] if q_unit else eps[:, :],
                                               scale=1.0 if q_unit else 1.0 / HD))
                        if u >= 2:
                            act.wait_ge(qn_ready, u - 1)
                        act.activation(rq[:, i, :], lns[:, i, :], ACT.Exp, scale=-0.5).then_inc(r_ready, 1)
                        if u >= 1:
                            evac(u - 1)
                    evac(len(UNITS) - 1)

                @block.vector
                def _(dve):
                    st = Steps(dve, dstep)
                    st.done(dve.memset(qn[:, :, :, :], 0.0))
                    st.done(dve.memset(qn[:, :, :, HD:HD + 1], 1.0))
                    dve.wait_ge(vf_ready, NT)
                    fb = par("f_bias").unsqueeze(1).to_broadcast([P, NT, H_FOX])
                    dve.tensor_tensor(fx[:, :, :], vf[:, :, FOX:W_VF], fb, ALU.add).then_inc(fx_ready, 1)
                    dve.wait_ge(fx_ready, 1)
                    st.done(dve.tensor_scalar(fmin[:, :, :], fx[:, :, :], 0.0, None, ALU.min))
                    dve.wait_ge(lf_act, 1)
                    dve.tensor_tensor(fx[:, :, :], fmin[:, :, :], fexp[:, :, :], ALU.subtract).then_inc(lf_ready, 1)

                    def cumulate():
                        dve.wait_ge(cs_ready, 1)
                        st.done(dve.memset(carry[:, 0, :], 0.0))
                        tot = PS[:, 7, 0:NT * H_FOX].rearrange("p (n h) -> p n h", h=H_FOX)
                        for n in range(1, NT):
                            st.done(dve.tensor_tensor(carry[:, n, :], carry[:, n - 1, :], tot[:, n - 1, :], ALU.add))
                        st.done(dve.tensor_tensor(neg_cum[:, :, :], carry[:, :, :],
                                                  PS[:, 6, 0:NT * H_FOX].rearrange("p (n h) -> p n h", h=H_FOX), ALU.add))
                        st.done(dve.tensor_scalar(neg_cum[:, :, :], neg_cum[:, :, :], -1.0, None, ALU.mult))

                    for u, (ch, n) in enumerate(UNITS):
                        i = u % 2
                        dve.wait_ge(sq_ready, u + 1)
                        dve.tensor_reduce(ss[:, i, :], sq[:, i, :].rearrange("p (h d) -> p h d", h=H_FOX), AX.X,
                                          ALU.add).then_inc(ss_ready, 1)
                        if u == 1:
                            cumulate()
                        dve.wait_ge(r_ready, u + 1)
                        if u >= 2:
                            dve.wait_ge(qn_turned, 2 * (u - 1))
                        rows = qn[:, i, :, 0:HD]
                        st.done(dve.tensor_tensor(rows, PS[:, i, 0:FOX].rearrange("p (h d) -> p h d", h=H_FOX),
                                                  rq[:, i, :].unsqueeze(2).to_broadcast([P, H_FOX, HD]), ALU.mult))
                        if ch == CH_K:
                            st.done(dve.tensor_copy(qn[:, i, :, HD], neg_cum[:, n, :]))
                        g = par("fox_q" if ch == CH_Q else "fox_k").unsqueeze(1).to_broadcast([P, H_FOX, HD])
                        dve.tensor_tensor(rows, rows, g, ALU.mult).then_inc(qn_ready, 1)

            with ExitStack() as c, nc.Block() as block:
                new_phase(c)
                pr = sb("pr", [P, 2, S], c=c)
                prT = sb("prT", [P, 2, NT, P], c=c)
                mx = sb("mx", [P, 2], c=c)
                den = sb("den", [P, 4], c=c)
                rden = sb("rden", [P, 2], c=c)
                sq = sb("sq2", [P, FOX], c=c)
                ss = sb("ss2", [P, H_FOX], c=c)
                rr = sb("rr2", [P, H_FOX], c=c)
                logits, mx_ready, p_ready = sem("logits"), sem("mx_ready"), sem("p_ready")
                p_turned, pT_ready, pv_ready, o_ready = sem("p_turned"), sem("pT_ready"), sem("pv_ready"), sem("o_ready")
                osq_ready, oss_ready, orr_ready, on_ready = sem("osq"), sem("oss"), sem("orr"), sem("on")
                dstep, astep = sem("a_dve_step"), sem("a_act_step")
                ATT = [(n, h) for n in range(NT) for h in range(H_FOX)]
                GR = [(u, g) for u, (n, h) in enumerate(ATT) for g in range((n + 4) // 4)]
                G0 = [sum(1 for x_ in GR if x_[0] < u) for u in range(len(ATT) + 1)]

                @block.sync
                def _(sp):
                    pass

                @block.tensor
                def _(pe):
                    def qk(u):
                        n, h = ATT[u]
                        i = u % 2
                        if u >= 2:
                            pe.wait_ge(p_ready, u - 1)
                        keys = (n + 1) * P
                        for a in range(0, keys, 512):
                            w = min(512, keys - a)
                            last = a + w == keys
                            mm = pe.matmul(PS[:, 2 * i + a // 512, 0:w], qT[:, h, n * P:(n + 1) * P], kT[:, h, a:a + w],
                                           start=True, stop=not last)
                        pe.matmul(PS[:, 2 * i + (keys - 1) // 512, w - P:w], identb, mask_q, start=False, stop=True)\
                          .then_inc(logits, 1)

                    def turn(u):
                        n, h = ATT[u]
                        i = u % 2
                        pe.wait_ge(p_ready, u + 1)
                        for g in range((n + 4) // 4):
                            G = G0[u] + g
                            if G >= 2:
                                pe.wait_ge(pT_ready, G - 1)
                            k0, k1 = 4 * g, min(4 * g + 4, n + 1)
                            for k in range(k0, k1):
                                t = pe.transpose(PS[:, 4 + G % 2, (k - k0) * P:(k - k0 + 1) * P], pr[:, i, k * P:(k + 1) * P], ident)
                            t.then_inc(p_turned, 1)

                    def pv(u):
                        n, h = ATT[u]
                        i = u % 2
                        if u >= 2:
                            pe.wait_ge(o_ready, u - 1)
                        for g in range((n + 4) // 4):
                            pe.wait_ge(pT_ready, G0[u] + g + 1)
                            for k in range(4 * g, min(4 * g + 4, n + 1)):
                                mm = pe.matmul(PS[:, 6 + i, 0:HD], prT[:, i, k, :], vf[:, k, h * HD:(h + 1) * HD],
                                               start=(k == 0), stop=(k == n))
                        mm.then_inc(pv_ready, 1)

                    for u in range(len(ATT) + 2):
                        if u < len(ATT):
                            qk(u)
                        if 1 <= u <= len(ATT):
                            turn(u - 1)
                        if u >= 2:
                            pv(u - 2)

                def norm_act(act, st, n):
                    act.wait_ge(o_ready, H_FOX * (n + 1))
                    if n >= 1:
                        act.wait_ge(on_ready, n)
                    act.activation(sq[:, :], mix[:, n, 0:FOX], ACT.Square).then_inc(osq_ready, 1)
                    act.wait_ge(oss_ready, n + 1)
                    st.done(act.activation(rr[:, :], ss[:, :], ACT.Ln, bias=eps[:, :], scale=1.0 / HD))
                    act.activation(rr[:, :], rr[:, :], ACT.Exp, scale=-0.5).then_inc(orr_ready, 1)

                @block.scalar
                def _(act):
                    st = Steps(act, astep)

                    def copy_turned(u):
                        n, i = ATT[u][0], u % 2
                        if u >= 2:
                            act.wait_ge(pv_ready, u - 1)
                        for g in range((n + 4) // 4):
                            G = G0[u] + g
                            k0, k1 = 4 * g, min(4 * g + 4, n + 1)
                            act.wait_ge(p_turned, G + 1)
                            act.activation(prT[:, i, k0:k1, :].rearrange("p k q -> p (k q)"), PS[:, 4 + G % 2, 0:(k1 - k0) * P],
                                           ACT.Copy).then_inc(pT_ready, 1)

                    for u, (n, h) in enumerate(ATT):
                        i = u % 2
                        keys = (n + 1) * P
                        act.wait_ge(mx_ready, u + 1)
                        if u >= 2:
                            act.wait_ge(p_turned, G0[u - 1])
                        if u >= 4:
                            act.wait_ge(o_ready, u - 3)
                        lg = PS[:, 2 * i:2 * i + 2, :].rearrange("p b k -> p (b k)")[:, 0:keys]
                        act.activation(pr[:, i, 0:keys], lg, ACT.Exp, bias=mx[:, i:i + 1],
                                       accum_out=den[:, u % 4:u % 4 + 1]).then_inc(p_ready, 1)
                        if u >= 1:
                            copy_turned(u - 1)
                        if h == 2 and n >= 1:
                            norm_act(act, st, n - 1)
                    copy_turned(len(ATT) - 1)
                    norm_act(act, st, NT - 1)

                @block.vector
                def _(dve):
                    st = Steps(dve, dstep)

                    def norm(n):
                        dve.wait_ge(osq_ready, n + 1)
                        dve.tensor_reduce(ss[:, :], sq[:, :].rearrange("p (h d) -> p h d", h=H_FOX), AX.X, ALU.add)\
                           .then_inc(oss_ready, 1)
                        dve.wait_ge(orr_ready, n + 1)
                        o = mix[:, n, 0:FOX].rearrange("p (h d) -> p h d", h=H_FOX)
                        st.done(dve.tensor_tensor(o, o, rr[:, :].unsqueeze(2).to_broadcast([P, H_FOX, HD]), ALU.mult))
                        dve.tensor_tensor(o, o, par("fox_o").unsqueeze(1).to_broadcast([P, H_FOX, HD]), ALU.mult)\
                           .then_inc(on_ready, 1)

                    def finish(u):
                        n, h = ATT[u]
                        i = u % 2
                        dve.wait_ge(pv_ready, u + 1)
                        st.done(dve.reciprocal(rden[:, i:i + 1], den[:, u % 4:u % 4 + 1]))
                        dve.tensor_scalar(mix[:, n, h * HD:(h + 1) * HD], PS[:, 6 + i, 0:HD], rden[:, i:i + 1], None,
                                          ALU.mult).then_inc(o_ready, 1)

                    for u, (n, h) in enumerate(ATT):
                        i = u % 2
                        keys = (n + 1) * P
                        dve.wait_ge(logits, u + 1)
                        if u >= 2:
                            dve.wait_ge(p_ready, u - 1)
                        lg = PS[:, 2 * i:2 * i + 2, :].rearrange("p b k -> p (b k)")[:, 0:keys]
                        dve.tensor_reduce(mx[:, i:i + 1], lg, AX.X, ALU.max, negate=True).then_inc(mx_ready, 1)
                        if u >= 2:
                            finish(u - 2)
                        if h == 2 and n >= 1:
                            norm(n - 1)
                    finish(len(ATT) - 2)
                    finish(len(ATT) - 1)
                    norm(NT - 1)
        with ExitStack() as gc:
            qkvT = sb("qkvT", [P, 9, S], c=gc)
            sgate = mix[:, :, FOX:FOX + GDN]
            N6 = [P, NT, H_GDN]
            g_ = sb("g_log", N6, c=gc)
            row_a, row_q = sb("row_a", N6, c=gc), sb("row_q", N6, c=gc)
            bias_j = sb("bias_j", N6, c=gc)
            beta, s_w, s_kd, s_q = (sb(n_, N6, c=gc) for n_ in ("beta", "s_w", "s_kd", "s_q"))
            e_last = sb("e_last", [P, NT, H_GDN // 2], c=gc)
            with ExitStack() as c, nc.Block() as block:
                new_phase(c)
                raw = sb("raw", [P, 2, S + 3], c=c)
                conv = sb("conv", [P, 2, S], c=c)
                sqT = sb("sqT", [P, S], c=c)
                ab = sb("ab", [P, NT, 2 * H_GDN], c=c)
                lnr = sb("lnr", [P, NT, 2 * H_GDN], c=c)
                t1, t2, t3 = (sb(n_, [P, NT, 2 * H_GDN], c=c) for n_ in ("t1", "t2", "t3"))
                ealog = sb("ealog", [P, H_GDN], c=c)
                projT, raw_ready, conv_ready, silu_ready = sem("projT"), sem("raw_ready"), sem("conv_ready"), sem("silu_ready")
                sqT_ready, sumsq_ready, gate_proj, gate_ready = sem("sqT_ready"), sem("sumsq"), sem("gate_proj"), sem("gate_ready")
                sc_dve, sc_act, sc_pe = sem("sc_dve"), sem("sc_act"), sem("sc_pe")
                dstep, astep, pads = sem("g_dve_step"), sem("g_act_step"), sem("pads")

                @block.sync
                def _(sp):
                    for k in range(6, 9):
                        load_chunk(sp, k)

                @block.tensor
                def _(pe):
                    def sumsq(g):
                        pe.wait_ge(sqT_ready, g + 1)
                        for n in range(NT):
                            at = n * 12 + 2 * g
                            mm = pe.matmul(PS[:, 6, at:at + 2], sqT[:, n * P:(n + 1) * P], kc[:, K_HO, 0:2], start=True, stop=True)
                        mm.then_inc(sumsq_ready, 1)

                    for g in range(9):
                        ch = CH_T0 + g // 4
                        if g % 4 == 0:
                            chunk_ready(pe, ch)
                        for b in range(2):
                            if g >= 2:
                                pe.wait_ge(raw_ready, 2 * (g - 2) + b + 1)
                            for k in range(KD):
                                mm = pe.matmul(PS[:, 2 * (g % 2) + b, :], wring[ch % 3][:, k, (g % 4) * P:(g % 4 + 1) * P],
                                               hT[:, k, 512 * b:512 * b + 512], start=(k == 0), stop=(k == KD - 1))
                            mm.then_inc(projT, 1)
                        if g % 4 == 3 or g == 8:
                            pe.wait_ge(projT, 2 * g + 2)
                            pe.nop().then_inc(w_used, 1)
                        if 1 <= g <= 6:
                            sumsq(g - 1)
                    chunk_ready(pe, CH_GAB)
                    for n in range(NT):
                        if n >= 2:
                            pe.wait_ge(gate_ready, n - 1)
                        project_tile(pe, CH_GAB, n, 4 + n % 2, W_GAB).then_inc(gate_proj, 1)
                    pe.wait_ge(gate_proj, NT)
                    pe.nop().then_inc(w_used, 1)
                    pe.wait_ge(sc_dve, 2)
                    for j, m in enumerate((U, L, ones)):
                        mm = pe.matmul(PS[:, 7, 48 * j:48 * j + 48], m, g_[:, :, :].rearrange("p n h -> p (n h)"), start=True, stop=True)
                    mm.then_inc(sc_pe, 1)

                @block.scalar
                def _(act):
                    st = Steps(act, astep)

                    def silu(g):
                        act.wait_ge(conv_ready, g + 1)
                        act.activation(qkvT[:, g, :], conv[:, g % 2, :], ACT.Silu).then_inc(silu_ready, 1)
                        if g < 6:
                            act.wait_ge(silu_ready, g + 1)
                            if g >= 1:
                                act.wait_ge(sumsq_ready, g)
                            act.activation(sqT[:, :], qkvT[:, g, :], ACT.Square).then_inc(sqT_ready, 1)

                    act.preload_act_table_set("silu_and_others")
                    act.wait_ge(pads, 1)
                    for g in range(9):
                        for b in range(2):
                            act.wait_ge(projT, 2 * g + b + 1)
                            if g >= 2:
                                act.wait_ge(conv_ready, g - 1)
                            act.activation(raw[:, g % 2, 3 + 512 * b:515 + 512 * b], PS[:, 2 * (g % 2) + b, :], ACT.Copy)\
                               .then_inc(raw_ready, 1)
                        if g >= 1:
                            silu(g - 1)
                    silu(8)
                    for n in range(NT):
                        act.wait_ge(gate_proj, n + 1)
                        st.done(act.activation(sgate[:, n, :], PS[:, 4 + n % 2, 0:GDN], ACT.Silu))
                        act.activation(ab[:, n, :], PS[:, 4 + n % 2, GDN:W_GAB], ACT.Copy).then_inc(gate_ready, 1)
                    act.wait_ge(sc_dve, 1)
                    act.preload_act_table_set("natural_log_exp_and_others")
                    st.done(act.activation(t2[:, :, :], t1[:, :, :], ACT.Abs))
                    st.done(act.activation(t2[:, :, :], t2[:, :, :], ACT.Exp, scale=-1.0))
                    st.done(act.activation(t2[:, :, :], t2[:, :, :], ACT.Ln, bias=1.0))
                    act.wait_ge(sumsq_ready, 6)
                    st.done(act.activation(lnr[:, :, :], PS[:, 6, 0:96].rearrange("p (n h) -> p n h", n=NT), ACT.Ln, bias=eps[:, :]))
                    act.activation(ealog[:, :], par("a_log"), ACT.Exp).then_inc(sc_act, 1)
                    act.wait_ge(sc_dve, 3)
                    for t, src in ((beta, beta), (s_w, row_a), (s_kd, s_kd), (s_q, row_q)):
                        st.done(act.activation(t[:, :, :], src[:, :, :], ACT.Exp))
                    for h in range(2):
                        tot = PS[64 * h:64 * h + 64, 7, 96:144].rearrange("p (n a s) -> p n a s", n=NT, s=2)[:, :, :, h]
                        st.done(act.activation(e_last[64 * h:64 * h + 64, :, :], tot, ACT.Exp))

                @block.vector
                def _(dve):
                    st = Steps(dve, dstep)
                    dve.memset(raw[:, :, 0:3], 0.0).then_inc(pads, 1)
                    w = par("conv").rearrange("p (g j) -> p g j", j=4)
                    dve.wait_ge(pads, 1)
                    for g in range(9):
                        dve.wait_ge(raw_ready, 2 * g + 2)
                        if g >= 2:
                            dve.wait_ge(silu_ready, g - 1)
                        y = conv[:, g % 2, :]
                        st.done(dve.tensor_scalar(y, raw[:, g % 2, 0:S], w[:, g, 0:1], None, ALU.mult))
                        for j in range(1, 4):
                            i = dve.scalar_tensor_tensor(out=y, in0=raw[:, g % 2, j:j + S], scalar=w[:, g, j:j + 1], in1=y,
                                                         op0=ALU.mult, op1=ALU.add)
                            st.done(i) if j < 3 else i.then_inc(conv_ready, 1)
                    dve.wait_ge(gate_ready, NT)
                    a, b = ab[:, :, 0:H_GDN], ab[:, :, H_GDN:12]
                    dt = par("dt_bias").unsqueeze(1).to_broadcast([P, NT, H_GDN])
                    st.done(dve.tensor_tensor(t1[:, :, 0:H_GDN], a, dt, ALU.add))
                    dve.tensor_copy(t1[:, :, H_GDN:12], b).then_inc(sc_dve, 1)
                    dve.wait_ge(sc_dve, 1)
                    st.done(dve.tensor_scalar(t3[:, :, 0:H_GDN], t1[:, :, 0:H_GDN], 0.0, None, ALU.max))
                    st.done(dve.tensor_scalar(t3[:, :, H_GDN:12], t1[:, :, H_GDN:12], 0.0, None, ALU.min))
                    dve.wait_ge(sc_act, 1)
                    st.done(dve.tensor_tensor(t3[:, :, 0:H_GDN], t3[:, :, 0:H_GDN], t2[:, :, 0:H_GDN], ALU.add))
                    st.done(dve.tensor_tensor(t3[:, :, H_GDN:12], t3[:, :, H_GDN:12], t2[:, :, H_GDN:12], ALU.subtract))
                    st.done(dve.tensor_scalar(ealog[:, :], ealog[:, :], -1.0, None, ALU.mult))
                    dve.tensor_tensor(g_[:, :, :], t3[:, :, 0:H_GDN],
                                      ealog[:, :].unsqueeze(1).to_broadcast([P, NT, H_GDN]), ALU.mult).then_inc(sc_dve, 1)
                    lb = t3[:, :, H_GDN:12]
                    st.done(dve.tensor_scalar(row_q[:, :, :], lnr[:, :, 0:6], -0.5, -0.5 * math.log(HD), ALU.mult, ALU.add))
                    st.done(dve.tensor_scalar(t2[:, :, 0:6], lnr[:, :, 6:12], -0.5, None, ALU.mult))
                    lnrk = t2[:, :, 0:6]
                    st.done(dve.tensor_tensor(row_a[:, :, :], lb, lnrk, ALU.add))
                    dve.wait_ge(sc_pe, 1)
                    d, dl = (PS[:, 7, 48 * j:48 * j + 48].rearrange("p (n h) -> p n h", n=NT) for j in range(2))
                    st.done(dve.tensor_copy(beta[:, :, :], lb))
                    st.done(dve.tensor_tensor(bias_j[:, :, :], lnrk, d, ALU.subtract))
                    st.done(dve.tensor_tensor(row_a[:, :, :], row_a[:, :, :], d, ALU.add))
                    st.done(dve.tensor_tensor(s_kd[:, :, :], lnrk, dl, ALU.add))
                    dve.tensor_tensor(row_q[:, :, :], row_q[:, :, :], d, ALU.add).then_inc(sc_dve, 1)
                    go = par("gdn_o").unsqueeze(1).to_broadcast([P, H_GDN, HD])
                    for n in range(NT):
                        sg = sgate[:, n, :].rearrange("p (h d) -> p h d", d=HD)
                        st.done(dve.tensor_tensor(sg, sg, go, ALU.mult))

            with ExitStack() as c, nc.Block() as block:
                new_phase(c)
                LV = 7
                TL = 2 * (LV - 1)
                kn, vn = sb("kn", [P, GDN], c=c), sb("vn", [P, GDN], c=c)
                rwv = sb("rwv", [P, 2, H_GDN, 2, HD], c=c)
                kd = sb("kd", [P, 2, GDN], c=c)
                free = wring[CH_GAB % 3][:, :, :].rearrange("p k n -> p (k n)")
                pads = free[:, 0:12 * P].rearrange("p (s g t) -> p s g t", s=2, g=6)
                diag = free[:, 12 * P:18 * P].rearrange("p (j a t) -> p j a t", j=2, a=3)
                wn = free[:, 18 * P:21 * P].rearrange("p (a s d) -> p a s d", a=3, s=2)
                wT = free[:, 21 * P:24 * P].rearrange("p (a t) -> p a t", a=3)
                vnew = free[:, 24 * P:27 * P].rearrange("p (a s d) -> p a s d", a=3, s=2)
                St = free[:, 27 * P:30 * P].rearrange("p (a s d) -> p a s d", a=3, s=2)
                AT, X, M, IT, Y = (sb(n_, [P, 2, 2, 3, P], c=c) for n_ in ("AT", "X", "M", "IT", "Y"))
                T1 = sb("T1", [P, 2, 3, P], c=c)
                oss, orr = sb("oss", [P, H_GDN], c=c), sb("orr", [P, H_GDN], c=c)
                kv_turned, kv_ready, sc_ready, pads_ready, diag_ready = (sem(n_) for n_ in (
                    "kv_turned", "kv_ready", "sc_ready", "pads_ready", "diag_ready"))
                dbc, gam_ready, kk, AT_ready = sem("dbc"), sem("gam_ready"), sem("kk"), sem("AT_ready")
                M_ready, M0_turned, X0_ready, Y0_ready = sem("M_ready"), sem("M0_turned"), sem("X0_ready"), sem("Y0_ready")
                X_ready, Y_ready, T1_mm, T1_ready, D_mm, YT_mm = (sem(n_) for n_ in (
                    "X_ready", "Y_ready", "T1_mm", "T1_ready", "D_mm", "YT_mm"))
                wu_mm, wn_ready, w_turned, wT_ready, v_mm, v_ready, o_mm, o_ready, S_ready = (sem(n_) for n_ in (
                    "wu_mm", "wn_ready", "w_turned", "wT_ready", "v_mm", "v_ready", "o_mm", "go_ready", "S_ready"))
                os_act, oss_rdy, orr_rdy, on_ready = (sem(n_) for n_ in ("os_act", "oss_rdy", "orr_rdy", "gon_ready"))
                dstep, astep = sem("h_dve_step"), sem("h_act_step")
                B_WU, B_Q, B_WS, B_OI, B_UPD, B_YT = (2, 3), 4, 5, 2, 3, (6, 7)

                def slots(ap, s):
                    return ap.rearrange("p (a s) -> p s a", s=2)[:, s, :]

                def by_head(ap):
                    return ap.rearrange("p (a s) -> p a s", s=2).unsqueeze(3).to_broadcast([P, 3, 2, HD])

                def bank3(b, w=P):
                    return PS[:, b, 0:3 * w].rearrange("p (a t) -> p a t", a=3)

                def lv(n, l, s):
                    return TL * n + 2 * (l - 1) + s + 1

                def out_and_square(n):
                    return qkvT[:, 3:6, n * P:(n + 1) * P], qkvT[:, 6:9, n * P:(n + 1) * P]

                def last_level(n, l):
                    return (n, l - 1) if l > 1 else (n - 1, LV - 1)

                @block.tensor
                def _(pe):
                    def natural_kv(n):
                        for j in range(2):
                            if n >= 1:
                                pe.wait_ge(Y_ready, lv(n - 1, 2, j))
                            for a in range(3):
                                mm = pe.transpose(PS[:, B_YT[j], a * P:(a + 1) * P], qkvT[:, 3 + 3 * j + a, n * P:(n + 1) * P], ident)
                            mm.then_inc(kv_turned, 1)

                    def decays(n, s):
                        pe.wait_ge(diag_ready, 4 * n + 2 * s + 2)
                        for j, (b, mask) in enumerate(((5, mask_strict), (4, mask_incl))):
                            if s == 1:
                                pe.wait_ge(gam_ready, 4 * n + j + 1)
                            elif j == 1 and n >= 2:
                                pe.wait_ge(o_ready, n - 1)
                            o = bank3(b)
                            pe.matmul(o, ones, diag[:, j, :, :], start=True, stop=False)
                            pe.matmul(o, identb, mask.unsqueeze(1).to_broadcast([P, 3, P]), start=False, stop=True).then_inc(dbc, 1)
                        pe.wait_ge(pads_ready, 2 * n + s + 1)
                        for j, b in enumerate((B_OI, B_UPD)):
                            if s == 1:
                                pe.wait_ge(AT_ready, 4 * n + j + 1)
                            elif j == 1 and n >= 2:
                                pe.wait_ge(S_ready, n)
                            for a in range(3):
                                mm = pe.matmul(PS[:, b, a * P:(a + 1) * P], qkvT[:, 3 + a, n * P:(n + 1) * P],
                                               pads[:, s, 3 * (1 - j) + a, :], start=True, stop=True)
                            mm.then_inc(kk, 1)

                    def turn_M0(n):
                        for s in range(2):
                            pe.wait_ge(M_ready, 2 * LV * n + s + 1)
                            pe.wait_ge(AT_ready, 4 * n + 4)
                            for a in range(3):
                                mm = pe.transpose(PS[:, 2 + s, a * P:(a + 1) * P], M[:, (LV * n) % 2, s, a, :], ident)
                            mm.then_inc(M0_turned, 1)

                    def turn_X(n, l):
                        for s in range(2):
                            pe.wait_ge(X_ready, lv(n, l, s))
                            if (n, l) > (0, 1):
                                pe.wait_ge(Y_ready, lv(*last_level(n, l), s))
                            if l == 3 and n + 1 < NT:
                                pe.wait_ge(kv_ready, 2 * (n + 1) + s + 1)
                            for a in range(3):
                                mm = pe.transpose(PS[:, B_YT[s], a * P:(a + 1) * P], X[:, n % 2, s, a, :], ident)
                            mm.then_inc(YT_mm, 1)

                    def scan(n, part):
                        t, i = slice(n * P, (n + 1) * P), n % 2
                        if part == 0:
                            pe.wait_ge(sc_ready, 3 * n + 3)
                            for s in range(2):
                                pe.wait_ge(Y_ready, lv(n, LV - 1, s))
                                pe.wait_ge(X0_ready, 2 * min(n + 1, NT - 1) + s + 1)
                                for a in range(3):
                                    mm = pe.matmul(PS[:, B_WU[s], a * P:(a + 1) * P], Y[:, i, s, a, :],
                                                   rwv[:, i, 2 * a + s, :, :].rearrange("p j d -> p (j d)"), start=True, stop=True)
                                mm.then_inc(wu_mm, 1)
                        if part == 1:
                            pe.wait_ge(wn_ready, 2 * n + 2)
                            for a in range(3):
                                mm = pe.transpose(PS[:, B_Q, a * P:(a + 1) * P], wn[:, a, :, :].rearrange("p s d -> p (s d)"), ident)
                            mm.then_inc(w_turned, 1)
                        if part == 2:
                            pe.wait_ge(wT_ready, n + 1)
                            pe.wait_ge(S_ready, n + 1)
                            for a in range(3):
                                mm = pe.matmul(PS[:, B_WS, a * P:(a + 1) * P], wT[:, a, :], St[:, a, :, :].rearrange("p s d -> p (s d)"),
                                               start=True, stop=True)
                            mm.then_inc(v_mm, 1)
                            for a in range(3):
                                mm = pe.matmul(PS[:, B_Q, a * P:(a + 1) * P], qkvT[:, a, t], St[:, a, :, :].rearrange("p s d -> p (s d)"),
                                               start=True, stop=True)
                            mm.then_inc(o_mm, 1)
                        if part == 3:
                            pe.wait_ge(v_ready, 2 * n + 2)
                            for h in range(H_GDN):
                                mm = pe.matmul(PS[:, B_OI, h * HD:(h + 1) * HD], IT[:, i, h % 2, h // 2, :], vnew[:, h // 2, h % 2, :],
                                               start=True, stop=True)
                            mm.then_inc(o_mm, 1)
                            for h in range(H_GDN):
                                a, s = h // 2, h % 2
                                mm = pe.matmul(PS[64 * s:64 * s + 64, B_UPD, a * HD:(a + 1) * HD], kd[:, i, h * HD:(h + 1) * HD],
                                               vnew[:, a, s, :], start=True, stop=True)
                            mm.then_inc(o_mm, 1)

                    def between(n, l, second):
                        if n >= 1:
                            for part, at in enumerate(((1, 1), (2, 0), (2, 1), (3, 1))):
                                if at == (l, second):
                                    scan(n - 1, part)
                        if n + 1 < NT:
                            if (l, second) == (3, 0):
                                natural_kv(n + 1)
                            if (l, second) == (4, 0):
                                decays(n + 1, 0)
                            if (l, second) == (5, 0):
                                decays(n + 1, 1)
                            if (l, second) == (6, 0):
                                turn_M0(n + 1)

                    natural_kv(0)
                    decays(0, 0)
                    decays(0, 1)
                    turn_M0(0)
                    for n in range(NT):
                        for l in range(1, LV):
                            for s in range(2):
                                pe.wait_ge(M_ready, 2 * LV * n + 2 * l + s + 1)
                                pe.wait_ge(X0_ready, 2 * n + s + 1)
                                if (n, l) > (0, 1):
                                    pe.wait_ge(X_ready, lv(*last_level(n, l), s))
                                for a in range(3):
                                    mm = pe.matmul(PS[:, s, a * P:(a + 1) * P], M[:, (LV * n + l) % 2, s, a, :], X[:, n % 2, s, a, :],
                                                   start=True, stop=True)
                                mm.then_inc(T1_mm, 1)
                            if (n, l) > (0, 1):
                                turn_X(*last_level(n, l))
                            between(n, l, 0)
                            for s in range(2):
                                pe.wait_ge(T1_ready, lv(n, l, s))
                                if l == 1:
                                    pe.wait_ge(Y0_ready, 2 * n + s + 1)
                                else:
                                    pe.wait_ge(Y_ready, lv(n, l - 1, s))
                                for a in range(3):
                                    mm = pe.matmul(PS[:, s, a * P:(a + 1) * P], Y[:, n % 2, s, a, :], T1[:, s, a, :], start=True, stop=True)
                                mm.then_inc(D_mm, 1)
                            between(n, l, 1)
                    turn_X(NT - 1, LV - 1)
                    for part in range(4):
                        scan(NT - 1, part)

                @block.scalar
                def _(act):
                    st = Steps(act, astep)

                    def natural_kv(n):
                        for j, dst in enumerate((kn, vn)):
                            act.wait_ge(kv_turned, 2 * n + j + 1)
                            if n >= 1:
                                act.wait_ge(sc_ready, 3 * n)
                            act.activation(dst[:, :], PS[:, B_YT[j], 0:GDN], ACT.Copy).then_inc(kv_ready, 1)

                    def decays(n, s):
                        for j in range(2):
                            act.wait_ge(dbc, 4 * n + 2 * s + j + 1)
                            if n >= 2:
                                act.wait_ge(M_ready, 2 * LV * (n - 1)) if j == 0 else act.wait_ge(o_mm, 3 * (n - 1))
                            for a in range(3):
                                h = 2 * a + s
                                i = act.activation((IT if j else AT)[:, n % 2, s, a, :], PS[:, 5 - j, a * P:(a + 1) * P], ACT.Exp,
                                                   bias=bias_j[:, n, h:h + 1])
                            i.then_inc(gam_ready, 1)

                    def copy_Y(n, l):
                        for s in range(2):
                            act.wait_ge(YT_mm, lv(n, l, s))
                            act.wait_ge(D_mm, lv(n, l, s))
                            act.activation(Y[:, n % 2, s, :, :], bank3(B_YT[s]), ACT.Copy).then_inc(Y_ready, 1)

                    def scan(n, part):
                        if part == 0:
                            if n >= 1:
                                act.wait_ge(w_turned, n)
                            for s in range(2):
                                act.wait_ge(wu_mm, 2 * n + s + 1)
                                act.activation(wn[:, :, s, :], bank3(B_WU[s])[:, :, 0:HD], ACT.Copy, scale=-1.0).then_inc(wn_ready, 1)
                        if part == 1:
                            act.wait_ge(w_turned, n + 1)
                            if n >= 1:
                                act.wait_ge(v_mm, n)
                            act.activation(wT[:, :, :], bank3(B_Q), ACT.Copy).then_inc(wT_ready, 1)
                        if part == 2:
                            act.wait_ge(o_ready, n + 1)
                            ob, osq = out_and_square(n)
                            act.activation(osq, ob, ACT.Square).then_inc(os_act, 1)
                        if part == 3:
                            act.wait_ge(oss_rdy, n + 1)
                            st.done(act.activation(orr[:, :], oss[:, :], ACT.Ln, bias=eps[:, :], scale=1.0 / HD))
                            act.activation(orr[:, :], orr[:, :], ACT.Exp, scale=-0.5).then_inc(orr_rdy, 1)

                    natural_kv(0)
                    decays(0, 0)
                    decays(0, 1)
                    for n in range(NT):
                        for l in range(1, LV):
                            for s in range(2):
                                act.wait_ge(T1_mm, lv(n, l, s))
                                if (n, l) > (0, 1):
                                    act.wait_ge(D_mm, lv(*last_level(n, l), s))
                                act.activation(T1[:, s, :, :], bank3(s), ACT.Copy).then_inc(T1_ready, 1)
                            if (n, l) > (0, 1):
                                copy_Y(*last_level(n, l))
                            if l == 3 and n + 1 < NT:
                                natural_kv(n + 1)
                            if l in (4, 5) and n + 1 < NT:
                                decays(n + 1, l - 4)
                            if n >= 1 and l in (1, 2, 4, 5):
                                scan(n - 1, (1, 2, 4, 5).index(l))
                    copy_Y(NT - 1, LV - 1)
                    for part in range(4):
                        scan(NT - 1, part)

                @block.gpsimd
                def _(pool):
                    def diagonals(n, s):
                        if n >= 1 or s == 1:
                            pool.wait_ge(dbc, 4 * n + 2 * s)
                        for j, row in enumerate((row_a, row_q)):
                            pool.tensor_tensor(diag[:, j, :, :], ident.unsqueeze(1).to_broadcast([P, 3, P]),
                                               slots(row[:, n, :], s).unsqueeze(2).to_broadcast([P, 3, P]), ALU.mult).then_inc(diag_ready, 1)

                    def right_sides(n):
                        pool.wait_ge(kv_ready, 2 * n + 2)
                        if n >= 2:
                            pool.wait_ge(o_mm, 3 * (n - 1))
                        for dst, src, by in ((rwv[:, n % 2, :, 0, :], kn, s_w), (rwv[:, n % 2, :, 1, :], vn, beta),
                                             (kd[:, n % 2, :].rearrange("p (h d) -> p h d", d=HD), kn, s_kd)):
                            pool.tensor_tensor(dst, src[:, :].rearrange("p (h d) -> p h d", d=HD),
                                               by[:, n, :].unsqueeze(2).to_broadcast([P, H_GDN, HD]), ALU.mult).then_inc(sc_ready, 1)

                    def cut(n, l):
                        for s in range(2):
                            pool.wait_ge(AT_ready, 4 * n + 2 * s + 1)
                            if l >= 3 or (l < 2 and n >= 1):
                                pool.wait_ge(T1_mm, lv(n, l - 2, s) if l >= 3 else lv(n - 1, LV - 2 + l, s))
                            if l == 2:
                                pool.wait_ge(M0_turned, 2 * n + s + 1)
                                pool.wait_ge(Y0_ready, 2 * n + s + 1)
                            lm = kc[:, K_LM + l, :].unsqueeze(1).to_broadcast([P, 3, P])
                            pool.tensor_tensor(M[:, (LV * n + l) % 2, s, :, :], AT[:, n % 2, s, :, :], lm, ALU.mult).then_inc(M_ready, 1)

                    diagonals(0, 0)
                    diagonals(0, 1)
                    right_sides(0)
                    cut(0, 0)
                    cut(0, 1)
                    for n in range(NT):
                        for l in range(1, LV):
                            if l < LV - 1:
                                cut(n, l + 1)
                            if n + 1 == NT:
                                continue
                            if l in (3, 4):
                                diagonals(n + 1, l - 3)
                            if l == 4:
                                right_sides(n + 1)
                            if l == 5:
                                cut(n + 1, 0)
                            if l == 6:
                                cut(n + 1, 1)

                @block.vector
                def _(dve):
                    st = Steps(dve, dstep)
                    st.done(dve.memset(pads[:, :, :, :], 0.0))
                    dve.memset(St[:, :, :, :], 0.0).then_inc(S_ready, 1)
                    idb3 = ident.unsqueeze(1).to_broadcast([P, 3, P])

                    def padded(n):
                        if n >= 1:
                            dve.wait_ge(kk, 4 * n)
                        for s in range(2):
                            hs = slice(64 * s, 64 * s + 64)
                            dve.tensor_copy(pads[hs, s, :, :], qkvT[hs, 0:6, n * P:(n + 1) * P]).then_inc(pads_ready, 1)

                    def decays(n, s):
                        for j in range(2):
                            dve.wait_ge(gam_ready, 4 * n + 2 * s + j + 1)
                            dve.wait_ge(kk, 4 * n + 2 * s + j + 1)
                            it = (IT if j else AT)[:, n % 2, s, :, :]
                            dve.tensor_tensor(it, bank3(2 + j), it, ALU.mult).then_inc(AT_ready, 1)

                    def first_X(n):
                        for s in range(2):
                            dve.wait_ge(M0_turned, 2 * n + s + 1)
                            if n >= 2:
                                dve.wait_ge(YT_mm, lv(n - 2, LV - 1, s))
                            dve.tensor_tensor(X[:, n % 2, s, :, :], idb3, bank3(2 + s), ALU.subtract).then_inc(X0_ready, 1)

                    def first_Y(n):
                        for s in range(2):
                            if n >= 2:
                                dve.wait_ge(wu_mm, 2 * (n - 2) + s + 1)
                            dve.wait_ge(M_ready, 2 * LV * n + s + 1)
                            dve.tensor_tensor(Y[:, n % 2, s, :, :], idb3, M[:, (LV * n) % 2, s, :, :], ALU.subtract).then_inc(Y0_ready, 1)

                    def scan(n, part):
                        if part == 0:
                            dve.wait_ge(v_mm, n + 1)
                            dve.wait_ge(wn_ready, 2 * n + 2)
                            if n >= 1:
                                dve.wait_ge(o_mm, 3 * n)
                            ws = PS[:, B_WS, 0:GDN].rearrange("p (a s d) -> p s a d", s=2, d=HD)
                            for s in range(2):
                                st.done(dve.tensor_copy(vnew[:, :, s, :], bank3(B_WU[s])[:, :, HD:P]))
                                dve.tensor_tensor(vnew[:, :, s, :], vnew[:, :, s, :], ws[:, s, :, :], ALU.add).then_inc(v_ready, 1)
                        if part == 1:
                            dve.wait_ge(o_mm, 3 * n + 2)
                            if n >= 1:
                                dve.wait_ge(on_ready, n)
                            ob = out_and_square(n)[0]
                            o = ob.rearrange("p a (s d) -> p a s d", d=HD)
                            st.done(dve.tensor_tensor(o, PS[:, B_Q, 0:GDN].rearrange("p (a s d) -> p a s d", s=2, d=HD),
                                                      by_head(s_q[:, n, :]), ALU.mult))
                            dve.tensor_tensor(ob, ob, bank3(B_OI), ALU.add).then_inc(o_ready, 1)
                            dve.wait_ge(o_mm, 3 * n + 3)
                            dve.wait_ge(S_ready, n + 1)
                            St3 = St[:, :, :, :].rearrange("p a s d -> p a (s d)")
                            st.done(dve.tensor_tensor(St3, St3, e_last[:, n, :].unsqueeze(2).to_broadcast([P, 3, P]), ALU.mult))
                            for s in range(2):
                                hs = slice(64 * s, 64 * s + 64)
                                upd = PS[hs, B_UPD, 0:3 * HD].rearrange("p (a d) -> p a d", a=3)
                                i = dve.tensor_tensor(St[hs, :, s, :], St[hs, :, s, :], upd, ALU.add)
                                st.done(i) if s == 0 else i.then_inc(S_ready, 1)
                        if part == 2:
                            dve.wait_ge(os_act, n + 1)
                            dve.tensor_reduce(oss[:, :].rearrange("p (a s) -> p a s", s=2),
                                              out_and_square(n)[1].rearrange("p a (s d) -> p a s d", d=HD), AX.X, ALU.add).then_inc(oss_rdy, 1)
                        if part == 3:
                            dve.wait_ge(orr_rdy, n + 1)
                            ob = out_and_square(n)[0]
                            o = ob.rearrange("p a (s d) -> p a s d", d=HD)
                            st.done(dve.tensor_tensor(o, o, by_head(orr[:, :]), ALU.mult))
                            sg = sgate[:, n, :].rearrange("p (a t) -> p a t", a=3)
                            dve.tensor_tensor(sg, ob, sg, ALU.mult).then_inc(on_ready, 1)

                    padded(0)
                    decays(0, 0)
                    decays(0, 1)
                    first_X(0)
                    first_Y(0)
                    for n in range(NT):
                        for l in range(1, LV):
                            if l == LV - 1 and n + 1 < NT:
                                first_X(n + 1)
                            for s in range(2):
                                dve.wait_ge(D_mm, lv(n, l, s))
                                xl = X[:, n % 2, s, :, :].rearrange("p a (b u w) -> p (a b) u w", u=2, w=1 << l)[:, :, 0, :]
                                d = PS[:, s, 0:3 * P].rearrange("p (c u w) -> p c u w", u=2, w=1 << l)[:, :, 0, :]
                                dve.tensor_tensor(xl, xl, d, ALU.subtract).then_inc(X_ready, 1)
                            if n + 1 < NT:
                                if l == 1:
                                    padded(n + 1)
                                if l in (4, 5):
                                    decays(n + 1, l - 4)
                                if l == LV - 1:
                                    first_Y(n + 1)
                            if n >= 1 and 2 <= l <= 5:
                                scan(n - 1, l - 2)
                    for part in range(4):
                        scan(NT - 1, part)

        with ExitStack() as lc:
            vl = sb("vl", [P, NT, GV], c=lc)
            slr = sb("slr", [P, NT, GV], c=lc)
            qlT, klT, bT = (sb(n_, [P, S], c=lc) for n_ in ("qlT", "klT", "bT"))
            with ExitStack() as c, nc.Block() as block:
                new_phase(c)
                wa2 = sb("wa2", [RANK, GK], c=c)
                la1T = sb("la1T", [RANK, S], c=c)
                lx, le, lm_ = (sb(n_, [P, NT, GK], c=c) for n_ in ("lx", "le", "lmin"))
                wa2_loaded, lproj, l_ready, nproj, n_ready = (sem(n_) for n_ in ("wa2_loaded", "lproj", "l_ready", "nproj", "n_ready"))
                la_mm, lx_ready, ls_act, ls_ready, b_mm, b_ready = (sem(n_) for n_ in ("la_mm", "lx_ready", "ls_act", "ls_ready", "b_mm", "b_ready"))
                dstep, astep = sem("l_dve_step"), sem("l_act_step")

                @block.sync
                def _(sp):
                    sp.dma_start(wa2[:, :], w_a2).then_inc(wa2_loaded, 16)
                    load_chunk(sp, 9)
                    load_chunk(sp, 10)

                @block.tensor
                def _(pe):
                    chunk_ready(pe, CH_L)
                    for j, (a, w) in enumerate(((2 * GK, RANK), (0, GK), (GK, GK))):
                        for b in range(2):
                            if j == 2:
                                pe.wait_ge(l_ready, b + 1)
                            for k in range(KD):
                                mm = pe.matmul(PS[0:w, 2 * (j % 2) + b, :], wring[CH_L % 3][:, k, a:a + w],
                                               hT[:, k, 512 * b:512 * b + 512], start=(k == 0), stop=(k == KD - 1))
                            mm.then_inc(lproj, 1)
                    pe.wait_ge(lproj, 6)
                    pe.nop().then_inc(w_used, 1)
                    pe.wait_ge(wa2_loaded, 16)
                    pe.wait_ge(l_ready, 2)
                    for n in range(NT):
                        mm = pe.matmul(PS[:, 6 + n // 4, (n % 4) * P:(n % 4 + 1) * P], la1T[:, n * P:(n + 1) * P], wa2[:, :],
                                       start=True, stop=True)
                    mm.then_inc(la_mm, 1)
                    chunk_ready(pe, CH_LVR)
                    for n in range(NT):
                        if n >= 2:
                            pe.wait_ge(n_ready, n - 1)
                        project_tile(pe, CH_LVR, n, 4 + n % 2, 512).then_inc(nproj, 1)
                    pe.wait_ge(nproj, NT)
                    pe.nop().then_inc(w_used, 1)
                    pe.wait_ge(ls_ready, 1)
                    for n in range(NT):
                        mm = pe.matmul(PS[:, 6 + n // 4, (n % 4) * P:(n % 4 + 1) * P], lx[:, n, :], U, start=True, stop=True)
                    mm.then_inc(b_mm, 1)

                @block.scalar
                def _(act):
                    st = Steps(act, astep)
                    act.preload_act_table_set("silu_and_others")
                    for j, dst in enumerate((la1T, qlT, klT)):
                        for b in range(2):
                            act.wait_ge(lproj, 2 * j + b + 1)
                            w = RANK if j == 0 else P
                            act.activation(dst[:, 512 * b:512 * b + 512], PS[0:w, 2 * (j % 2) + b, :], ACT.Copy).then_inc(l_ready, 1)
                    for n in range(NT):
                        act.wait_ge(nproj, n + 1)
                        st.done(act.activation(vl[:, n, :], PS[:, 4 + n % 2, 0:GV], ACT.Copy))
                        act.activation(slr[:, n, :], PS[:, 4 + n % 2, GV:512], ACT.Silu).then_inc(n_ready, 1)
                    act.wait_ge(lx_ready, 1)
                    act.preload_act_table_set("natural_log_exp_and_others")
                    st.done(act.activation(le[:, :, :], lx[:, :, :], ACT.Abs))
                    st.done(act.activation(le[:, :, :], le[:, :, :], ACT.Exp, scale=-1.0))
                    act.activation(le[:, :, :], le[:, :, :], ACT.Ln, bias=1.0).then_inc(ls_act, 1)
                    act.wait_ge(b_mm, 1)
                    for b in range(2):
                        act.activation(bT[:, 512 * b:512 * b + 512], PS[:, 6 + b, :], ACT.Copy, scale=1.0 / 16).then_inc(b_ready, 1)

                @block.vector
                def _(dve):
                    st = Steps(dve, dstep)
                    dve.wait_ge(la_mm, 1)
                    ba = par("b_a").unsqueeze(1).to_broadcast([P, 4, GK])
                    for b in range(2):
                        i = dve.tensor_tensor(lx[:, 4 * b:4 * b + 4, :], PS[:, 6 + b, :].rearrange("p (n c) -> p n c", n=4), ba, ALU.add)
                        st.done(i) if b == 0 else i.then_inc(lx_ready, 1)
                    dve.wait_ge(lx_ready, 1)
                    st.done(dve.tensor_scalar(lm_[:, :, :], lx[:, :, :], 0.0, None, ALU.min))
                    dve.wait_ge(ls_act, 1)
                    dve.tensor_tensor(lx[:, :, :], lm_[:, :, :], le[:, :, :], ALU.subtract).then_inc(ls_ready, 1)
                    go = par("gla_o").unsqueeze(1).to_broadcast([P, NT * H_GLA, HD])
                    sg = slr[:, :, :].rearrange("p n (h d) -> p (n h) d", d=HD)
                    dve.wait_ge(n_ready, NT)
                    st.done(dve.tensor_tensor(sg, sg, go, ALU.mult))

            with ExitStack() as c, nc.Block() as block:
                new_phase(c)
                ql, kl = sb("ql", [P, S], c=c), sb("kl", [P, S], c=c)
                el_ = sb("el_", [P, S], c=c)
                sc = sb("sc", [P, NT, H_GLA, P], c=c)
                qe, kdT = sb("qe", [P, S], c=c), sb("kdT", [P, S], c=c)
                kdn = sb("kdn", [P, GK], c=c)
                e_end = sb("e_end", [P, NT], c=c)
                Sg = sb("Sg", [P, GV], c=c)
                kvm = sb("kvm", [P, GV], c=c)
                osq = sb("osq", [P, NT, GV], c=c)
                oss, orr = sb("loss", [P, NT * H_GLA], c=c), sb("lorr", [P, NT * H_GLA], c=c)
                diff_ready, e_ready, qk_ready, sc_mm, sc_done = (sem(n_) for n_ in ("diff_ready", "e_ready", "qk_ready", "sc_mm", "sc_done"))
                kd_turned, kdn_ready, o_mm, kv_mm, o_ready, S_ready = (sem(n_) for n_ in (
                    "lkd_turned", "kdn_ready", "lo_mm", "kv_mm", "lo_ready", "lS_ready"))
                sq_done, ss_done, rr_done = sem("lsq_done"), sem("lss_done"), sem("lrr_done")
                dstep = sem("m_dve_step")
                astep = sem("m_act_step")
                LV = 7

                def halves(t, l):
                    v = t[:, :].rearrange("p (b u w) -> p b u w", u=2, w=1 << l)
                    return v[:, :, 0, :], v[:, :, 1, :]

                @block.tensor
                def _(pe):
                    for l in range(LV + 1):
                        for n in range(NT):
                            pe.wait_ge(qk_ready, min(l + 1, LV + 1))
                            u = l * NT + n
                            if u >= 2:
                                pe.wait_ge(sc_done, u - 1)
                            t = slice(n * P, (n + 1) * P)
                            q_, k_ = (ql, kl) if l < LV else (qlT, klT)
                            for h in range(H_GLA):
                                hs = slice(DK * h, DK * h + DK)
                                mm = pe.matmul(PS[:, 4 * (u % 2) + h, 0:P], k_[hs, t], q_[hs, t], start=True, stop=True,
                                               tile_position=(DK * h, 0))
                            mm.then_inc(sc_mm, 1)
                    for n in range(NT):
                        t = slice(n * P, (n + 1) * P)
                        pe.wait_ge(qk_ready, LV + 2)
                        if n == 0:
                            pe.wait_ge(sc_done, (LV + 1) * NT)
                        pe.wait_ge(o_ready, n) if n else None
                        if n:
                            pe.wait_ge(kdn_ready, n)
                            pe.wait_ge(S_ready, n + 1)
                        pe.transpose(PS[:, 0, 0:P], kdT[:, t], ident).then_inc(kd_turned, 1)
                        pe.wait_ge(S_ready, n + 1)
                        pe.matmul(PS[:, 1 + n % 2, 0:GV], qe[:, t], Sg[:, :], start=True, stop=False)
                        for h in range(H_GLA):
                            mm = pe.matmul(PS[:, 1 + n % 2, h * HD:(h + 1) * HD], sc[:, n, h, :], vl[:, n, h * HD:(h + 1) * HD],
                                           start=False, stop=(h == H_GLA - 1))
                        mm.then_inc(o_mm, 1)
                        pe.wait_ge(kdn_ready, n + 1)
                        pe.matmul(PS[:, 3, 0:GV], kdn[:, :], vl[:, n, :], start=True, stop=True).then_inc(kv_mm, 1)

                @block.scalar
                def _(act):
                    st = Steps(act, astep)
                    for l in range(LV + 2):
                        act.wait_ge(diff_ready, l + 1)
                        act.activation(el_[:, :], el_[:, :], ACT.Exp).then_inc(e_ready, 1)
                    for n in range(NT):
                        act.wait_ge(kd_turned, n + 1)
                        if n:
                            act.wait_ge(kv_mm, n)
                        act.activation(kdn[:, :], PS[:, 0, 0:P], ACT.Copy).then_inc(kdn_ready, 1)
                        act.wait_ge(o_mm, n + 1)
                        act.activation(mix[:, n, FOX + GDN:D], PS[:, 1 + n % 2, 0:GV], ACT.Copy, scale=float(DK) ** -0.5)\
                           .then_inc(o_ready, 1)
                    act.wait_ge(o_ready, NT)
                    act.activation(osq[:, :, :], mix[:, :, FOX + GDN:D], ACT.Square).then_inc(sq_done, 1)
                    act.wait_ge(ss_done, 1)
                    st.done(act.activation(orr[:, :], oss[:, :], ACT.Ln, bias=eps[:, :], scale=1.0 / HD))
                    act.activation(orr[:, :], orr[:, :], ACT.Exp, scale=-0.5).then_inc(rr_done, 1)

                @block.vector
                def _(dve):
                    st = Steps(dve, dstep)
                    for t_ in (ql, kl, sc):
                        st.done(dve.memset(t_[tuple(slice(None) for _ in t_.shape)], 0.0))
                    dve.memset(Sg[:, :], 0.0).then_inc(S_ready, 1)

                    def scores(u):
                        l, n = u // NT, u % NT
                        dve.wait_ge(sc_mm, u + 1)
                        lm = (kc[:, K_LM + l, :] if l < LV else ident).bitcast(U32).unsqueeze(1).to_broadcast([P, H_GLA, P])
                        src = PS[:, 4 * (u % 2):4 * (u % 2) + 4, 0:P]
                        dve.copy_predicated(sc[:, n, :, :], lm, src).then_inc(sc_done, 1)

                    for l in range(LV):
                        w = 1 << l
                        blo, bhi = halves(bT, l)
                        elo, ehi = halves(el_, l)
                        ref = bhi[:, :, 0:1].to_broadcast([P, S // (2 * w), w])
                        if l:
                            dve.wait_ge(qk_ready, l)
                        st.done(dve.tensor_tensor(elo, ref, blo, ALU.subtract))
                        dve.tensor_tensor(ehi, bhi, ref, ALU.subtract).then_inc(diff_ready, 1)
                        if l:
                            for n in range(NT):
                                scores((l - 1) * NT + n)
                        dve.wait_ge(e_ready, l + 1)
                        dve.wait_ge(sc_mm, l * NT) if l else None
                        st.done(dve.tensor_tensor(halves(kl, l)[0], halves(klT, l)[0], elo, ALU.mult))
                        dve.tensor_tensor(halves(ql, l)[1], halves(qlT, l)[1], ehi, ALU.mult).then_inc(qk_ready, 1)
                    dve.wait_ge(qk_ready, LV)
                    dve.tensor_copy(el_[:, :], bT[:, :]).then_inc(diff_ready, 1)
                    for n in range(NT):
                        scores((LV - 1) * NT + n)
                    dve.wait_ge(e_ready, LV + 1)
                    v = el_[:, :].rearrange("p (n t) -> p n t", n=NT)
                    st.done(dve.tensor_copy(e_end[:, :], v[:, :, P - 1]))
                    dve.tensor_tensor(qe[:, :], qlT[:, :], el_[:, :], ALU.mult).then_inc(qk_ready, 1)
                    dve.wait_ge(qk_ready, LV + 1)
                    bv = bT[:, :].rearrange("p (n t) -> p n t", n=NT)
                    dve.tensor_tensor(v, bv[:, :, P - 1:P].to_broadcast([P, NT, P]), bv, ALU.subtract).then_inc(diff_ready, 1)
                    for n in range(NT):
                        scores(LV * NT + n)
                    dve.wait_ge(e_ready, LV + 2)
                    dve.tensor_tensor(kdT[:, :], klT[:, :], el_[:, :], ALU.mult).then_inc(qk_ready, 1)
                    for n in range(NT):
                        dve.wait_ge(kv_mm, n + 1)
                        st.done(dve.tensor_tensor(kvm[:, :], PS[:, 3, 0:GV], kc[:, K_BD:K_BD + 2, :].rearrange("p a b -> p (a b)"), ALU.mult))
                        dve.scalar_tensor_tensor(out=Sg[:, :], in0=Sg[:, :], scalar=e_end[:, n:n + 1], in1=kvm[:, :],
                                                 op0=ALU.mult, op1=ALU.add).then_inc(S_ready, 1)
                    dve.wait_ge(sq_done, 1)
                    dve.tensor_reduce(oss[:, :], osq[:, :, :].rearrange("p n (h d) -> p (n h) d", d=HD), AX.X, ALU.add).then_inc(ss_done, 1)
                    dve.wait_ge(rr_done, 1)
                    o = mix[:, :, FOX + GDN:D]
                    for n in range(NT):
                        o3 = o[:, n, :].rearrange("p (h d) -> p h d", d=HD)
                        st.done(dve.tensor_tensor(o3, o3, orr[:, H_GLA * n:H_GLA * n + H_GLA].unsqueeze(2).to_broadcast([P, H_GLA, HD]), ALU.mult))
                    st.done(dve.tensor_tensor(o, o, slr[:, :, :], ALU.mult))

        rl = sb("rl", [P, NT, NG + NE])
        with ExitStack() as c, nc.Block() as block:
            new_phase(c)
            xr = sb("xr", [P, 2, D], c=c)
            mT = sb("mT", [P, 2, KD, P], c=c)
            h2 = sb("h2", [P, 2, D], c=c)
            wr = sb("wr", [P, KD, NG + NE], c=c)
            junk = sb("junk2", [P, D], c=c)
            zy = sb("zy", [P, D], c=c)
            zy_ready, zy_stored = sem("zy_ready"), sem("zy_stored")
            ss, rr = sb("oss2", [P, NT], c=c), sb("orr2", [P, NT], c=c)
            xr_loaded, wr_loaded = [sem("xr_loaded0"), sem("xr_loaded1")], sem("wr_loaded")
            m_turned, mT_ready, y_mm, x1_ready = sem("m_turned"), sem("mT_ready"), sem("y_mm"), sem("x1_ready")
            r2_ready, h2_ready, h2_turned, h2T_ready, rl_mm, rl_ready = (sem(n_) for n_ in (
                "r2_ready", "h2_ready", "h2_turned", "h2T_ready", "rl_mm", "rl_ready"))
            h2_stored = [sem("h2_stored0"), sem("h2_stored1")]
            astep = sem("o_act_step")

            @block.sync
            def _(sp):
                sp.dma_start(wr[:, :, :], w_router.rearrange("(k p) n -> p k n", p=P)).then_inc(wr_loaded, 16)
                for n in range(NT):
                    if n >= 2:
                        sp.wait_ge(x1_ready, 2 * (n - 1))
                    sp.dma_start(xr[:, n % 2, :], x[n * P:(n + 1) * P, :]).then_inc(xr_loaded[n % 2], 16)
                    if n >= 1:
                        sp.wait_ge(h2_ready, n)
                        sp.dma_start(h2_dram[(n - 1) * P:n * P, :], h2[:, (n - 1) % 2, :]).then_inc(h2_stored[(n - 1) % 2], 16)
                sp.wait_ge(h2_ready, NT)
                sp.dma_start(h2_dram[(NT - 1) * P:S, :], h2[:, (NT - 1) % 2, :]).then_inc(h2_stored[(NT - 1) % 2], 16)
                for i in range(2):
                    sp.wait_ge(h2_stored[i], 16 * NT // 2)
                sp.wait_ge(zy_stored, 16)

            @block.gpsimd
            def _(pool):
                pool.memset(zy[:, :], 0.0).then_inc(zy_ready, 1)
                pool.wait_ge(zy_ready, 1)
                pool.dma_start(y_dram[NE * P:, :].rearrange("(b p) d -> p b d", p=P),
                               zy[:, :].unsqueeze(1).to_broadcast([P, MAXB - NE, D])).then_inc(zy_stored, 16)

            @block.tensor
            def _(pe):
                def project(n):
                    for b in range(2):
                        if n >= 1:
                            pe.wait_ge(mT_ready, 2 * (n - 1) + b + 1)
                        for k in range(4):
                            mm = pe.transpose(PS[:, b, k * P:(k + 1) * P], mix[:, n, (4 * b + k) * P:(4 * b + k + 1) * P], ident)
                        mm.then_inc(m_turned, 1)
                    for b in range(2):
                        if n == 0:
                            chunk_ready(pe, CH_O0 + b)
                        else:
                            pe.wait_ge(x1_ready, 2 * (n - 1) + b + 1)
                        for k in range(KD):
                            pe.wait_ge(mT_ready, 2 * n + k // 4 + 1) if b == 0 and k % 4 == 0 else None
                            mm = pe.matmul(PS[:, 2 + b, :], mT[:, n % 2, k, :], wring[(CH_O0 + b) % 3][:, k, :],
                                           start=(k == 0), stop=(k == KD - 1))
                        mm.then_inc(y_mm, 1)

                def route(n):
                    pe.wait_ge(h2_ready, n + 1)
                    for b in range(2):
                        if n >= 1:
                            pe.wait_ge(h2T_ready, 2 * (n - 1) + b + 1)
                        for k in range(4):
                            mm = pe.transpose(PS[:, 4 + b, k * P:(k + 1) * P], h2[:, n % 2, (4 * b + k) * P:(4 * b + k + 1) * P], ident)
                        mm.then_inc(h2_turned, 1)
                    pe.wait_ge(h2T_ready, 2 * n + 2)
                    if n >= 1:
                        pe.wait_ge(rl_ready, n)
                    for k in range(KD):
                        mm = pe.matmul(PS[:, 6, 0:NG + NE], hT[:, k, n * P:(n + 1) * P], wr[:, k, :], start=(k == 0), stop=(k == KD - 1))
                    mm.then_inc(rl_mm, 1)

                pe.wait_ge(wr_loaded, 16)
                for n in range(NT):
                    project(n)
                    if n >= 1:
                        route(n - 1)
                route(NT - 1)
                pe.wait_ge(y_mm, 2 * NT)
                pe.nop().then_inc(w_used, 2)

            @block.scalar
            def _(act):
                st = Steps(act, astep)
                for n in range(NT):
                    for b in range(2):
                        act.wait_ge(m_turned, 2 * n + b + 1)
                        if n >= 2:
                            act.wait_ge(y_mm, 2 * (n - 1))
                        act.activation(mT[:, n % 2, 4 * b:4 * b + 4, :], PS[:, b, :].rearrange("p (k t) -> p k t", k=4), ACT.Copy)\
                           .then_inc(mT_ready, 1)
                    act.wait_ge(x1_ready, 2 * n + 2)
                    st.done(act.activation(junk[:, :], mix[:, n, :], ACT.Square, accum_out=ss[:, n:n + 1]))
                    st.done(act.activation(rr[:, n:n + 1], ss[:, n:n + 1], ACT.Ln, bias=eps[:, :], scale=1.0 / D))
                    act.activation(rr[:, n:n + 1], rr[:, n:n + 1], ACT.Exp, scale=-0.5).then_inc(r2_ready, 1)

            @block.vector
            def _(dve):
                def residual(n):
                    dve.wait_ge(xr_loaded[n % 2], 16 * (n // 2 + 1))
                    for b in range(2):
                        dve.wait_ge(y_mm, 2 * n + b + 1)
                        if b == 0:
                            dve.wait_ge(m_turned, 2 * n + 2)
                        c_ = slice(512 * b, 512 * b + 512)
                        dve.tensor_tensor(mix[:, n, c_], PS[:, 2 + b, :], xr[:, n % 2, c_], ALU.add).then_inc(x1_ready, 1)

                def norm(n):
                    dve.wait_ge(r2_ready, n + 1)
                    if n >= 2:
                        dve.wait_ge(h2_stored[n % 2], 16 * (n // 2))
                    dve.tensor_scalar(h2[:, n % 2, :], mix[:, n, :], rr[:, n:n + 1], None, ALU.mult).then_inc(h2_ready, 1)
                    for b in range(2):
                        dve.wait_ge(h2_turned, 2 * n + b + 1)
                        g = par("ffn_gain")[:, 4 * b:4 * b + 4].unsqueeze(2).to_broadcast([P, 4, P])
                        dve.tensor_tensor(hT[:, 4 * b:4 * b + 4, n * P:(n + 1) * P],
                                          PS[:, 4 + b, :].rearrange("p (k t) -> p k t", k=4), g, ALU.mult).then_inc(h2T_ready, 1)

                def logits(n):
                    dve.wait_ge(rl_mm, n + 1)
                    dve.tensor_tensor(rl[:, n, :], PS[:, 6, 0:NG + NE], prm[:, PC["b_rg"][0]:PC["b_re"][1]], ALU.add).then_inc(rl_ready, 1)

                for n in range(NT):
                    residual(n)
                    if n >= 1:
                        norm(n - 1)
                        logits(n - 1)
                norm(NT - 1)
                logits(NT - 1)

        dest_i = sb("dest_i", [P, NT, 2], I32)
        gates = sb("gates", [P, NT, 2])
        plan = sb("plan", [1, 2 + 16], I32)
        slots_i = sb("slots_i", [P, LST], I32)
        with ExitStack() as c, nc.Block() as block:
            new_phase(c)
            def rt(name, *shape, dt=F32):
                return sb(name, [P, *shape], dt, c=c)
            glp, g8, gi8 = rt("glp", NT, 8), rt("g8", NT, 8), rt("gi8", NT, 8, dt=U32)
            gidx, oh_g, gd, gs = rt("gidx", NT), rt("oh_g", NT, NG), rt("gd", NT, NG), rt("gs", NT)
            eall, esel = rt("eall", NT, NG, EPG), rt("esel", NT, EPG)
            e8, ei8, eid, rr = rt("e8", NT, 8), rt("ei8", NT, 8, dt=U32), rt("eid", NT, 2), rt("rr3", NT)
            Mk, Mb, onesb = rt("Mk", 2, NT, NE), rt("Mb", NT, NE, dt=BF16), rt("onesb", P, dt=BF16)
            pre, rank, ov, cum, big = rt("pre", NT, NE), rt("rank", NT, NE), rt("ov", NE), rt("cum", 2, NE), rt("big", NT, NE)
            cnt, ia, ib = rt("cnt", NE), rt("ia", NE), rt("ib", NE)
            tmpd, dest_f, nb_f, cmp_, tok = rt("tmpd", NT, NE), rt("dest_f", NT, 2), rt("nb_f", 18), rt("cmp", 16, NE), rt("tok", NT)
            zl = sb("zl", [LST, P], c=c)
            lrow = sb("lrow", [LST, P], c=c)
            g_exp, g_act, Mb_ready, rank_mm, dest_ready, zl_ready = (sem(n_) for n_ in (
                "g_exp", "g_act", "Mb_ready", "rank_mm", "dest_ready", "zl_ready"))
            zl_stored, listed, lrow_loaded, l_turned = sem("zl_stored"), sem("listed"), sem("lrow_loaded"), sem("l_turned")
            dstep = sem("r_dve_step")

            @block.sync
            def _(sp):
                sp.wait_ge(zl_ready, 1)
                sp.dma_start(list_dram.rearrange("(a b) o -> a (b o)", b=P), zl[:, :]).then_inc(zl_stored, 16)
                sp.wait_ge(listed, 16 * 2 * NT)
                sp.dma_start(lrow[:, :], list_dram.rearrange("(a b) o -> a (b o)", b=P)).then_inc(lrow_loaded, 16)

            @block.gpsimd
            def _(pool):
                pool.wait_ge(zl_stored, 16)
                pool.wait_ge(dest_ready, 1)
                for n in range(NT):
                    for k in range(2):
                        pool.indirect_dma_start(list_dram, bass.IndirectOffsetOnAxis(ap=dest_i[:, n, k:k + 1], axis=0),
                                                tok[:, n:n + 1], None).then_inc(listed, 16)

            @block.tensor
            def _(pe):
                pe.wait_ge(Mb_ready, 1)
                m = Mb[:, :, :].rearrange("p n e -> p (n e)")
                pe.matmul(PS[:, 0, 0:NT * NE], before, m, start=True, stop=True)
                pe.matmul(PS[:, 1, 0:NT * NE], onesb[:, :], m, start=True, stop=True).then_inc(rank_mm, 1)
                pe.wait_ge(lrow_loaded, 16)
                pe.transpose(PS[:, 2, 0:LST], lrow[:, :], ident[0:LST, 0:LST]).then_inc(l_turned, 1)

            @block.scalar
            def _(act):
                act.wait_ge(g_exp, 1)
                act.activation(gd[:, :, :], gd[:, :, :], ACT.Exp).then_inc(g_act, 1)
                act.wait_ge(g_exp, 2)
                act.activation(rr[:, :], rr[:, :], ACT.Exp).then_inc(g_act, 1)

            @block.vector
            def _(dve):
                st = Steps(dve, dstep)
                dve.memset(zl[:, :], 0.0).then_inc(zl_ready, 1)
                st.done(dve.memset(onesb[:, :], 1.0))
                st.done(dve.memset(glp[:, :, :], NEG))
                st.done(dve.tensor_copy(glp[:, :, 0:NG], rl[:, :, 0:NG]))
                for n in range(NT):
                    st.done(dve.max(g8[:, n, :], glp[:, n, :]))
                    st.done(dve.max_index(gi8[:, n, :], g8[:, n, :], glp[:, n, :]))
                st.done(dve.tensor_copy(gidx[:, :], gi8[:, :, 0]))
                iota = kc[:, K_IOTA, :]
                st.done(dve.tensor_tensor(oh_g[:, :, :], iota[:, 0:NG].unsqueeze(1).to_broadcast([P, NT, NG]),
                                          gidx[:, :].unsqueeze(2).to_broadcast([P, NT, NG]), ALU.is_equal))
                dve.tensor_tensor(gd[:, :, :], rl[:, :, 0:NG], g8[:, :, 0:1].to_broadcast([P, NT, NG]), ALU.subtract).then_inc(g_exp, 1)
                for n in range(NT):
                    st.done(dve.tensor_tensor(eall[:, n, :, :], rl[:, n, NG:].rearrange("p (g e) -> p g e", g=NG),
                                              oh_g[:, n, :].unsqueeze(2).to_broadcast([P, NG, EPG]), ALU.mult))
                    st.done(dve.tensor_reduce(esel[:, n, :], eall[:, n, :, :].rearrange("p g e -> p e g"), AX.X, ALU.add))
                    st.done(dve.max(e8[:, n, :], esel[:, n, :]))
                    st.done(dve.max_index(ei8[:, n, :], e8[:, n, :], esel[:, n, :]))
                dve.tensor_tensor(rr[:, :], e8[:, :, 1], e8[:, :, 0], ALU.subtract).then_inc(g_exp, 1)
                st.done(dve.tensor_copy(eid[:, :, :], ei8[:, :, 0:2]))
                st.done(dve.tensor_scalar(gidx[:, :], gidx[:, :], float(EPG), None, ALU.mult))
                st.done(dve.tensor_tensor(eid[:, :, :], eid[:, :, :], gidx[:, :].unsqueeze(2).to_broadcast([P, NT, 2]), ALU.add))
                for k in range(2):
                    st.done(dve.tensor_tensor(Mk[:, k, :, :], iota[:, 0:NE].unsqueeze(1).to_broadcast([P, NT, NE]),
                                              eid[:, :, k:k + 1].to_broadcast([P, NT, NE]), ALU.is_equal))
                dve.tensor_tensor(Mb[:, :, :], Mk[:, 0, :, :], Mk[:, 1, :, :], ALU.add).then_inc(Mb_ready, 1)
                dve.wait_ge(g_act, 2)
                st.done(dve.tensor_reduce(gs[:, :], gd[:, :, :], AX.X, ALU.add))
                st.done(dve.reciprocal(gs[:, :], gs[:, :]))
                st.done(dve.tensor_scalar(gates[:, :, 1], rr[:, :], 1.0, None, ALU.add))
                st.done(dve.reciprocal(gates[:, :, 1], gates[:, :, 1]))
                st.done(dve.tensor_tensor(gates[:, :, 0], gates[:, :, 1], gs[:, :], ALU.mult))
                st.done(dve.tensor_tensor(gates[:, :, 1], gates[:, :, 0], rr[:, :], ALU.mult))
                dve.wait_ge(rank_mm, 1)
                st.done(dve.memset(pre[:, 0, :], 0.0))
                tot = PS[:, 1, 0:NT * NE].rearrange("p (n e) -> p n e", n=NT)
                for n in range(1, NT):
                    st.done(dve.tensor_tensor(pre[:, n, :], pre[:, n - 1, :], tot[:, n - 1, :], ALU.add))
                st.done(dve.tensor_tensor(cnt[:, :], pre[:, NT - 1, :], tot[:, NT - 1, :], ALU.add))
                st.done(dve.tensor_tensor(rank[:, :, :], pre[:, :, :], PS[:, 0, 0:NT * NE].rearrange("p (n e) -> p n e", n=NT), ALU.add))
                st.done(dve.tensor_scalar(ov[:, :], cnt[:, :], float(P), None, ALU.is_gt))
                for m in range(2, NT):
                    st.done(dve.scalar_tensor_tensor(out=ov[:, :], in0=cnt[:, :], scalar=float(P * m), in1=ov[:, :], op0=ALU.is_gt, op1=ALU.add))
                st.done(dve.tensor_copy(cum[:, 0, :], ov[:, :]))
                a = 0
                for sh in (1, 2, 4, 8, 16):
                    st.done(dve.tensor_copy(cum[:, 1 - a, 0:sh], cum[:, a, 0:sh]))
                    st.done(dve.tensor_tensor(cum[:, 1 - a, sh:NE], cum[:, a, sh:NE], cum[:, a, 0:NE - sh], ALU.add))
                    a = 1 - a
                incl = cum[:, a, :]
                st.done(dve.tensor_scalar(ia[:, :], iota[:, 0:NE], float(P), None, ALU.mult))
                st.done(dve.tensor_tensor(ib[:, :], incl, ov[:, :], ALU.subtract))
                st.done(dve.tensor_scalar(ib[:, :], ib[:, :], float(NE - 1), float(P), ALU.add, ALU.mult))
                st.done(dve.tensor_tensor(ib[:, :], ib[:, :], ia[:, :], ALU.subtract))
                st.done(dve.tensor_scalar(big[:, :, :], rank[:, :, :], float(P), None, ALU.is_ge))
                st.done(dve.tensor_tensor(big[:, :, :], big[:, :, :], ib[:, :].unsqueeze(1).to_broadcast([P, NT, NE]), ALU.mult))
                st.done(dve.tensor_tensor(rank[:, :, :], rank[:, :, :], big[:, :, :], ALU.add))
                st.done(dve.tensor_tensor(rank[:, :, :], rank[:, :, :], ia[:, :].unsqueeze(1).to_broadcast([P, NT, NE]), ALU.add))
                for k in range(2):
                    st.done(dve.tensor_tensor(tmpd[:, :, :], rank[:, :, :], Mk[:, k, :, :], ALU.mult))
                    st.done(dve.tensor_reduce(dest_f[:, :, k], tmpd[:, :, :], AX.X, ALU.add))
                for n in range(NT):
                    st.done(dve.tensor_scalar(tok[:, n:n + 1], kc[:, K_HO, 2:3], float(n * P), None, ALU.add))
                dve.tensor_copy(dest_i[:, :, :], dest_f[:, :, :]).then_inc(dest_ready, 1)
                st.done(dve.tensor_scalar(nb_f[:, 0:1], incl[:, NE - 1:NE], float(NE), None, ALU.add))
                st.done(dve.memset(nb_f[:, 1:2], float(NE - 1)))
                st.done(dve.tensor_tensor(cmp_[:, :, :], incl.unsqueeze(1).to_broadcast([P, 16, NE]),
                                          iota[:, 0:16].unsqueeze(2).to_broadcast([P, 16, NE]), ALU.is_le))
                st.done(dve.tensor_reduce(nb_f[:, 2:18], cmp_[:, :, :], AX.X, ALU.add))
                st.done(dve.tensor_scalar(nb_f[:, 2:18], nb_f[:, 2:18], float(NE - 1), None, ALU.min))
                st.done(dve.tensor_copy(plan[:, :], nb_f[0:1, :]))
                dve.wait_ge(l_turned, 1)
                st.done(dve.tensor_copy(slots_i[:, :], PS[:, 2, 0:LST]))

        n_chunks = len(chunks)
        SL = [(n_chunks + j) % 3 for j in range(3)]
        BASE = [seen[s] for s in SL]
        wg_s, wu_s = wring[SL[0]], wring[SL[1]]
        wd_s = wring[SL[2]][:, :, :].rearrange("p k n -> p (k n)").rearrange("p (k n) -> p k n", k=DE // P)
        KH = DE // P
        with ExitStack() as c, nc.Block() as block:
            new_phase(c)
            idxb = sb("idxb", [P, 1], I32, c=c)
            settle, settled = sb("settle", [P, 1], c=c), sb("settled", [P, 1], c=c)
            xg = sb("xg", [P, D], c=c)
            xT = sb("xT", [P, KD, P], c=c)
            sg = sb("sg", [P, DE], c=c)
            ac = sb("ac", [P, DE], c=c)
            aT = sb("aT", [P, KH, P], c=c)
            ysb = sb("ysb", [P, D], c=c)
            idx_ready, x_gathered = sem("idx_ready"), sem("x_gathered")
            x_turned, xT_ready, silu_ready, ac_ready, a_turned, aT_ready = (sem(n_) for n_ in (
                "x_turned", "xT_ready", "e_silu_ready", "ac_ready", "a_turned", "aT_ready"))
            y0_mm, ysb0_ready, ysb1_ready, y_stored = sem("y0_mm"), sem("ysb0_ready"), sem("ysb1_ready"), sem("y_stored")
            gate_done, up_done, down_done = (sem(n_) for n_ in ("gate_done", "up_done", "down_done"))

            def blocks(eng):
                return eng.value_load(plan[0:1, 0:1], min_val=NE, max_val=MAXB)

            @block.sync
            def _(sp):
                def load(j, e, i):
                    src = (w_g, w_u, w_d)[j]
                    src = src[e] if isinstance(e, int) else src[bass.ds(e, 1), :, :].rearrange("o a b -> (o a) b")
                    dst = (wg_s[:, :, :], wu_s[:, :, :], wd_s)[j]
                    sp.wait_ge((gate_done, up_done, down_done)[j], i + 1)
                    sp.dma_start(dst, src.rearrange("(k p) n -> p k n", p=P)).then_inc(w_loaded[SL[j]], 16)

                def expert(i):
                    return sp.value_load(plan[0:1, bass.ds(i - (NE - 2), 1)], min_val=0, max_val=NE - 1)

                load(0, 0, 0)
                load(1, 0, 0)
                with sp.Fori(1, NE) as i:
                    load(0, i, i)
                    load(2, i - 1, i - 1)
                    load(1, i, i)
                nb = blocks(sp)
                with sp.If(nb > NE):
                    with sp.Fori(NE, nb) as i:
                        e = expert(i)
                        load(0, e, i)
                        load(2, expert(i - 1), i - 1)
                        load(1, e, i)
                load(2, expert(nb - 1), nb - 1)

            @block.gpsimd
            def _(pool):
                nb = blocks(pool)
                with pool.Fori(0, nb) as i:
                    pool.wait_ge(x_turned, 2 * i + 1)
                    pool.tensor_copy(idxb[:, :], slots_i[:, bass.ds(i, 1)]).then_inc(idx_ready, 1)
                    pool.wait_ge(idx_ready, i + 1)
                    pool.tensor_tensor(settle[:, :], eps[:, :], eps[:, :], ALU.add)
                    pool.indirect_dma_start(xg[:, :], None, h2_dram, bass.IndirectOffsetOnAxis(ap=idxb[:, 0:1], axis=0))\
                        .then_inc(x_gathered, 16)

            @block.tensor
            def _(pe):
                def turn_x(b, i):
                    if b == 0:
                        pe.wait_ge(x_gathered, 16 * i + 16)
                    pe.wait_ge(xT_ready, 2 * i)
                    for k in range(4):
                        mm = pe.transpose(PS[:, b, k * P:(k + 1) * P], xg[:, (4 * b + k) * P:(4 * b + k + 1) * P], ident)
                    mm.then_inc(x_turned, 1)

                def gate(b, i):
                    if b == 0:
                        pe.wait_ge(w_loaded[SL[0]], 16 * i + BASE[0] + 16)
                        pe.wait_ge(silu_ready, i + 1)
                    pe.wait_ge(xT_ready, 2 * i + b + 2)
                    for k in range(4 * b, 4 * b + 4):
                        mm = pe.matmul(PS[:, 2, :], xT[:, k, :], wg_s[:, k, :], start=(k == 0), stop=(k == KD - 1))
                    if b == 1:
                        mm.then_inc(gate_done, 1)

                def up(b, i):
                    if b == 0:
                        pe.wait_ge(w_loaded[SL[1]], 16 * i + BASE[1] + 16)
                        pe.wait_ge(ac_ready, i + 1)
                    for k in range(4 * b, 4 * b + 4):
                        mm = pe.matmul(PS[:, 3, :], xT[:, k, :], wu_s[:, k, :], start=(k == 0), stop=(k == KD - 1))
                    if b == 1:
                        mm.then_inc(up_done, 1)

                def turn_a(i):
                    pe.wait_ge(ac_ready, i + 2)
                    pe.wait_ge(aT_ready, i + 1)
                    for k in range(KH):
                        mm = pe.transpose(PS[:, 4, k * P:(k + 1) * P], ac[:, k * P:(k + 1) * P], ident)
                    mm.then_inc(a_turned, 1)

                def down(i):
                    pe.wait_ge(w_loaded[SL[2]], 16 * i + BASE[2] + 16)
                    pe.wait_ge(aT_ready, i + 2)
                    for b, (s_mm, s_out) in enumerate(((y0_mm, ysb0_ready), (down_done, ysb1_ready))):
                        pe.wait_ge(s_out, i + 1)
                        for k in range(KH):
                            mm = pe.matmul(PS[:, 5 + b, :], aT[:, k, :], wd_s[:, k, 512 * b:512 * b + 512], start=(k == 0), stop=(k == KH - 1))
                        mm.then_inc(s_mm, 1)

                for s_ in (x_turned, gate_done, up_done, down_done):
                    pe.nop().then_inc(s_, 1)
                nb = blocks(pe)
                for b in range(2):
                    if b == 0:
                        pe.wait_ge(x_gathered, 16)
                    for k in range(4):
                        mm = pe.transpose(PS[:, b, k * P:(k + 1) * P], xg[:, (4 * b + k) * P:(4 * b + k + 1) * P], ident)
                    mm.then_inc(x_turned, 1)
                gate(0, 0)
                gate(1, 0)
                with pe.Fori(1, nb) as i:
                    up(0, i - 1)
                    turn_x(0, i)
                    up(1, i - 1)
                    turn_x(1, i)
                    gate(0, i)
                    turn_a(i - 1)
                    gate(1, i)
                    down(i - 1)
                up(0, nb - 1)
                up(1, nb - 1)
                turn_a(nb - 1)
                down(nb - 1)

            @block.scalar
            def _(act):
                act.preload_act_table_set("silu_and_others")
                for s_ in (silu_ready, aT_ready, ysb0_ready):
                    act.nop().then_inc(s_, 1)
                act.nop().then_inc(y_stored, 16)
                nb = blocks(act)
                with act.Fori(0, nb) as i:
                    act.wait_ge(gate_done, i + 2)
                    act.wait_ge(ac_ready, i + 1)
                    act.activation(sg[:, :], PS[:, 2, :], ACT.Silu).then_inc(silu_ready, 1)
                    act.wait_ge(a_turned, i + 1)
                    act.wait_ge(down_done, i + 1)
                    act.activation(aT[:, :, :], PS[:, 4, :].rearrange("p (k t) -> p k t", k=KH), ACT.Copy).then_inc(aT_ready, 1)
                    act.wait_ge(y0_mm, i + 1)
                    act.wait_ge(y_stored, 16 * i + 16)
                    act.activation(ysb[:, 0:512], PS[:, 5, :], ACT.Copy).then_inc(ysb0_ready, 1)
                    act.wait_ge(ysb0_ready, i + 2)
                    act.wait_ge(ysb1_ready, i + 2)
                    act.dma_start(y_dram[bass.ds(i * P, P), :], ysb[:, :]).then_inc(y_stored, 16)
                act.wait_ge(y_stored, 16 * nb + 16)
                act.activation(settled[:, :], eps[:, :], ACT.Copy)

            @block.vector
            def _(dve):
                def rows(b, i):
                    dve.wait_ge(x_turned, 2 * i + b + 2)
                    g = par("ffn_gain")[:, 4 * b:4 * b + 4].unsqueeze(2).to_broadcast([P, 4, P])
                    dve.tensor_tensor(xT[:, 4 * b:4 * b + 4, :], PS[:, b, :].rearrange("p (k t) -> p k t", k=4), g, ALU.mult)\
                       .then_inc(xT_ready, 1)

                def act_mul(i):
                    dve.wait_ge(up_done, i + 2)
                    dve.wait_ge(silu_ready, i + 2)
                    dve.tensor_tensor(ac[:, :], sg[:, :], PS[:, 3, :], ALU.mult).then_inc(ac_ready, 1)

                def y_half(i):
                    dve.wait_ge(down_done, i + 2)
                    dve.wait_ge(y_stored, 16 * i + 16)
                    dve.tensor_copy(ysb[:, 512:D], PS[:, 6, :]).then_inc(ysb1_ready, 1)

                for s_ in (xT_ready, ac_ready, ysb1_ready):
                    dve.nop().then_inc(s_, 1)
                nb = blocks(dve)
                rows(0, 0)
                rows(1, 0)
                with dve.Fori(1, nb) as i:
                    rows(0, i)
                    act_mul(i - 1)
                    rows(1, i)
                    y_half(i - 1)
                act_mul(nb - 1)
                y_half(nb - 1)

        with ExitStack() as c, nc.Block() as block:
            new_phase(c)
            yg = sb("yg", [P, 2, 2, D], c=c)
            y_gathered = [sem("y_gathered0"), sem("y_gathered1")]
            sum_ready, out_stored, cstep = sem("sum_ready"), sem("out_stored"), sem("c_step")

            @block.gpsimd
            def _(pool):
                for n in range(NT):
                    if n >= 2:
                        pool.wait_ge(sum_ready, n - 1)
                    for k in range(2):
                        pool.indirect_dma_start(yg[:, n % 2, k, :], None, y_dram,
                                                bass.IndirectOffsetOnAxis(ap=dest_i[:, n, k:k + 1], axis=0)).then_inc(y_gathered[n % 2], 16)

            @block.vector
            def _(dve):
                st = Steps(dve, cstep)
                for n in range(NT):
                    dve.wait_ge(y_gathered[n % 2], 32 * (n // 2 + 1))
                    st.done(dve.scalar_tensor_tensor(out=mix[:, n, :], in0=yg[:, n % 2, 0, :], scalar=gates[:, n, 0:1], in1=mix[:, n, :],
                                                     op0=ALU.mult, op1=ALU.add))
                    dve.scalar_tensor_tensor(out=mix[:, n, :], in0=yg[:, n % 2, 1, :], scalar=gates[:, n, 1:2], in1=mix[:, n, :],
                                             op0=ALU.mult, op1=ALU.add).then_inc(sum_ready, 1)

            @block.sync
            def _(sp):
                for n in range(NT):
                    sp.wait_ge(sum_ready, n + 1)
                    sp.dma_start(out[n * P:(n + 1) * P, :], mix[:, n, :]).then_inc(out_stored, 16)
                sp.wait_ge(out_stored, 16 * NT)
    return nc


def shape_constants(np, bf16):
    kc = np.zeros((P, NKC, P), np.float32)
    i = np.arange(P)
    kc[:, K_ID] = np.eye(P)
    kc[:, K_U] = i[:, None] <= i[None, :]
    kc[:, K_L] = i[:, None] > i[None, :]
    kc[:, K_ONE] = 1
    for l in range(7):
        same = (i[:, None] >> (l + 1)) == (i[None, :] >> (l + 1))
        kc[:, K_LM + l] = same & (((i[:, None] >> l) & 1) == 0) & (((i[None, :] >> l) & 1) == 1)
    for h in range(H_GLA):
        bd = kc[:, K_BD:K_BD + 2].reshape(P, GV)
        kc[:, K_BD + h // 2, (h % 2) * HD:(h % 2 + 1) * HD] = (i[:, None] // DK) == h
    kc[0:HD, K_HO, 0] = 1
    kc[HD:P, K_HO, 1] = 1
    kc[:, K_IOTA] = i[None, :]
    kc[:, K_HO, 2] = i
    km = np.zeros((P, 5, P), np.float32)
    km[:, 0] = np.eye(P)
    km[:, 1] = np.where(i[None, :] > i[:, None], NEG, 0)
    km[:, 2] = np.where(i[:, None] > i[None, :], NEG, 0)
    km[:, 3] = np.where(i[:, None] >= i[None, :], NEG, 0)
    km[:, 4] = i[:, None] < i[None, :]
    return kc, km.astype(bf16)


def layout(np, inputs):
    a = {k: np.asarray(v)[0] if k != "x" else np.asarray(v)[0] for k, v in inputs.items()}

    def cols(v):
        return np.ascontiguousarray(v.reshape(-1, P).T)

    def rows(v):
        return np.broadcast_to(v[None, :], (P, v.shape[0]))

    prm = np.concatenate([cols(a["attn_norm"]), cols(a["ffn_norm"]), rows(a["fox_q_norm"]), rows(a["fox_k_norm"]),
                          rows(a["fox_o_norm"]), rows(a["gdn_o_norm"]), rows(a["gla_o_norm"]), rows(a["fox_f_bias"]),
                          rows(a["gdn_dt_bias"]), rows(a["gdn_a_log"]),
                          a["gdn_conv"].reshape(4, 9, P).transpose(2, 1, 0).reshape(P, 36),
                          rows(a["b_router_group"]), rows(a["b_router_expert"]), rows(a["gla_b_a"])], axis=1)
    return {
        "x": a["x"], "w_in": a["w_in"], "w_out": a["w_out"],
        "w_router": np.concatenate([a["w_router_group"], a["w_router_expert"]], axis=1),
        "w_a2": a["gla_w_a2"], "w_g": a["w_expert_gate"], "w_u": a["w_expert_up"], "w_d": a["w_expert_down"],
        "params": np.ascontiguousarray(prm),
    }


def kernel(**inputs):
    import numpy as np
    import ml_dtypes
    import concourse.bacc as bacc
    from concourse.bass_utils import run_bass_kernel_spmd

    nc = bacc.Bacc("TRN2", target_bir_lowering=False, num_devices=1)
    data = layout(np, inputs)
    data["consts"], data["masks"] = shape_constants(np, ml_dtypes.bfloat16)
    arrays, args = {}, {}
    for name, v in data.items():
        v = np.ascontiguousarray(v)
        arrays["in_" + name] = v
        args[name] = nc.dram_tensor("in_" + name, v.shape, mybir.dt.from_np(v.dtype), kind="ExternalInput").ap()
    out = nc.dram_tensor("out_0", (S, D), F32, kind="ExternalOutput").ap()
    trunk_kernel(nc, out=out, **args)
    r = run_bass_kernel_spmd(nc, [arrays], core_ids=[0])
    return r.results[0]["out_0"].reshape(1, S, D)
```

```python
import math
from contextlib import ExitStack

import concourse.bass as bass
from concourse import mybir

P = 128
S = 1024
D = 1024
KD = D // P
NT = S // P
HD = 64
H_FOX, H_GDN, H_GLA = 6, 6, 4
FOX, GDN = H_FOX * HD, H_GDN * HD
DK, GK, GV = 32, 128, 256
RANK = 16
NG, EPG, NE = 4, 8, 32
DE = 512
EPS = 1e-6
NEG = -1e30
MAXB = NE + 2 * S // P - 1
LST = 48

F32 = mybir.dt.float32
BF16 = mybir.dt.bfloat16
I32 = mybir.dt.int32
U32 = mybir.dt.uint32
ALU = mybir.AluOpType
ACT = mybir.ActivationFunctionType
AX = mybir.AxisListType

C_FQ, C_FK, C_FV = 0, FOX, 2 * FOX
C_GQKV = 3 * FOX + H_FOX
C_GATE = C_GQKV + 3 * GDN
C_LQ = C_GATE + GDN + 2 * H_GDN
C_LV = C_LQ + 2 * GK
C_LA = C_LV + 2 * GV
N_IN = C_LA + RANK
W_VF = FOX + H_FOX
W_GAB = GDN + 2 * H_GDN

(K_ID, K_U, K_L, K_ONE, K_LM) = (0, 1, 2, 3, 4)
KR = 96
K_BD = 11
K_HO = 13
K_PAIR = 26
K_IOTA = 14
NKC = 15
PC = {}
_at = 0
for _n, _w in (("attn_gain", KD), ("ffn_gain", KD), ("fox_q", HD), ("fox_k", HD), ("fox_o", HD), ("gdn_o", HD),
               ("gla_o", HD), ("f_bias", H_FOX), ("dt_bias", H_GDN), ("a_log", H_GDN), ("conv", 36),
               ("b_rg", NG), ("b_re", NE), ("b_a", GK)):
    PC[_n] = (_at, _at + _w)
    _at += _w
NPC = _at


class Steps:

    def __init__(self, eng, sem):
        self.eng, self.sem, self.n = eng, sem, 0

    def done(self, ins):
        self.n += 1
        ins.then_inc(self.sem, 1)
        self.eng.wait_ge(self.sem, self.n)


def trunk_kernel(nc, x, w_in, w_out, w_router, w_a2, w_g, w_u, w_d, params, consts, masks, out):
    ctx = ExitStack()

    names = {}

    def sb(name, shape, dt=F32, c=None):
        names[name] = names.get(name, -1) + 1
        name += f"_{names[name]}" if names[name] else ""
        return (c or ctx).enter_context(nc.sbuf_tensor(name, shape, dt))

    phase_sems = [None]

    def sem(name):
        handle = nc.alloc_semaphore(name)
        if phase_sems[0] is not None:
            phase_sems[0].append(handle)
        return handle

    def new_phase(c):
        phase_sems[0] = []
        c.callback(end_phase)

    def end_phase():
        nc.clear_and_free_semaphores(phase_sems[0])
        nc.all_engine_barrier()
        phase_sems[0] = None

    with ctx:
        PS = ctx.enter_context(nc.psum_tensor("PS", [P, 8, 512], F32))
        kc = sb("kc", [P, NKC, P])
        km = sb("km", [P, 5, P], BF16)
        prm = sb("prm", [P, NPC])
        eps = sb("eps", [P, 1])
        eps_hd = sb("eps_hd", [P, 1])
        wslots = sb("wslots", [P, 3, KD, 512])
        wring = [wslots[:, i, :, :] for i in range(3)]
        hT = sb("hT", [P, KD, S])
        mix = sb("mix", [P, NT, D])
        h2_dram = nc.dram_tensor("h2_scratch", (S, D), F32, kind="Internal").ap()
        y_dram = nc.dram_tensor("y_scratch", (MAXB * P, D), F32, kind="Internal").ap()
        list_dram = nc.dram_tensor("list_scratch", (LST * P, 1), F32, kind="Internal").ap()

        ident, U, L, ones = (kc[:, i, :] for i in (K_ID, K_U, K_L, K_ONE))
        identb, mask_q, mask_incl, mask_strict, before = (km[:, i, :] for i in range(5))

        def par(name):
            a, b = PC[name]
            return prm[:, a:b]

        w_loaded = [sem(f"w_loaded{i}") for i in range(3)]
        w_used = sem("w_used")
        const_loaded = sem("const_loaded")

        w_in_v = w_in.rearrange("(k p) n -> p k n", p=P)
        w_out_v = w_out.rearrange("(k p) n -> p k n", p=P)
        chunks = [[(w_in_v[:, :, a:b], 0)] for a, b in
                  ((C_FV, C_FV + W_VF), (C_FQ, C_FK), (C_FK, C_FV),
                   (C_GATE, C_LQ), (C_GQKV, C_GQKV + 512), (C_GQKV + 512, C_GQKV + 1024), (C_GQKV + 1024, C_GATE),
                   (C_LQ, C_LV), (C_LV, C_LA))]
        chunks[7].append((w_in_v[:, :, C_LA:N_IN], 2 * GK))
        chunks += [[(w_out_v[:, :, a:a + 512], 0)] for a in (0, 512)]
        CH_VF, CH_Q, CH_K, CH_GAB, CH_T0, CH_T1, CH_T2, CH_L, CH_LVR, CH_O0, CH_O1 = range(11)
        n_loads, seen = [], [0, 0, 0]
        for c, parts in enumerate(chunks):
            seen[c % 3] += 16 * len(parts)
            n_loads.append(seen[c % 3])

        def load_chunk(eng, c):
            if c >= 3:
                eng.wait_ge(w_used, c - 2)
            for src, at in chunks[c]:
                eng.dma_start(wring[c % 3][:, :, at:at + src.shape[2]], src).then_inc(w_loaded[c % 3], 16)

        def chunk_ready(eng, c):
            eng.wait_ge(w_loaded[c % 3], n_loads[c])

        def project_tile(pe, c, n, bank, cols):
            for k in range(KD):
                mm = pe.matmul(PS[:, bank, 0:cols], hT[:, k, n * P:(n + 1) * P], wring[c % 3][:, k, 0:cols],
                               start=(k == 0), stop=(k == KD - 1))
            return mm

        fox = ExitStack()
        vf = sb("vf", [P, NT, W_VF], c=fox)
        with ExitStack() as c, nc.Block() as block:
            new_phase(c)
            NX = 4
            xin = sb("xin", [P, NX, D], c=c)
            junk = sb("junk", [P, D], c=c)
            ss = sb("ss", [P, NT], c=c)
            lnss = sb("lnss", [P, NT], c=c)
            rstd = sb("rstd", [P, NT], c=c)
            x_loaded = [sem(f"x_loaded{i}") for i in range(NX)]
            vf_proj, vf_ready = sem("vf_proj"), sem("vf_ready")
            rstd_ready, act_step = sem("rstd_ready"), sem("act_step")
            h_ready, h_turned, hT_ready, eps_ready = sem("h_ready"), sem("h_turned"), sem("hT_ready"), sem("eps_ready")

            @block.sync
            def _(sp):
                for n in range(2):
                    sp.dma_start(xin[:, n, :], x[n * P:(n + 1) * P, :]).then_inc(x_loaded[n], 16)
                sp.dma_start(prm[:, :], params).then_inc(const_loaded, 16)
                sp.dma_start(kc[:, :, :], consts).then_inc(const_loaded, 16)
                sp.dma_start(km[:, :, :], masks).then_inc(const_loaded, 16)
                for n in range(2, NT):
                    if n == 3:
                        load_chunk(sp, 0)
                    if n >= NX:
                        sp.wait_ge(h_turned, 2 * (n - NX + 1))
                    sp.dma_start(xin[:, n % NX, :], x[n * P:(n + 1) * P, :]).then_inc(x_loaded[n % NX], 16)
                for k in (1, 2):
                    load_chunk(sp, k)

            @block.gpsimd
            def _(pool):
                pool.memset(eps_hd[:, :], EPS * HD).then_inc(eps_ready, 1)
                pool.memset(eps[:, :], EPS).then_inc(eps_ready, 1)

            @block.scalar
            def _(act):
                st = Steps(act, act_step)

                def values(n):
                    act.wait_ge(vf_proj, n + 1)
                    act.activation(vf[:, n, :], PS[:, 4 + n % 2, 0:W_VF], ACT.Copy).then_inc(vf_ready, 1)

                act.wait_ge(eps_ready, 2)
                act.preload_act_table_set("natural_log_exp_and_others")
                for n in range(NT):
                    act.wait_ge(x_loaded[n % NX], 16 * (n // NX + 1))
                    st.done(act.activation(junk[:, :], xin[:, n % NX, :], ACT.Square, accum_out=ss[:, n:n + 1]))
                    st.done(act.activation(lnss[:, n:n + 1], ss[:, n:n + 1], ACT.Ln, bias=eps[:, :], scale=1.0 / D))
                    act.activation(rstd[:, n:n + 1], lnss[:, n:n + 1], ACT.Exp, scale=-0.5).then_inc(rstd_ready, 1)
                    if n >= 2:
                        values(n - 2)
                values(NT - 2)
                values(NT - 1)

            @block.vector
            def _(dve):
                dve.wait_ge(const_loaded, 48)
                for n in range(NT):
                    dve.wait_ge(rstd_ready, n + 1)
                    dve.tensor_scalar(xin[:, n % NX, :], xin[:, n % NX, :], rstd[:, n:n + 1], None, ALU.mult).then_inc(h_ready, 1)
                    for b in range(2):
                        dve.wait_ge(h_turned, 2 * n + b + 1)
                        bank = 2 * (n % 2) + b
                        g = par("attn_gain")[:, 4 * b:4 * b + 4].unsqueeze(2).to_broadcast([P, 4, P])
                        dve.tensor_tensor(hT[:, 4 * b:4 * b + 4, n * P:(n + 1) * P],
                                          PS[:, bank, :].rearrange("p (k t) -> p k t", k=4), g, ALU.mult).then_inc(hT_ready, 1)

            @block.tensor
            def _(pe):
                def values(n):
                    if n == 0:
                        chunk_ready(pe, CH_VF)
                    pe.wait_ge(hT_ready, 2 * n + 2)
                    if n >= 2:
                        pe.wait_ge(vf_ready, n - 1)
                    project_tile(pe, CH_VF, n, 4 + n % 2, W_VF).then_inc(vf_proj, 1)

                pe.wait_ge(const_loaded, 48)
                for n in range(NT):
                    pe.wait_ge(h_ready, n + 1)
                    for b in range(2):
                        if n >= 2:
                            pe.wait_ge(hT_ready, 2 * (n - 2) + b + 1)
                        for k in range(4):
                            kk = 4 * b + k
                            t = pe.transpose(PS[:, 2 * (n % 2) + b, k * P:(k + 1) * P],
                                             xin[:, n % NX, kk * P:(kk + 1) * P], ident)
                        t.then_inc(h_turned, 1)
                    if n >= 1:
                        values(n - 1)
                values(NT - 1)
                pe.wait_ge(vf_proj, NT)
                pe.nop().then_inc(w_used, 1)

        with ExitStack() as fc:
            qT = sb("qT", [KR, H_FOX, S], c=fc)
            kT = sb("kT", [KR, H_FOX, S], c=fc)
            with ExitStack() as c, nc.Block() as block:
                new_phase(c)
                fx = sb("fx", [P, NT, H_FOX], c=c)
                fmin = sb("fmin", [P, NT, H_FOX], c=c)
                fexp = sb("fexp", [P, NT, H_FOX], c=c)
                carry = sb("carry", [P, NT, H_FOX], c=c)
                neg_cum = sb("neg_cum", [P, NT, H_FOX], c=c)
                sq = sb("sq", [P, 2, FOX], c=c)
                qn = sb("qn", [P, 2, H_FOX, KR], c=c)
                ss = sb("ss", [P, 2, H_FOX], c=c)
                lns = sb("lns", [P, 2, H_FOX], c=c)
                rq = sb("rq", [P, 2, H_FOX], c=c)
                proj_ready, sq_ready, ss_ready = sem("fproj"), sem("fsq"), sem("fss")
                r_ready, qn_ready, qn_turned, qT_ready = sem("fr"), sem("fqn"), sem("fqnt"), sem("fqT")
                fx_ready, lf_act, lf_ready, cs_ready = sem("ffx"), sem("lf_act"), sem("lf_ready"), sem("cs_ready")
                dstep, astep = sem("f_dve_step"), sem("f_act_step")
                UNITS = [(c_, n) for c_ in (CH_Q, CH_K) for n in range(NT)]

                @block.sync
                def _(sp):
                    for k in range(3, 6):
                        load_chunk(sp, k)

                @block.tensor
                def _(pe):
                    def turn(u):
                        pe.wait_ge(qn_ready, u + 1)
                        for b in range(2):
                            if u >= 1:
                                pe.wait_ge(qT_ready, 2 * (u - 1) + b + 1)
                            for j in range(3):
                                t = pe.transpose(PS[0:KR, 4 + b, j * P:(j + 1) * P], qn[:, u % 2, 3 * b + j, :], ident)
                            t.then_inc(qn_turned, 1)

                    for u, (ch, n) in enumerate(UNITS):
                        if n == 0:
                            chunk_ready(pe, ch)
                        if u >= 2:
                            pe.wait_ge(qn_ready, u - 1)
                        mm = project_tile(pe, ch, n, u % 2, FOX)
                        mm.then_inc(proj_ready, 1)
                        if n == NT - 1:
                            pe.wait_ge(proj_ready, u + 1)
                            pe.nop().then_inc(w_used, 1)
                        if u == 1:
                            pe.wait_ge(lf_ready, 1)
                            lf = fx[:, :, :].rearrange("p n h -> p (n h)")
                            pe.matmul(PS[:, 6, 0:NT * H_FOX], U, lf, start=True, stop=True)
                            pe.matmul(PS[:, 7, 0:NT * H_FOX], ones, lf, start=True, stop=True).then_inc(cs_ready, 1)
                        if u >= 1:
                            turn(u - 1)
                    turn(len(UNITS) - 1)

                @block.scalar
                def _(act):
                    st = Steps(act, astep)
                    act.wait_ge(fx_ready, 1)
                    st.done(act.activation(fexp[:, :, :], fx[:, :, :], ACT.Abs))
                    st.done(act.activation(fexp[:, :, :], fexp[:, :, :], ACT.Exp, scale=-1.0))
                    act.activation(fexp[:, :, :], fexp[:, :, :], ACT.Ln, bias=1.0).then_inc(lf_act, 1)

                    def evac(u):
                        ch, n = UNITS[u]
                        dst = qT if ch == CH_Q else kT
                        for b in range(2):
                            act.wait_ge(qn_turned, 2 * u + b + 1)
                            act.activation(dst[:, 3 * b:3 * b + 3, n * P:(n + 1) * P],
                                           PS[0:KR, 4 + b, 0:3 * P].rearrange("p (h t) -> p h t", h=3),
                                           ACT.Copy).then_inc(qT_ready, 1)

                    for u, (ch, n) in enumerate(UNITS):
                        i = u % 2
                        act.wait_ge(proj_ready, u + 1)
                        if u >= 2:
                            act.wait_ge(ss_ready, u - 1)
                        act.activation(sq[:, i, :], PS[:, i, 0:FOX], ACT.Square).then_inc(sq_ready, 1)
                        act.wait_ge(ss_ready, u + 1)
                        q_unit = ch == CH_Q
                        st.done(act.activation(lns[:, i, :], ss[:, i, :], ACT.Ln, bias=eps_hd[:, :] if q_unit else eps[:, :],
                                               scale=1.0 if q_unit else 1.0 / HD))
                        if u >= 2:
                            act.wait_ge(qn_ready, u - 1)
                        act.activation(rq[:, i, :], lns[:, i, :], ACT.Exp, scale=-0.5).then_inc(r_ready, 1)
                        if u >= 1:
                            evac(u - 1)
                    evac(len(UNITS) - 1)

                @block.vector
                def _(dve):
                    st = Steps(dve, dstep)
                    st.done(dve.memset(qn[:, :, :, :], 0.0))
                    st.done(dve.memset(qn[:, :, :, HD:HD + 1], 1.0))
                    fb = par("f_bias").unsqueeze(1).to_broadcast([P, NT, H_FOX])
                    dve.tensor_tensor(fx[:, :, :], vf[:, :, FOX:W_VF], fb, ALU.add).then_inc(fx_ready, 1)
                    dve.wait_ge(fx_ready, 1)
                    st.done(dve.tensor_scalar(fmin[:, :, :], fx[:, :, :], 0.0, None, ALU.min))
                    dve.wait_ge(lf_act, 1)
                    dve.tensor_tensor(fx[:, :, :], fmin[:, :, :], fexp[:, :, :], ALU.subtract).then_inc(lf_ready, 1)

                    def cumulate():
                        dve.wait_ge(cs_ready, 1)
                        st.done(dve.memset(carry[:, 0, :], 0.0))
                        tot = PS[:, 7, 0:NT * H_FOX].rearrange("p (n h) -> p n h", h=H_FOX)
                        for n in range(1, NT):
                            st.done(dve.tensor_tensor(carry[:, n, :], carry[:, n - 1, :], tot[:, n - 1, :], ALU.add))
                        st.done(dve.tensor_tensor(neg_cum[:, :, :], carry[:, :, :],
                                                  PS[:, 6, 0:NT * H_FOX].rearrange("p (n h) -> p n h", h=H_FOX), ALU.add))
                        st.done(dve.tensor_scalar(neg_cum[:, :, :], neg_cum[:, :, :], -1.0, None, ALU.mult))

                    for u, (ch, n) in enumerate(UNITS):
                        i = u % 2
                        dve.wait_ge(sq_ready, u + 1)
                        dve.tensor_reduce(ss[:, i, :], sq[:, i, :].rearrange("p (h d) -> p h d", h=H_FOX), AX.X,
                                          ALU.add).then_inc(ss_ready, 1)
                        if u == 1:
                            cumulate()
                        dve.wait_ge(r_ready, u + 1)
                        if u >= 2:
                            dve.wait_ge(qn_turned, 2 * (u - 1))
                        rows = qn[:, i, :, 0:HD]
                        st.done(dve.tensor_tensor(rows, PS[:, i, 0:FOX].rearrange("p (h d) -> p h d", h=H_FOX),
                                                  rq[:, i, :].unsqueeze(2).to_broadcast([P, H_FOX, HD]), ALU.mult))
                        if ch == CH_K:
                            st.done(dve.tensor_copy(qn[:, i, :, HD], neg_cum[:, n, :]))
                        g = par("fox_q" if ch == CH_Q else "fox_k").unsqueeze(1).to_broadcast([P, H_FOX, HD])
                        dve.tensor_tensor(rows, rows, g, ALU.mult).then_inc(qn_ready, 1)

            with ExitStack() as c, nc.Block() as block:
                new_phase(c)
                pr = sb("pr", [P, 2, S], c=c)
                prT = sb("prT", [P, 2, NT, P], c=c)
                mx = sb("mx", [P, 2], c=c)
                den = sb("den", [P, 4], c=c)
                rden = sb("rden", [P, 2], c=c)
                sq = sb("sq2", [P, FOX], c=c)
                ss = sb("ss2", [P, H_FOX], c=c)
                rr = sb("rr2", [P, H_FOX], c=c)
                logits, mx_ready, p_ready = sem("logits"), sem("mx_ready"), sem("p_ready")
                p_turned, pT_ready, pv_ready, o_ready = sem("p_turned"), sem("pT_ready"), sem("pv_ready"), sem("o_ready")
                osq_ready, oss_ready, orr_ready, on_ready = sem("osq"), sem("oss"), sem("orr"), sem("on")
                dstep, astep = sem("a_dve_step"), sem("a_act_step")
                ATT = [(n, h) for n in range(NT) for h in range(H_FOX)]
                GR = [(u, g) for u, (n, h) in enumerate(ATT) for g in range((n + 4) // 4)]
                G0 = [sum(1 for x_ in GR if x_[0] < u) for u in range(len(ATT) + 1)]

                @block.sync
                def _(sp):
                    pass

                @block.tensor
                def _(pe):
                    def qk(u):
                        n, h = ATT[u]
                        i = u % 2
                        if u >= 2:
                            pe.wait_ge(p_ready, u - 1)
                        keys = (n + 1) * P
                        for a in range(0, keys, 512):
                            w = min(512, keys - a)
                            last = a + w == keys
                            mm = pe.matmul(PS[:, 2 * i + a // 512, 0:w], qT[:, h, n * P:(n + 1) * P], kT[:, h, a:a + w],
                                           start=True, stop=not last)
                        pe.matmul(PS[:, 2 * i + (keys - 1) // 512, w - P:w], identb, mask_q, start=False, stop=True)\
                          .then_inc(logits, 1)

                    def turn(u):
                        n, h = ATT[u]
                        i = u % 2
                        pe.wait_ge(p_ready, u + 1)
                        for g in range((n + 4) // 4):
                            G = G0[u] + g
                            if G >= 2:
                                pe.wait_ge(pT_ready, G - 1)
                            k0, k1 = 4 * g, min(4 * g + 4, n + 1)
                            for k in range(k0, k1):
                                t = pe.transpose(PS[:, 4 + G % 2, (k - k0) * P:(k - k0 + 1) * P], pr[:, i, k * P:(k + 1) * P], ident)
                            t.then_inc(p_turned, 1)

                    def pv(u):
                        n, h = ATT[u]
                        i = u % 2
                        if u >= 2:
                            pe.wait_ge(o_ready, u - 1)
                        for g in range((n + 4) // 4):
                            pe.wait_ge(pT_ready, G0[u] + g + 1)
                            for k in range(4 * g, min(4 * g + 4, n + 1)):
                                mm = pe.matmul(PS[:, 6 + i, 0:HD], prT[:, i, k, :], vf[:, k, h * HD:(h + 1) * HD],
                                               start=(k == 0), stop=(k == n))
                        mm.then_inc(pv_ready, 1)

                    for u in range(len(ATT) + 2):
                        if u < len(ATT):
                            qk(u)
                        if 1 <= u <= len(ATT):
                            turn(u - 1)
                        if u >= 2:
                            pv(u - 2)

                def norm_act(act, st, n):
                    act.wait_ge(o_ready, H_FOX * (n + 1))
                    if n >= 1:
                        act.wait_ge(on_ready, n)
                    act.activation(sq[:, :], mix[:, n, 0:FOX], ACT.Square).then_inc(osq_ready, 1)
                    act.wait_ge(oss_ready, n + 1)
                    st.done(act.activation(rr[:, :], ss[:, :], ACT.Ln, bias=eps[:, :], scale=1.0 / HD))
                    act.activation(rr[:, :], rr[:, :], ACT.Exp, scale=-0.5).then_inc(orr_ready, 1)

                @block.scalar
                def _(act):
                    st = Steps(act, astep)

                    def copy_turned(u):
                        n, i = ATT[u][0], u % 2
                        if u >= 2:
                            act.wait_ge(pv_ready, u - 1)
                        for g in range((n + 4) // 4):
                            G = G0[u] + g
                            k0, k1 = 4 * g, min(4 * g + 4, n + 1)
                            act.wait_ge(p_turned, G + 1)
                            act.activation(prT[:, i, k0:k1, :].rearrange("p k q -> p (k q)"), PS[:, 4 + G % 2, 0:(k1 - k0) * P],
                                           ACT.Copy).then_inc(pT_ready, 1)

                    for u, (n, h) in enumerate(ATT):
                        i = u % 2
                        keys = (n + 1) * P
                        act.wait_ge(mx_ready, u + 1)
                        if u >= 2:
                            act.wait_ge(p_turned, G0[u - 1])
                        if u >= 4:
                            act.wait_ge(o_ready, u - 3)
                        lg = PS[:, 2 * i:2 * i + 2, :].rearrange("p b k -> p (b k)")[:, 0:keys]
                        act.activation(pr[:, i, 0:keys], lg, ACT.Exp, bias=mx[:, i:i + 1],
                                       accum_out=den[:, u % 4:u % 4 + 1]).then_inc(p_ready, 1)
                        if u >= 1:
                            copy_turned(u - 1)
                        if h == 2 and n >= 1:
                            norm_act(act, st, n - 1)
                    copy_turned(len(ATT) - 1)
                    norm_act(act, st, NT - 1)

                @block.vector
                def _(dve):
                    st = Steps(dve, dstep)

                    def norm(n):
                        dve.wait_ge(osq_ready, n + 1)
                        dve.tensor_reduce(ss[:, :], sq[:, :].rearrange("p (h d) -> p h d", h=H_FOX), AX.X, ALU.add)\
                           .then_inc(oss_ready, 1)
                        dve.wait_ge(orr_ready, n + 1)
                        o = mix[:, n, 0:FOX].rearrange("p (h d) -> p h d", h=H_FOX)
                        st.done(dve.tensor_tensor(o, o, rr[:, :].unsqueeze(2).to_broadcast([P, H_FOX, HD]), ALU.mult))
                        dve.tensor_tensor(o, o, par("fox_o").unsqueeze(1).to_broadcast([P, H_FOX, HD]), ALU.mult)\
                           .then_inc(on_ready, 1)

                    def finish(u):
                        n, h = ATT[u]
                        i = u % 2
                        dve.wait_ge(pv_ready, u + 1)
                        st.done(dve.reciprocal(rden[:, i:i + 1], den[:, u % 4:u % 4 + 1]))
                        dve.tensor_scalar(mix[:, n, h * HD:(h + 1) * HD], PS[:, 6 + i, 0:HD], rden[:, i:i + 1], None,
                                          ALU.mult).then_inc(o_ready, 1)

                    for u, (n, h) in enumerate(ATT):
                        i = u % 2
                        keys = (n + 1) * P
                        dve.wait_ge(logits, u + 1)
                        if u >= 2:
                            dve.wait_ge(p_ready, u - 1)
                        lg = PS[:, 2 * i:2 * i + 2, :].rearrange("p b k -> p (b k)")[:, 0:keys]
                        dve.tensor_reduce(mx[:, i:i + 1], lg, AX.X, ALU.max, negate=True).then_inc(mx_ready, 1)
                        if u >= 2:
                            finish(u - 2)
                        if h == 2 and n >= 1:
                            norm(n - 1)
                    finish(len(ATT) - 2)
                    finish(len(ATT) - 1)
                    norm(NT - 1)
        fox.close()
        with ExitStack() as gc:
            qkvT = sb("qkvT", [P, 9, S], c=gc)
            sgate = mix[:, :, FOX:FOX + GDN]
            N6 = [P, NT, H_GDN]
            g_ = sb("g_log", N6, c=gc)
            row_a, row_q = sb("row_a", N6, c=gc), sb("row_q", N6, c=gc)
            bias_j = sb("bias_j", N6, c=gc)
            beta, s_w, s_kd, s_q = (sb(n_, N6, c=gc) for n_ in ("beta", "s_w", "s_kd", "s_q"))
            e_last = sb("e_last", [P, NT, H_GDN // 2], c=gc)
            with ExitStack() as c, nc.Block() as block:
                new_phase(c)
                raw = sb("raw", [P, 2, S + 3], c=c)
                conv = sb("conv", [P, 2, S], c=c)
                sqT = sb("sqT", [P, 2, S], c=c)
                ssT = sb("ssT", [2 * H_GDN, S], c=c)
                ab = sb("ab", [P, NT, 2 * H_GDN], c=c)
                lnr = sb("lnr", [P, NT, 2 * H_GDN], c=c)
                t1, t2, t3 = (sb(n_, [P, NT, 2 * H_GDN], c=c) for n_ in ("t1", "t2", "t3"))
                ealog = sb("ealog", [P, H_GDN], c=c)
                projT, raw_ready, conv_ready, silu_ready = sem("projT"), sem("raw_ready"), sem("conv_ready"), sem("silu_ready")
                sqT_ready, sumsq_ready, gate_proj, gate_ready = sem("sqT_ready"), sem("sumsq"), sem("gate_proj"), sem("gate_ready")
                sc_dve, sc_act, sc_pe = sem("sc_dve"), sem("sc_act"), sem("sc_pe")
                ssT_ready, ss_turned = sem("ssT_ready"), sem("ss_turned")
                dstep, astep, pads = sem("g_dve_step"), sem("g_act_step"), sem("pads")

                @block.sync
                def _(sp):
                    for k in range(6, 9):
                        load_chunk(sp, k)

                @block.tensor
                def _(pe):
                    def running_sums():
                        pe.wait_ge(sc_dve, 2)
                        for j, m in enumerate((U, L, ones)):
                            mm = pe.matmul(PS[:, 7, 48 * j:48 * j + 48], m, g_[:, :, :].rearrange("p n h -> p (n h)"), start=True, stop=True)
                        mm.then_inc(sc_pe, 1)

                    def sumsq(g):
                        pe.wait_ge(sqT_ready, g + 1)
                        at = K_PAIR - 2 * g
                        for b in range(2):
                            mm = pe.matmul(PS[0:2 * H_GDN, 4 + b, :], kc[:, K_HO, at:at + 2 * H_GDN], sqT[:, g % 2, 512 * b:512 * b + 512],
                                           start=(g == 0), stop=(g == 5))
                        mm.then_inc(sumsq_ready, 1)

                    def turn_sums():
                        pe.wait_ge(ssT_ready, 1)
                        for n in range(NT):
                            mm = pe.transpose(PS[:, 6, n * 12:(n + 1) * 12], ssT[:, n * P:(n + 1) * P], ident[0:12, 0:12])
                        mm.then_inc(ss_turned, 1)

                    chunk_ready(pe, CH_GAB)
                    for n in range(NT):
                        if n >= 2:
                            pe.wait_ge(gate_ready, n - 1)
                        project_tile(pe, CH_GAB, n, 4 + n % 2, W_GAB).then_inc(gate_proj, 1)
                    pe.wait_ge(gate_proj, NT)
                    pe.nop().then_inc(w_used, 1)
                    for g in range(9):
                        ch = CH_T0 + g // 4
                        if g % 4 == 0:
                            chunk_ready(pe, ch)
                        for b in range(2):
                            if g >= 2:
                                pe.wait_ge(raw_ready, 2 * (g - 2) + b + 1)
                            for k in range(KD):
                                mm = pe.matmul(PS[:, 2 * (g % 2) + b, :], wring[ch % 3][:, k, (g % 4) * P:(g % 4 + 1) * P],
                                               hT[:, k, 512 * b:512 * b + 512], start=(k == 0), stop=(k == KD - 1))
                            mm.then_inc(projT, 1)
                        if g % 4 == 3 or g == 8:
                            pe.wait_ge(projT, 2 * g + 2)
                            pe.nop().then_inc(w_used, 1)
                        if g == 1:
                            pe.wait_ge(gate_ready, NT)
                        if 2 <= g <= 7:
                            sumsq(g - 2)
                        if g == 6:
                            running_sums()
                    turn_sums()

                @block.scalar
                def _(act):
                    st = Steps(act, astep)

                    def silu(g):
                        act.wait_ge(conv_ready, g + 1)
                        act.activation(qkvT[:, g, :], conv[:, g % 2, :], ACT.Silu).then_inc(silu_ready, 1)
                        if g < 6:
                            act.wait_ge(silu_ready, g + 1)
                            if g >= 2:
                                act.wait_ge(sumsq_ready, g - 1)
                            act.activation(sqT[:, g % 2, :], qkvT[:, g, :], ACT.Square).then_inc(sqT_ready, 1)

                    act.preload_act_table_set("silu_and_others")
                    for n in range(NT):
                        act.wait_ge(gate_proj, n + 1)
                        st.done(act.activation(sgate[:, n, :], PS[:, 4 + n % 2, 0:GDN], ACT.Silu))
                        act.activation(ab[:, n, :], PS[:, 4 + n % 2, GDN:W_GAB], ACT.Copy).then_inc(gate_ready, 1)
                    act.wait_ge(sc_dve, 1)
                    act.preload_act_table_set("natural_log_exp_and_others")
                    st.done(act.activation(t2[:, :, :], t1[:, :, :], ACT.Abs))
                    st.done(act.activation(t2[:, :, :], t2[:, :, :], ACT.Exp, scale=-1.0))
                    st.done(act.activation(t2[:, :, :], t2[:, :, :], ACT.Ln, bias=1.0))
                    act.activation(ealog[:, :], par("a_log"), ACT.Exp).then_inc(sc_act, 1)
                    act.preload_act_table_set("silu_and_others")
                    act.wait_ge(pads, 1)
                    for g in range(9):
                        for b in range(2):
                            act.wait_ge(projT, 2 * g + b + 1)
                            if g >= 2:
                                act.wait_ge(conv_ready, g - 1)
                            act.activation(raw[:, g % 2, 3 + 512 * b:515 + 512 * b], PS[:, 2 * (g % 2) + b, :], ACT.Copy)\
                               .then_inc(raw_ready, 1)
                        if g >= 1:
                            silu(g - 1)
                    act.wait_ge(sumsq_ready, 6)
                    act.activation(ssT[:, :].rearrange("p (b t) -> p b t", b=2), PS[0:2 * H_GDN, 4:6, :], ACT.Copy).then_inc(ssT_ready, 1)
                    silu(8)
                    act.preload_act_table_set("natural_log_exp_and_others")
                    act.wait_ge(ss_turned, 1)
                    act.activation(lnr[:, :, :], PS[:, 6, 0:96].rearrange("p (n h) -> p n h", n=NT), ACT.Ln, bias=eps[:, :]).then_inc(sc_act, 1)
                    act.wait_ge(sc_dve, 3)
                    for t, src in ((beta, beta), (s_w, row_a), (s_kd, s_kd), (s_q, row_q)):
                        st.done(act.activation(t[:, :, :], src[:, :, :], ACT.Exp))
                    for h in range(2):
                        tot = PS[64 * h:64 * h + 64, 7, 96:144].rearrange("p (n a s) -> p n a s", n=NT, s=2)[:, :, :, h]
                        st.done(act.activation(e_last[64 * h:64 * h + 64, :, :], tot, ACT.Exp))

                @block.vector
                def _(dve):
                    st = Steps(dve, dstep)
                    dve.memset(raw[:, :, 0:3], 0.0).then_inc(pads, 1)
                    dve.wait_ge(gate_ready, NT)
                    a, b = ab[:, :, 0:H_GDN], ab[:, :, H_GDN:12]
                    dt = par("dt_bias").unsqueeze(1).to_broadcast([P, NT, H_GDN])
                    st.done(dve.tensor_tensor(t1[:, :, 0:H_GDN], a, dt, ALU.add))
                    dve.tensor_copy(t1[:, :, H_GDN:12], b).then_inc(sc_dve, 1)
                    dve.wait_ge(sc_dve, 1)
                    st.done(dve.tensor_scalar(t3[:, :, 0:H_GDN], t1[:, :, 0:H_GDN], 0.0, None, ALU.max))
                    st.done(dve.tensor_scalar(t3[:, :, H_GDN:12], t1[:, :, H_GDN:12], 0.0, None, ALU.min))
                    dve.wait_ge(sc_act, 1)
                    st.done(dve.tensor_tensor(t3[:, :, 0:H_GDN], t3[:, :, 0:H_GDN], t2[:, :, 0:H_GDN], ALU.add))
                    st.done(dve.tensor_tensor(t3[:, :, H_GDN:12], t3[:, :, H_GDN:12], t2[:, :, H_GDN:12], ALU.subtract))
                    st.done(dve.tensor_scalar(ealog[:, :], ealog[:, :], -1.0, None, ALU.mult))
                    dve.tensor_tensor(g_[:, :, :], t3[:, :, 0:H_GDN],
                                      ealog[:, :].unsqueeze(1).to_broadcast([P, NT, H_GDN]), ALU.mult).then_inc(sc_dve, 1)
                    go = par("gdn_o").unsqueeze(1).to_broadcast([P, H_GDN, HD])
                    for n in range(NT):
                        sg = sgate[:, n, :].rearrange("p (h d) -> p h d", d=HD)
                        st.done(dve.tensor_tensor(sg, sg, go, ALU.mult))
                    w = par("conv").rearrange("p (g j) -> p g j", j=4)
                    dve.wait_ge(pads, 1)
                    for g in range(9):
                        dve.wait_ge(raw_ready, 2 * g + 2)
                        if g >= 2:
                            dve.wait_ge(silu_ready, g - 1)
                        y = conv[:, g % 2, :]
                        st.done(dve.tensor_scalar(y, raw[:, g % 2, 0:S], w[:, g, 0:1], None, ALU.mult))
                        for j in range(1, 4):
                            i = dve.scalar_tensor_tensor(out=y, in0=raw[:, g % 2, j:j + S], scalar=w[:, g, j:j + 1], in1=y,
                                                         op0=ALU.mult, op1=ALU.add)
                            st.done(i) if j < 3 else i.then_inc(conv_ready, 1)
                    lb = t3[:, :, H_GDN:12]
                    dve.wait_ge(sc_act, 2)
                    st.done(dve.tensor_scalar(row_q[:, :, :], lnr[:, :, 0:6], -0.5, -0.5 * math.log(HD), ALU.mult, ALU.add))
                    st.done(dve.tensor_scalar(t2[:, :, 0:6], lnr[:, :, 6:12], -0.5, None, ALU.mult))
                    lnrk = t2[:, :, 0:6]
                    st.done(dve.tensor_tensor(row_a[:, :, :], lb, lnrk, ALU.add))
                    dve.wait_ge(sc_pe, 1)
                    d, dl = (PS[:, 7, 48 * j:48 * j + 48].rearrange("p (n h) -> p n h", n=NT) for j in range(2))
                    st.done(dve.tensor_copy(beta[:, :, :], lb))
                    st.done(dve.tensor_tensor(bias_j[:, :, :], lnrk, d, ALU.subtract))
                    st.done(dve.tensor_tensor(row_a[:, :, :], row_a[:, :, :], d, ALU.add))
                    st.done(dve.tensor_tensor(s_kd[:, :, :], lnrk, dl, ALU.add))
                    dve.tensor_tensor(row_q[:, :, :], row_q[:, :, :], d, ALU.add).then_inc(sc_dve, 1)

            with ExitStack() as c, nc.Block() as block:
                new_phase(c)
                LV = 7
                TL = 2 * (LV - 1)
                kn, vn = sb("kn", [P, GDN], c=c), sb("vn", [P, GDN], c=c)
                rwv = sb("rwv", [P, 2, H_GDN, 2, HD], c=c)
                kd = sb("kd", [P, 2, GDN], c=c)
                free = wring[CH_T2 % 3][:, :, :].rearrange("p k n -> p (k n)")
                pads = free[:, 0:12 * P].rearrange("p (s g t) -> p s g t", s=2, g=6)
                diag = free[:, 12 * P:18 * P].rearrange("p (j a t) -> p j a t", j=2, a=3)
                wn = free[:, 18 * P:21 * P].rearrange("p (a s d) -> p a s d", a=3, s=2)
                wT = free[:, 21 * P:24 * P].rearrange("p (a t) -> p a t", a=3)
                vnew = free[:, 24 * P:27 * P].rearrange("p (a s d) -> p a s d", a=3, s=2)
                St = free[:, 27 * P:30 * P].rearrange("p (a s d) -> p a s d", a=3, s=2)
                AT, X, M, IT, Y = (sb(n_, [P, 2, 2, 3, P], c=c) for n_ in ("AT", "X", "M", "IT", "Y"))
                T1 = sb("T1", [P, 2, 3, P], c=c)
                oss, orr = sb("oss", [P, H_GDN], c=c), sb("orr", [P, H_GDN], c=c)
                kv_turned, kv_ready, sc_ready, pads_ready, diag_ready = (sem(n_) for n_ in (
                    "kv_turned", "kv_ready", "sc_ready", "pads_ready", "diag_ready"))
                dbc, gam_ready, kk, AT_ready = sem("dbc"), sem("gam_ready"), sem("kk"), sem("AT_ready")
                M_ready, M0_turned, X0_ready, Y0_ready = sem("M_ready"), sem("M0_turned"), sem("X0_ready"), sem("Y0_ready")
                X_ready, Y_ready, T1_mm, T1_ready, D_mm, YT_mm = (sem(n_) for n_ in (
                    "X_ready", "Y_ready", "T1_mm", "T1_ready", "D_mm", "YT_mm"))
                wu_mm, wn_ready, w_turned, wT_ready, v_mm, v_ready, o_mm, o_ready, S_ready = (sem(n_) for n_ in (
                    "wu_mm", "wn_ready", "w_turned", "wT_ready", "v_mm", "v_ready", "o_mm", "go_ready", "S_ready"))
                os_act, oss_rdy, orr_rdy, on_ready = (sem(n_) for n_ in ("os_act", "oss_rdy", "orr_rdy", "gon_ready"))
                dstep, astep = sem("h_dve_step"), sem("h_act_step")
                B_WU, B_Q, B_WS, B_OI, B_UPD, B_YT = (2, 3), 4, 5, 2, 3, (6, 7)

                def slots(ap, s):
                    return ap.rearrange("p (a s) -> p s a", s=2)[:, s, :]

                def by_head(ap):
                    return ap.rearrange("p (a s) -> p a s", s=2).unsqueeze(3).to_broadcast([P, 3, 2, HD])

                def bank3(b, w=P):
                    return PS[:, b, 0:3 * w].rearrange("p (a t) -> p a t", a=3)

                def lv(n, l, s):
                    return TL * n + 2 * (l - 1) + s + 1

                def out_and_square(n):
                    return qkvT[:, 3:6, n * P:(n + 1) * P], qkvT[:, 6:9, n * P:(n + 1) * P]

                def last_level(n, l):
                    return (n, l - 1) if l > 1 else (n - 1, LV - 1)

                @block.tensor
                def _(pe):
                    def natural_kv(n):
                        for j in range(2):
                            if n >= 1:
                                pe.wait_ge(Y_ready, lv(n - 1, 2, j))
                            for a in range(3):
                                mm = pe.transpose(PS[:, B_YT[j], a * P:(a + 1) * P], qkvT[:, 3 + 3 * j + a, n * P:(n + 1) * P], ident)
                            mm.then_inc(kv_turned, 1)

                    def decays(n, s):
                        pe.wait_ge(diag_ready, 4 * n + 2 * s + 2)
                        for j, (b, mask) in enumerate(((5, mask_strict), (4, mask_incl))):
                            if s == 1:
                                pe.wait_ge(gam_ready, 4 * n + j + 1)
                            elif j == 1 and n >= 2:
                                pe.wait_ge(o_ready, n - 1)
                            o = bank3(b)
                            pe.matmul(o, ones, diag[:, j, :, :], start=True, stop=False)
                            pe.matmul(o, identb, mask.unsqueeze(1).to_broadcast([P, 3, P]), start=False, stop=True).then_inc(dbc, 1)
                        pe.wait_ge(pads_ready, 2 * n + s + 1)
                        for j, b in enumerate((B_OI, B_UPD)):
                            if s == 1:
                                pe.wait_ge(AT_ready, 4 * n + j + 1)
                            elif j == 1 and n >= 2:
                                pe.wait_ge(S_ready, n)
                            for a in range(3):
                                mm = pe.matmul(PS[:, b, a * P:(a + 1) * P], qkvT[:, 3 + a, n * P:(n + 1) * P],
                                               pads[:, s, 3 * (1 - j) + a, :], start=True, stop=True)
                            mm.then_inc(kk, 1)

                    def turn_M0(n):
                        for s in range(2):
                            pe.wait_ge(M_ready, 2 * LV * n + s + 1)
                            pe.wait_ge(AT_ready, 4 * n + 4)
                            for a in range(3):
                                mm = pe.transpose(PS[:, 2 + s, a * P:(a + 1) * P], M[:, (LV * n) % 2, s, a, :], ident)
                            mm.then_inc(M0_turned, 1)

                    def turn_X(n, l):
                        for s in range(2):
                            pe.wait_ge(X_ready, lv(n, l, s))
                            if (n, l) > (0, 1):
                                pe.wait_ge(Y_ready, lv(*last_level(n, l), s))
                            if l == 3 and n + 1 < NT:
                                pe.wait_ge(kv_ready, 2 * (n + 1) + s + 1)
                            for a in range(3):
                                mm = pe.transpose(PS[:, B_YT[s], a * P:(a + 1) * P], X[:, n % 2, s, a, :], ident)
                            mm.then_inc(YT_mm, 1)

                    def scan(n, part):
                        t, i = slice(n * P, (n + 1) * P), n % 2
                        if part == 0:
                            pe.wait_ge(sc_ready, 3 * n + 3)
                            for s in range(2):
                                pe.wait_ge(Y_ready, lv(n, LV - 1, s))
                                pe.wait_ge(X0_ready, 2 * min(n + 1, NT - 1) + s + 1)
                                for a in range(3):
                                    mm = pe.matmul(PS[:, B_WU[s], a * P:(a + 1) * P], Y[:, i, s, a, :],
                                                   rwv[:, i, 2 * a + s, :, :].rearrange("p j d -> p (j d)"), start=True, stop=True)
                                mm.then_inc(wu_mm, 1)
                        if part == 1:
                            pe.wait_ge(wn_ready, 2 * n + 2)
                            for a in range(3):
                                mm = pe.transpose(PS[:, B_Q, a * P:(a + 1) * P], wn[:, a, :, :].rearrange("p s d -> p (s d)"), ident)
                            mm.then_inc(w_turned, 1)
                        if part == 2:
                            pe.wait_ge(wT_ready, n + 1)
                            pe.wait_ge(S_ready, n + 1)
                            for a in range(3):
                                mm = pe.matmul(PS[:, B_WS, a * P:(a + 1) * P], wT[:, a, :], St[:, a, :, :].rearrange("p s d -> p (s d)"),
                                               start=True, stop=True)
                            mm.then_inc(v_mm, 1)
                            for a in range(3):
                                mm = pe.matmul(PS[:, B_Q, a * P:(a + 1) * P], qkvT[:, a, t], St[:, a, :, :].rearrange("p s d -> p (s d)"),
                                               start=True, stop=True)
                            mm.then_inc(o_mm, 1)
                        if part == 3:
                            pe.wait_ge(v_ready, 2 * n + 2)
                            for h in range(H_GDN):
                                mm = pe.matmul(PS[:, B_OI, h * HD:(h + 1) * HD], IT[:, i, h % 2, h // 2, :], vnew[:, h // 2, h % 2, :],
                                               start=True, stop=True)
                            mm.then_inc(o_mm, 1)
                            for h in range(H_GDN):
                                a, s = h // 2, h % 2
                                mm = pe.matmul(PS[64 * s:64 * s + 64, B_UPD, a * HD:(a + 1) * HD], kd[:, i, h * HD:(h + 1) * HD],
                                               vnew[:, a, s, :], start=True, stop=True)
                            mm.then_inc(o_mm, 1)

                    def between(n, l, second):
                        if n >= 1:
                            for part, at in enumerate(((1, 1), (2, 0), (2, 1), (3, 1))):
                                if at == (l, second):
                                    scan(n - 1, part)
                        if n + 1 < NT:
                            if (l, second) == (3, 0):
                                natural_kv(n + 1)
                            if (l, second) == (4, 0):
                                decays(n + 1, 0)
                            if (l, second) == (5, 0):
                                decays(n + 1, 1)
                            if (l, second) == (6, 0):
                                turn_M0(n + 1)

                    natural_kv(0)
                    decays(0, 0)
                    decays(0, 1)
                    turn_M0(0)
                    for n in range(NT):
                        for l in range(1, LV):
                            for s in range(2):
                                pe.wait_ge(M_ready, 2 * LV * n + 2 * l + s + 1)
                                pe.wait_ge(X0_ready, 2 * n + s + 1)
                                if (n, l) > (0, 1):
                                    pe.wait_ge(X_ready, lv(*last_level(n, l), s))
                                for a in range(3):
                                    mm = pe.matmul(PS[:, s, a * P:(a + 1) * P], M[:, (LV * n + l) % 2, s, a, :], X[:, n % 2, s, a, :],
                                                   start=True, stop=True)
                                mm.then_inc(T1_mm, 1)
                            if (n, l) > (0, 1):
                                turn_X(*last_level(n, l))
                            between(n, l, 0)
                            for s in range(2):
                                pe.wait_ge(T1_ready, lv(n, l, s))
                                if l == 1:
                                    pe.wait_ge(Y0_ready, 2 * n + s + 1)
                                else:
                                    pe.wait_ge(Y_ready, lv(n, l - 1, s))
                                for a in range(3):
                                    mm = pe.matmul(PS[:, s, a * P:(a + 1) * P], Y[:, n % 2, s, a, :], T1[:, s, a, :], start=True, stop=True)
                                mm.then_inc(D_mm, 1)
                            between(n, l, 1)
                    turn_X(NT - 1, LV - 1)
                    for part in range(4):
                        scan(NT - 1, part)

                @block.scalar
                def _(act):
                    st = Steps(act, astep)

                    def natural_kv(n):
                        for j, dst in enumerate((kn, vn)):
                            act.wait_ge(kv_turned, 2 * n + j + 1)
                            if n >= 1:
                                act.wait_ge(sc_ready, 3 * n)
                            act.activation(dst[:, :], PS[:, B_YT[j], 0:GDN], ACT.Copy).then_inc(kv_ready, 1)

                    def decays(n, s):
                        for j in range(2):
                            act.wait_ge(dbc, 4 * n + 2 * s + j + 1)
                            if n >= 2:
                                act.wait_ge(M_ready, 2 * LV * (n - 1)) if j == 0 else act.wait_ge(o_mm, 3 * (n - 1))
                            for a in range(3):
                                h = 2 * a + s
                                i = act.activation((IT if j else AT)[:, n % 2, s, a, :], PS[:, 5 - j, a * P:(a + 1) * P], ACT.Exp,
                                                   bias=bias_j[:, n, h:h + 1])
                            i.then_inc(gam_ready, 1)

                    def copy_Y(n, l):
                        for s in range(2):
                            act.wait_ge(YT_mm, lv(n, l, s))
                            act.wait_ge(D_mm, lv(n, l, s))
                            act.activation(Y[:, n % 2, s, :, :], bank3(B_YT[s]), ACT.Copy).then_inc(Y_ready, 1)

                    def scan(n, part):
                        if part == 0:
                            if n >= 1:
                                act.wait_ge(w_turned, n)
                            for s in range(2):
                                act.wait_ge(wu_mm, 2 * n + s + 1)
                                act.activation(wn[:, :, s, :], bank3(B_WU[s])[:, :, 0:HD], ACT.Copy, scale=-1.0).then_inc(wn_ready, 1)
                        if part == 1:
                            act.wait_ge(w_turned, n + 1)
                            if n >= 1:
                                act.wait_ge(v_mm, n)
                            act.activation(wT[:, :, :], bank3(B_Q), ACT.Copy).then_inc(wT_ready, 1)
                        if part == 2:
                            act.wait_ge(o_ready, n + 1)
                            ob, osq = out_and_square(n)
                            act.activation(osq, ob, ACT.Square).then_inc(os_act, 1)
                        if part == 3:
                            act.wait_ge(oss_rdy, n + 1)
                            st.done(act.activation(orr[:, :], oss[:, :], ACT.Ln, bias=eps[:, :], scale=1.0 / HD))
                            act.activation(orr[:, :], orr[:, :], ACT.Exp, scale=-0.5).then_inc(orr_rdy, 1)

                    natural_kv(0)
                    decays(0, 0)
                    decays(0, 1)
                    for n in range(NT):
                        for l in range(1, LV):
                            for s in range(2):
                                act.wait_ge(T1_mm, lv(n, l, s))
                                if (n, l) > (0, 1):
                                    act.wait_ge(D_mm, lv(*last_level(n, l), s))
                                act.activation(T1[:, s, :, :], bank3(s), ACT.Copy).then_inc(T1_ready, 1)
                            if (n, l) > (0, 1):
                                copy_Y(*last_level(n, l))
                            if l == 3 and n + 1 < NT:
                                natural_kv(n + 1)
                            if l in (4, 5) and n + 1 < NT:
                                decays(n + 1, l - 4)
                            if n >= 1 and l in (1, 2, 4, 5):
                                scan(n - 1, (1, 2, 4, 5).index(l))
                    copy_Y(NT - 1, LV - 1)
                    for part in range(4):
                        scan(NT - 1, part)

                @block.gpsimd
                def _(pool):
                    def diagonals(n, s):
                        if n >= 1 or s == 1:
                            pool.wait_ge(dbc, 4 * n + 2 * s)
                        for j, row in enumerate((row_a, row_q)):
                            pool.tensor_tensor(diag[:, j, :, :], ident.unsqueeze(1).to_broadcast([P, 3, P]),
                                               slots(row[:, n, :], s).unsqueeze(2).to_broadcast([P, 3, P]), ALU.mult).then_inc(diag_ready, 1)

                    def right_sides(n):
                        pool.wait_ge(kv_ready, 2 * n + 2)
                        if n >= 2:
                            pool.wait_ge(o_mm, 3 * (n - 1))
                        for dst, src, by in ((rwv[:, n % 2, :, 0, :], kn, s_w), (rwv[:, n % 2, :, 1, :], vn, beta),
                                             (kd[:, n % 2, :].rearrange("p (h d) -> p h d", d=HD), kn, s_kd)):
                            pool.tensor_tensor(dst, src[:, :].rearrange("p (h d) -> p h d", d=HD),
                                               by[:, n, :].unsqueeze(2).to_broadcast([P, H_GDN, HD]), ALU.mult).then_inc(sc_ready, 1)

                    def cut(n, l):
                        for s in range(2):
                            pool.wait_ge(AT_ready, 4 * n + 2 * s + 1)
                            if l >= 3 or (l < 2 and n >= 1):
                                pool.wait_ge(T1_mm, lv(n, l - 2, s) if l >= 3 else lv(n - 1, LV - 2 + l, s))
                            if l == 2:
                                pool.wait_ge(M0_turned, 2 * n + s + 1)
                                pool.wait_ge(Y0_ready, 2 * n + s + 1)
                            lm = kc[:, K_LM + l, :].unsqueeze(1).to_broadcast([P, 3, P])
                            pool.tensor_tensor(M[:, (LV * n + l) % 2, s, :, :], AT[:, n % 2, s, :, :], lm, ALU.mult).then_inc(M_ready, 1)

                    diagonals(0, 0)
                    diagonals(0, 1)
                    right_sides(0)
                    cut(0, 0)
                    cut(0, 1)
                    for n in range(NT):
                        for l in range(1, LV):
                            if l < LV - 1:
                                cut(n, l + 1)
                            if n + 1 == NT:
                                continue
                            if l in (3, 4):
                                diagonals(n + 1, l - 3)
                            if l == 4:
                                right_sides(n + 1)
                            if l == 5:
                                cut(n + 1, 0)
                            if l == 6:
                                cut(n + 1, 1)

                @block.vector
                def _(dve):
                    st = Steps(dve, dstep)
                    st.done(dve.memset(pads[:, :, :, :], 0.0))
                    dve.memset(St[:, :, :, :], 0.0).then_inc(S_ready, 1)
                    idb3 = ident.unsqueeze(1).to_broadcast([P, 3, P])

                    def padded(n):
                        if n >= 1:
                            dve.wait_ge(kk, 4 * n)
                        for s in range(2):
                            hs = slice(64 * s, 64 * s + 64)
                            dve.tensor_copy(pads[hs, s, :, :], qkvT[hs, 0:6, n * P:(n + 1) * P]).then_inc(pads_ready, 1)

                    def decays(n, s):
                        for j in range(2):
                            dve.wait_ge(gam_ready, 4 * n + 2 * s + j + 1)
                            dve.wait_ge(kk, 4 * n + 2 * s + j + 1)
                            it = (IT if j else AT)[:, n % 2, s, :, :]
                            dve.tensor_tensor(it, bank3(2 + j), it, ALU.mult).then_inc(AT_ready, 1)

                    def first_X(n):
                        for s in range(2):
                            dve.wait_ge(M0_turned, 2 * n + s + 1)
                            if n >= 2:
                                dve.wait_ge(YT_mm, lv(n - 2, LV - 1, s))
                            dve.tensor_tensor(X[:, n % 2, s, :, :], idb3, bank3(2 + s), ALU.subtract).then_inc(X0_ready, 1)

                    def first_Y(n):
                        for s in range(2):
                            if n >= 2:
                                dve.wait_ge(wu_mm, 2 * (n - 2) + s + 1)
                            dve.wait_ge(M_ready, 2 * LV * n + s + 1)
                            dve.tensor_tensor(Y[:, n % 2, s, :, :], idb3, M[:, (LV * n) % 2, s, :, :], ALU.subtract).then_inc(Y0_ready, 1)

                    def scan(n, part):
                        if part == 0:
                            dve.wait_ge(v_mm, n + 1)
                            dve.wait_ge(wn_ready, 2 * n + 2)
                            if n >= 1:
                                dve.wait_ge(o_mm, 3 * n)
                            ws = PS[:, B_WS, 0:GDN].rearrange("p (a s d) -> p s a d", s=2, d=HD)
                            for s in range(2):
                                st.done(dve.tensor_copy(vnew[:, :, s, :], bank3(B_WU[s])[:, :, HD:P]))
                                dve.tensor_tensor(vnew[:, :, s, :], vnew[:, :, s, :], ws[:, s, :, :], ALU.add).then_inc(v_ready, 1)
                        if part == 1:
                            dve.wait_ge(o_mm, 3 * n + 2)
                            if n >= 1:
                                dve.wait_ge(on_ready, n)
                            ob = out_and_square(n)[0]
                            o = ob.rearrange("p a (s d) -> p a s d", d=HD)
                            st.done(dve.tensor_tensor(o, PS[:, B_Q, 0:GDN].rearrange("p (a s d) -> p a s d", s=2, d=HD),
                                                      by_head(s_q[:, n, :]), ALU.mult))
                            dve.tensor_tensor(ob, ob, bank3(B_OI), ALU.add).then_inc(o_ready, 1)
                            dve.wait_ge(o_mm, 3 * n + 3)
                            dve.wait_ge(S_ready, n + 1)
                            St3 = St[:, :, :, :].rearrange("p a s d -> p a (s d)")
                            st.done(dve.tensor_tensor(St3, St3, e_last[:, n, :].unsqueeze(2).to_broadcast([P, 3, P]), ALU.mult))
                            for s in range(2):
                                hs = slice(64 * s, 64 * s + 64)
                                upd = PS[hs, B_UPD, 0:3 * HD].rearrange("p (a d) -> p a d", a=3)
                                i = dve.tensor_tensor(St[hs, :, s, :], St[hs, :, s, :], upd, ALU.add)
                                st.done(i) if s == 0 else i.then_inc(S_ready, 1)
                        if part == 2:
                            dve.wait_ge(os_act, n + 1)
                            dve.tensor_reduce(oss[:, :].rearrange("p (a s) -> p a s", s=2),
                                              out_and_square(n)[1].rearrange("p a (s d) -> p a s d", d=HD), AX.X, ALU.add).then_inc(oss_rdy, 1)
                        if part == 3:
                            dve.wait_ge(orr_rdy, n + 1)
                            ob = out_and_square(n)[0]
                            o = ob.rearrange("p a (s d) -> p a s d", d=HD)
                            st.done(dve.tensor_tensor(o, o, by_head(orr[:, :]), ALU.mult))
                            sg = sgate[:, n, :].rearrange("p (a t) -> p a t", a=3)
                            dve.tensor_tensor(sg, ob, sg, ALU.mult).then_inc(on_ready, 1)

                    padded(0)
                    decays(0, 0)
                    decays(0, 1)
                    first_X(0)
                    first_Y(0)
                    for n in range(NT):
                        for l in range(1, LV):
                            if l == LV - 1 and n + 1 < NT:
                                first_X(n + 1)
                            for s in range(2):
                                dve.wait_ge(D_mm, lv(n, l, s))
                                xl = X[:, n % 2, s, :, :].rearrange("p a (b u w) -> p (a b) u w", u=2, w=1 << l)[:, :, 0, :]
                                d = PS[:, s, 0:3 * P].rearrange("p (c u w) -> p c u w", u=2, w=1 << l)[:, :, 0, :]
                                dve.tensor_tensor(xl, xl, d, ALU.subtract).then_inc(X_ready, 1)
                            if n + 1 < NT:
                                if l == 1:
                                    padded(n + 1)
                                if l in (4, 5):
                                    decays(n + 1, l - 4)
                                if l == LV - 1:
                                    first_Y(n + 1)
                            if n >= 1 and 2 <= l <= 5:
                                scan(n - 1, l - 2)
                    for part in range(4):
                        scan(NT - 1, part)

        with ExitStack() as lc:
            vl = sb("vl", [P, NT, GV], c=lc)
            slr = sb("slr", [P, NT, GV], c=lc)
            qlT, klT, bT = (sb(n_, [P, S], c=lc) for n_ in ("qlT", "klT", "bT"))
            with ExitStack() as c, nc.Block() as block:
                new_phase(c)
                wa2 = sb("wa2", [RANK, GK], c=c)
                la1T = sb("la1T", [RANK, S], c=c)
                lx, le, lm_ = (sb(n_, [P, NT, GK], c=c) for n_ in ("lx", "le", "lmin"))
                wa2_loaded, lproj, l_ready, nproj, n_ready = (sem(n_) for n_ in ("wa2_loaded", "lproj", "l_ready", "nproj", "n_ready"))
                la_mm, lx_ready, ls_act, ls_ready, b_mm, b_ready = (sem(n_) for n_ in ("la_mm", "lx_ready", "ls_act", "ls_ready", "b_mm", "b_ready"))
                dstep, astep = sem("l_dve_step"), sem("l_act_step")

                @block.sync
                def _(sp):
                    sp.dma_start(wa2[:, :], w_a2).then_inc(wa2_loaded, 16)
                    load_chunk(sp, 9)
                    load_chunk(sp, 10)

                @block.tensor
                def _(pe):
                    chunk_ready(pe, CH_L)
                    for j, (a, w) in enumerate(((2 * GK, RANK), (0, GK), (GK, GK))):
                        for b in range(2):
                            if j == 2:
                                pe.wait_ge(l_ready, b + 1)
                            for k in range(KD):
                                mm = pe.matmul(PS[0:w, 2 * (j % 2) + b, :], wring[CH_L % 3][:, k, a:a + w],
                                               hT[:, k, 512 * b:512 * b + 512], start=(k == 0), stop=(k == KD - 1))
                            mm.then_inc(lproj, 1)
                    pe.wait_ge(lproj, 6)
                    pe.nop().then_inc(w_used, 1)
                    pe.wait_ge(wa2_loaded, 16)
                    pe.wait_ge(l_ready, 2)
                    for n in range(NT):
                        mm = pe.matmul(PS[:, 6 + n // 4, (n % 4) * P:(n % 4 + 1) * P], la1T[:, n * P:(n + 1) * P], wa2[:, :],
                                       start=True, stop=True)
                    mm.then_inc(la_mm, 1)
                    chunk_ready(pe, CH_LVR)
                    for n in range(NT):
                        if n >= 2:
                            pe.wait_ge(n_ready, n - 1)
                        project_tile(pe, CH_LVR, n, 4 + n % 2, 512).then_inc(nproj, 1)
                    pe.wait_ge(nproj, NT)
                    pe.nop().then_inc(w_used, 1)
                    pe.wait_ge(ls_ready, 1)
                    for n in range(NT):
                        mm = pe.matmul(PS[:, 6 + n // 4, (n % 4) * P:(n % 4 + 1) * P], lx[:, n, :], U, start=True, stop=True)
                    mm.then_inc(b_mm, 1)

                @block.scalar
                def _(act):
                    st = Steps(act, astep)
                    act.preload_act_table_set("silu_and_others")
                    for j, dst in enumerate((la1T, qlT, klT)):
                        for b in range(2):
                            act.wait_ge(lproj, 2 * j + b + 1)
                            w = RANK if j == 0 else P
                            act.activation(dst[:, 512 * b:512 * b + 512], PS[0:w, 2 * (j % 2) + b, :], ACT.Copy).then_inc(l_ready, 1)
                    for n in range(NT):
                        act.wait_ge(nproj, n + 1)
                        st.done(act.activation(vl[:, n, :], PS[:, 4 + n % 2, 0:GV], ACT.Copy))
                        act.activation(slr[:, n, :], PS[:, 4 + n % 2, GV:512], ACT.Silu).then_inc(n_ready, 1)
                    act.wait_ge(lx_ready, 1)
                    act.preload_act_table_set("natural_log_exp_and_others")
                    st.done(act.activation(le[:, :, :], lx[:, :, :], ACT.Abs))
                    st.done(act.activation(le[:, :, :], le[:, :, :], ACT.Exp, scale=-1.0))
                    act.activation(le[:, :, :], le[:, :, :], ACT.Ln, bias=1.0).then_inc(ls_act, 1)
                    act.wait_ge(b_mm, 1)
                    for b in range(2):
                        act.activation(bT[:, 512 * b:512 * b + 512], PS[:, 6 + b, :], ACT.Copy, scale=1.0 / 16).then_inc(b_ready, 1)

                @block.vector
                def _(dve):
                    st = Steps(dve, dstep)
                    dve.wait_ge(la_mm, 1)
                    ba = par("b_a").unsqueeze(1).to_broadcast([P, 4, GK])
                    for b in range(2):
                        i = dve.tensor_tensor(lx[:, 4 * b:4 * b + 4, :], PS[:, 6 + b, :].rearrange("p (n c) -> p n c", n=4), ba, ALU.add)
                        st.done(i) if b == 0 else i.then_inc(lx_ready, 1)
                    dve.wait_ge(lx_ready, 1)
                    st.done(dve.tensor_scalar(lm_[:, :, :], lx[:, :, :], 0.0, None, ALU.min))
                    dve.wait_ge(ls_act, 1)
                    dve.tensor_tensor(lx[:, :, :], lm_[:, :, :], le[:, :, :], ALU.subtract).then_inc(ls_ready, 1)
                    go = par("gla_o").unsqueeze(1).to_broadcast([P, NT * H_GLA, HD])
                    sg = slr[:, :, :].rearrange("p n (h d) -> p (n h) d", d=HD)
                    dve.wait_ge(n_ready, NT)
                    st.done(dve.tensor_tensor(sg, sg, go, ALU.mult))

            with ExitStack() as c, nc.Block() as block:
                new_phase(c)
                LV = 7
                H2 = S // 2
                el_, kl = sb("el_", [P, 2, S], c=c), sb("kl", [P, 2, S], c=c)
                qc = sb("qc", [P, 2, H2], c=c)
                qe, kdT = sb("qe", [P, S], c=c), sb("kdT", [P, S], c=c)
                qk = sb("qk", [P, S], c=c)
                kdn = sb("kdn", [P, NT, GK], c=c)
                e_end = sb("e_end", [P, NT], c=c)
                Sg = sb("Sg", [P, NT, GV], c=c)
                kvm = sb("kvm", [P, GV], c=c)
                oss, orr = sb("loss", [P, NT * H_GLA], c=c), sb("lorr", [P, NT * H_GLA], c=c)
                place = hT[:, :, :].rearrange("p k t -> p (k t)")
                qm = place[:, 0:2 * H_GLA * H2].rearrange("p (b h t) -> p b h t", b=2, h=H_GLA)
                sc = place[:, 2 * H_GLA * H2:].rearrange("p (n h t) -> p n h t", n=NT, h=H_GLA)
                osq = el_[:, :, :].rearrange("p b t -> p (b t)").rearrange("p (n v) -> p n v", n=NT)
                diff_ready, e_ready, kl_ready, qc_ready, qm_ready, sc_mm, sc_done, zeroed = (sem(n_) for n_ in (
                    "diff_ready", "e_ready", "kl_ready", "qc_ready", "qm_ready", "sc_mm", "sc_done", "sc_zeroed"))
                eb_ready, end_diff, ekd_ready, qe_ready, kdT_ready = (sem(n_) for n_ in (
                    "eb_ready", "end_diff", "ekd_ready", "qe_ready", "kdT_ready"))
                kd_turned, kdn_ready, kv_mm, S_ready, qk_ready, diag_mm, diag_done = (sem(n_) for n_ in (
                    "lkd_turned", "kdn_ready", "kv_mm", "lS_ready", "qk_ready", "diag_mm", "diag_done"))
                o_mm, o_ready, sq_done, ss_done, rr_done = (sem(n_) for n_ in ("lo_mm", "lo_ready", "lsq_done", "lss_done", "lrr_done"))
                dstep, astep = sem("m_dve_step"), sem("m_act_step")
                B_SC = (0, 1, 6, 7)
                B_KV, B_O, B_DG = (2, 3, 4, 5), (3, 4), 5

                def halves(t, l):
                    v = t.rearrange("p (b u w) -> p b u w", u=2, w=1 << l)
                    return v[:, :, 0, :], v[:, :, 1, :]

                def upper(t, l):
                    return t.rearrange("p (b w) -> p b w", w=1 << l)

                def head_rows(h):
                    return kc[:, K_BD + h // 2, (h % 2) * HD:(h % 2) * HD + 1]

                @block.gpsimd
                def _(pool):
                    for l in range(LV):
                        blo, bhi = halves(bT[:, :], l)
                        elo, ehi = halves(el_[:, l % 2, :], l)
                        ref = bhi[:, :, 0:1].to_broadcast([P, S >> (l + 1), 1 << l])
                        if l >= 2:
                            pool.wait_ge(kl_ready, l - 1)
                            pool.wait_ge(qc_ready, l - 1)
                        pool.tensor_tensor(elo, ref, blo, ALU.subtract).then_inc(diff_ready, 1)
                        pool.tensor_tensor(ehi, bhi, ref, ALU.subtract).then_inc(diff_ready, 1)
                        if l == 0:
                            pool.memset(sc, 0.0).then_inc(zeroed, 1)

                @block.tensor
                def _(pe):
                    pe.wait_ge(kdT_ready, 1)
                    for b in range(2):
                        for n in range(4 * b, 4 * b + 4):
                            mm = pe.transpose(PS[:, b, (n % 4) * P:(n % 4 + 1) * P], kdT[:, n * P:(n + 1) * P], ident)
                        mm.then_inc(kd_turned, 1)
                    for n in range(NT):
                        pe.wait_ge(kdn_ready, n // 4 + 1)
                        mm = pe.matmul(PS[:, B_KV[n // 2], (n % 2) * GV:(n % 2 + 1) * GV], kdn[:, n, :], vl[:, n, :], start=True, stop=True)
                        if n % 2:
                            mm.then_inc(kv_mm, 1)
                    for l in range(LV):
                        pe.wait_ge(kl_ready, l + 1)
                        pe.wait_ge(qm_ready, l + 1)
                        for n in range(NT):
                            u = l * NT + n
                            if u >= 4:
                                pe.wait_ge(sc_done, u - 3)
                            pe.matmul(PS[:, B_SC[u % 4], 0:4 * 64], kl[:, l % 2, n * P:(n + 1) * P], qm[:, l % 2, :, 64 * n:64 * n + 64],
                                      start=True, stop=True).then_inc(sc_mm, 1)
                        if l == 1:
                            pe.wait_ge(qk_ready, 1)
                            pe.wait_ge(S_ready, NT)
                            for n in range(NT):
                                mm = pe.matmul(PS[:, B_DG, n * H_GLA:(n + 1) * H_GLA], qk[:, n * P:(n + 1) * P],
                                               kc[:, K_BD:K_BD + 2, 0:P:HD].rearrange("p a b -> p (a b)"), start=True, stop=True)
                            mm.then_inc(diag_mm, 1)
                    pe.wait_ge(qe_ready, 1)
                    pe.wait_ge(diag_done, 1)
                    for n in range(NT):
                        pe.wait_ge(sc_done, (LV - 1) * NT + n + 1)
                        if n >= 2:
                            pe.wait_ge(o_ready, n - 1)
                        pe.matmul(PS[:, B_O[n % 2], 0:GV], qe[:, n * P:(n + 1) * P], Sg[:, n, :], start=True, stop=False)
                        for h in range(H_GLA):
                            mm = pe.matmul(PS[:, B_O[n % 2], h * HD:(h + 1) * HD], sc[:, n, h, :], vl[:, n, h * HD:(h + 1) * HD],
                                           start=False, stop=(h == H_GLA - 1))
                        mm.then_inc(o_mm, 1)

                @block.scalar
                def _(act):
                    st = Steps(act, astep)

                    def exp_level(l):
                        act.wait_ge(diff_ready, 2 * l + 2)
                        act.activation(el_[:, l % 2, :], el_[:, l % 2, :], ACT.Exp).then_inc(e_ready, 1)

                    def mask_queries(l):
                        act.wait_ge(qc_ready, l + 1)
                        if l >= 2:
                            act.wait_ge(sc_mm, NT * (l - 1))
                        for h in range(H_GLA):
                            i = act.activation(qm[:, l % 2, h, :], qc[:, l % 2, :], ACT.Copy, scale=head_rows(h))
                        i.then_inc(qm_ready, 1)

                    act.activation(qe[:, :], bT[:, :], ACT.Exp).then_inc(eb_ready, 1)
                    act.wait_ge(end_diff, 1)
                    act.activation(kdT[:, :], kdT[:, :], ACT.Exp).then_inc(ekd_ready, 1)
                    exp_level(0)
                    for b in range(2):
                        act.wait_ge(kd_turned, b + 1)
                        act.activation(kdn[:, 4 * b:4 * b + 4, :], PS[:, b, :].rearrange("p (n t) -> p n t", n=4), ACT.Copy).then_inc(kdn_ready, 1)
                    exp_level(1)
                    for l in range(LV):
                        mask_queries(l)
                        if l + 2 < LV:
                            exp_level(l + 2)
                    for n in range(NT):
                        act.wait_ge(o_mm, n + 1)
                        act.activation(mix[:, n, FOX + GDN:D], PS[:, B_O[n % 2], 0:GV], ACT.Copy, scale=float(DK) ** -0.5)\
                           .then_inc(o_ready, 1)
                        if n % 4 == 3:
                            act.wait_ge(o_ready, n + 1)
                            t = slice(n - 3, n + 1)
                            act.activation(osq[:, t, :], mix[:, t, FOX + GDN:D], ACT.Square).then_inc(sq_done, 1)
                            if n == NT - 1:
                                for g in range(2):
                                    hs = slice(4 * H_GLA * g, 4 * H_GLA * (g + 1))
                                    act.wait_ge(ss_done, g + 1)
                                    st.done(act.activation(orr[:, hs], oss[:, hs], ACT.Ln, bias=eps[:, :], scale=1.0 / HD))
                                    act.activation(orr[:, hs], orr[:, hs], ACT.Exp, scale=-0.5).then_inc(rr_done, 1)

                @block.vector
                def _(dve):
                    st = Steps(dve, dstep)
                    bv = bT[:, :].rearrange("p (n t) -> p n t", n=NT)
                    dve.tensor_tensor(kdT[:, :].rearrange("p (n t) -> p n t", n=NT), bv[:, :, P - 1:P].to_broadcast([P, NT, P]), bv,
                                      ALU.subtract).then_inc(end_diff, 1)
                    st.done(dve.memset(kl[:, :, :], 0.0))
                    dve.memset(Sg[:, 0, :], 0.0).then_inc(S_ready, 1)
                    dve.tensor_tensor(qk[:, :], qlT[:, :], klT[:, :], ALU.mult).then_inc(qk_ready, 1)
                    dve.wait_ge(ekd_ready, 1)
                    dve.tensor_tensor(kdT[:, :], kdT[:, :], klT[:, :], ALU.mult).then_inc(kdT_ready, 1)
                    dve.wait_ge(eb_ready, 1)
                    st.done(dve.tensor_copy(e_end[:, :], qe[:, :].rearrange("p (n t) -> p n t", n=NT)[:, :, P - 1]))
                    dve.tensor_tensor(qe[:, :], qe[:, :], qlT[:, :], ALU.mult).then_inc(qe_ready, 1)

                    def factors(l):
                        dve.wait_ge(e_ready, l + 1)
                        elo, ehi = halves(el_[:, l % 2, :], l)
                        if l >= 2:
                            dve.wait_ge(sc_mm, NT * (l - 1))
                            dve.wait_ge(qm_ready, l - 1)
                        dve.tensor_tensor(halves(kl[:, l % 2, :], l)[0], halves(klT[:, :], l)[0], elo, ALU.mult).then_inc(kl_ready, 1)
                        dve.tensor_tensor(upper(qc[:, l % 2, :], l), halves(qlT[:, :], l)[1], ehi, ALU.mult).then_inc(qc_ready, 1)

                    def take_scores(l):
                        w = 1 << l
                        for n in range(NT):
                            dve.wait_ge(sc_mm, l * NT + n + 1)
                            dst = sc[:, n, :, :].rearrange("p h (b u w) -> p h b u w", u=2, w=w)[:, :, :, 1, :]
                            lm = kc[:, K_LM + l, :].bitcast(U32).rearrange("p (b u w) -> p b u w", u=2, w=w)[:, :, 1, :]
                            src = PS[:, B_SC[(l * NT + n) % 4], 0:4 * 64].rearrange("p (h b w) -> p h b w", h=H_GLA, w=w)
                            dve.copy_predicated(dst, lm.unsqueeze(1).to_broadcast([P, H_GLA, 64 // w, w]), src).then_inc(sc_done, 1)

                    def states():
                        for n in range(NT - 1):
                            dve.wait_ge(kv_mm, n // 2 + 1)
                            dve.wait_ge(S_ready, n + 1)
                            kv = PS[:, B_KV[n // 2], (n % 2) * GV:(n % 2 + 1) * GV]
                            st.done(dve.tensor_tensor(kvm[:, :], kv, kc[:, K_BD:K_BD + 2, :].rearrange("p a b -> p (a b)"), ALU.mult))
                            dve.scalar_tensor_tensor(out=Sg[:, n + 1, :], in0=Sg[:, n, :], scalar=e_end[:, n:n + 1], in1=kvm[:, :],
                                                     op0=ALU.mult, op1=ALU.add).then_inc(S_ready, 1)

                    factors(0)
                    factors(1)
                    states()
                    dve.wait_ge(zeroed, 1)
                    take_scores(0)
                    for l in range(1, LV):
                        if l + 1 < LV:
                            factors(l + 1)
                        take_scores(l)
                        if l == 1:
                            dve.wait_ge(diag_mm, 1)
                            d = PS[:, B_DG, 0:NT * H_GLA].rearrange("p (n h) -> p n h", n=NT)
                            for n in range(NT):
                                i = dve.copy_predicated(sc[:, n, :, :], ident.bitcast(U32).unsqueeze(1).to_broadcast([P, H_GLA, P]),
                                                        d[:, n, :].unsqueeze(2).to_broadcast([P, H_GLA, P]))
                                st.done(i) if n < NT - 1 else i.then_inc(diag_done, 1)
                    for g in range(2):
                        dve.wait_ge(sq_done, g + 1)
                        dve.tensor_reduce(oss[:, 16 * g:16 * g + 16], osq[:, 4 * g:4 * g + 4, :].rearrange("p n (h d) -> p (n h) d", d=HD),
                                          AX.X, ALU.add).then_inc(ss_done, 1)
                    for g in range(2):
                        dve.wait_ge(rr_done, g + 1)
                        o = mix[:, 4 * g:4 * g + 4, FOX + GDN:D]
                        for n in range(4 * g, 4 * g + 4):
                            o3 = mix[:, n, FOX + GDN:D].rearrange("p (h d) -> p h d", d=HD)
                            i = dve.tensor_tensor(o3, o3, orr[:, H_GLA * n:H_GLA * n + H_GLA].unsqueeze(2).to_broadcast([P, H_GLA, HD]), ALU.mult)
                            st.done(i)
                        st.done(dve.tensor_tensor(o, o, slr[:, 4 * g:4 * g + 4, :], ALU.mult))

        raw_g = hT[:, :, :].rearrange("p k t -> p (k t)").rearrange("p (b n) -> p b n", b=2)
        raw_u = wslots[:, 0:2, :, :].rearrange("p b k n -> p b (k n)")
        raw_d = wslots[:, 2, :, :].rearrange("p k n -> p (k n)")

        def raw_gate_up(j, i):
            v = (raw_g, raw_u)[j]
            return v[:, i % 2, :] if isinstance(i, int) else v[:, bass.ds(i & 1, 1), :].rearrange("p o n -> p (o n)")

        raw_loaded = [sem(n_) for n_ in ("gate_loaded", "up_loaded", "down_loaded")]
        KH = DE // P

        def load_raw(eng, j, e, i):
            src = (w_g, w_u, w_d)[j]
            src = src[e] if isinstance(e, int) else src[bass.ds(e, 1), :, :].rearrange("o a b -> (o a) b")
            dst = raw_d if j == 2 else raw_gate_up(j, i)
            eng.dma_start(dst.rearrange("p (k n) -> p k n", k=KH if j == 2 else KD), src.rearrange("(k p) n -> p k n", p=P))\
               .then_inc(raw_loaded[j], 16)

        rl = sb("rl", [P, NT, NG + NE])
        with ExitStack() as c, nc.Block() as block:
            new_phase(c)
            xr = sb("xr", [P, 2, D], c=c)
            mT = sb("mT", [P, 2, KD, P], c=c)
            h2 = sb("h2", [P, 2, D], c=c)
            wr = sb("wr", [P, KD, NG + NE], c=c)
            junk = sb("junk2", [P, D], c=c)
            zy = sb("zy", [P, D], c=c)
            zy_ready, zy_stored = sem("zy_ready"), sem("zy_stored")
            ss, rr = sb("oss2", [P, NT], c=c), sb("orr2", [P, NT], c=c)
            xr_loaded, wr_loaded = [sem("xr_loaded0"), sem("xr_loaded1")], sem("wr_loaded")
            m_turned, mT_ready, y_mm, x1_ready = sem("m_turned"), sem("mT_ready"), sem("y_mm"), sem("x1_ready")
            r2_ready, h2_ready, h2_turned, h2T_ready, rl_mm, rl_ready = (sem(n_) for n_ in (
                "r2_ready", "h2_ready", "h2_turned", "h2T_ready", "rl_mm", "rl_ready"))
            h2_stored = [sem("h2_stored0"), sem("h2_stored1")]
            astep = sem("o_act_step")
            rlT = sb("rlT", [NG + NE, 512], c=c)
            rlT_ready, rl_turned = sem("rlT_ready"), sem("rl_turned")

            @block.sync
            def _(sp):
                sp.dma_start(wr[:, :, :], w_router.rearrange("(k p) n -> p k n", p=P)).then_inc(wr_loaded, 16)
                load_raw(sp, 2, 0, 0)
                for n in range(NT):
                    if n >= 2:
                        sp.wait_ge(x1_ready, 2 * (n - 1))
                    sp.dma_start(xr[:, n % 2, :], x[n * P:(n + 1) * P, :]).then_inc(xr_loaded[n % 2], 16)
                    if n >= 1:
                        sp.wait_ge(h2_ready, n)
                        sp.dma_start(h2_dram[(n - 1) * P:n * P, :], h2[:, (n - 1) % 2, :]).then_inc(h2_stored[(n - 1) % 2], 16)
                sp.wait_ge(h2_ready, NT)
                sp.dma_start(h2_dram[(NT - 1) * P:S, :], h2[:, (NT - 1) % 2, :]).then_inc(h2_stored[(NT - 1) % 2], 16)
                for i in range(2):
                    sp.wait_ge(h2_stored[i], 16 * NT // 2)
                sp.wait_ge(zy_stored, 16)

            @block.gpsimd
            def _(pool):
                pool.memset(zy[:, :], 0.0).then_inc(zy_ready, 1)
                pool.wait_ge(zy_ready, 1)
                pool.dma_start(y_dram[NE * P:, :].rearrange("(b p) d -> p b d", p=P),
                               zy[:, :].unsqueeze(1).to_broadcast([P, MAXB - NE, D])).then_inc(zy_stored, 16)

            @block.tensor
            def _(pe):
                def turn(n):
                    for b in range(2):
                        if n >= 1:
                            pe.wait_ge(mT_ready, 2 * (n - 1) + b + 1)
                        for k in range(4):
                            mm = pe.transpose(PS[:, b, k * P:(k + 1) * P], mix[:, n, (4 * b + k) * P:(4 * b + k + 1) * P], ident)
                        mm.then_inc(m_turned, 1)

                def project(n):
                    for b in range(2):
                        if n == 0:
                            chunk_ready(pe, CH_O0 + b)
                        else:
                            pe.wait_ge(x1_ready, 2 * (n - 1) + b + 1)
                        for k in range(KD):
                            pe.wait_ge(mT_ready, 2 * n + k // 4 + 1) if b == 0 and k % 4 == 0 else None
                            mm = pe.matmul(PS[:, 2 + b, :], mT[:, n % 2, k, :], wring[(CH_O0 + b) % 3][:, k, :],
                                           start=(k == 0), stop=(k == KD - 1))
                        mm.then_inc(y_mm, 1)

                def route(n):
                    pe.wait_ge(h2_ready, n + 1)
                    for b in range(2):
                        if n >= 1:
                            pe.wait_ge(h2T_ready, 2 * (n - 1) + b + 1)
                        for k in range(4):
                            mm = pe.transpose(PS[:, 4 + b, k * P:(k + 1) * P], h2[:, n % 2, (4 * b + k) * P:(4 * b + k + 1) * P], ident)
                        mm.then_inc(h2_turned, 1)

                def logits(g):
                    pe.wait_ge(h2T_ready, 8 * (g + 1))
                    for k in range(KD):
                        mm = pe.matmul(PS[0:NG + NE, 6, :], wr[:, k, :], hT[:, k, 512 * g:512 * g + 512], start=(k == 0), stop=(k == KD - 1))
                    mm.then_inc(rl_mm, 1)

                def turn_logits(g):
                    pe.wait_ge(rlT_ready, g + 1)
                    if g:
                        pe.wait_ge(rl_ready, 4 * g)
                    for n in range(4):
                        mm = pe.transpose(PS[:, 7, n * (NG + NE):(n + 1) * (NG + NE)], rlT[:, n * P:(n + 1) * P], ident[0:NG + NE, 0:NG + NE])
                    mm.then_inc(rl_turned, 1)

                pe.wait_ge(wr_loaded, 16)
                turn(0)
                for n in range(NT):
                    if n + 1 < NT:
                        turn(n + 1)
                    project(n)
                    if n == 5:
                        turn_logits(0)
                    if n >= 1:
                        route(n - 1)
                    if n == 4:
                        logits(0)
                route(NT - 1)
                logits(1)
                turn_logits(1)
                pe.wait_ge(y_mm, 2 * NT)
                pe.nop().then_inc(w_used, 2)

            @block.scalar
            def _(act):
                st = Steps(act, astep)

                def turned(n):
                    for b in range(2):
                        act.wait_ge(m_turned, 2 * n + b + 1)
                        if n >= 2:
                            act.wait_ge(y_mm, 2 * (n - 1))
                        act.activation(mT[:, n % 2, 4 * b:4 * b + 4, :], PS[:, b, :].rearrange("p (k t) -> p k t", k=4), ACT.Copy)\
                           .then_inc(mT_ready, 1)

                def logit_rows(g):
                    act.wait_ge(rl_mm, g + 1)
                    if g:
                        act.wait_ge(rl_turned, g)
                    act.activation(rlT[:, :], PS[0:NG + NE, 6, :], ACT.Copy).then_inc(rlT_ready, 1)

                turned(0)
                for n in range(NT):
                    if n + 1 < NT:
                        turned(n + 1)
                    if n == 5:
                        logit_rows(0)
                    act.wait_ge(x1_ready, 2 * n + 2)
                    st.done(act.activation(junk[:, :], mix[:, n, :], ACT.Square, accum_out=ss[:, n:n + 1]))
                    st.done(act.activation(rr[:, n:n + 1], ss[:, n:n + 1], ACT.Ln, bias=eps[:, :], scale=1.0 / D))
                    act.activation(rr[:, n:n + 1], rr[:, n:n + 1], ACT.Exp, scale=-0.5).then_inc(r2_ready, 1)
                logit_rows(1)

            @block.vector
            def _(dve):
                def residual(n):
                    dve.wait_ge(xr_loaded[n % 2], 16 * (n // 2 + 1))
                    for b in range(2):
                        dve.wait_ge(y_mm, 2 * n + b + 1)
                        if b == 0:
                            dve.wait_ge(m_turned, 2 * n + 2)
                        c_ = slice(512 * b, 512 * b + 512)
                        dve.tensor_tensor(mix[:, n, c_], PS[:, 2 + b, :], xr[:, n % 2, c_], ALU.add).then_inc(x1_ready, 1)

                def norm(n):
                    dve.wait_ge(r2_ready, n + 1)
                    if n >= 2:
                        dve.wait_ge(h2_stored[n % 2], 16 * (n // 2))
                    dve.tensor_scalar(h2[:, n % 2, :], mix[:, n, :], rr[:, n:n + 1], None, ALU.mult).then_inc(h2_ready, 1)
                    for b in range(2):
                        dve.wait_ge(h2_turned, 2 * n + b + 1)
                        g = par("ffn_gain")[:, 4 * b:4 * b + 4].unsqueeze(2).to_broadcast([P, 4, P])
                        dve.tensor_tensor(hT[:, 4 * b:4 * b + 4, n * P:(n + 1) * P],
                                          PS[:, 4 + b, :].rearrange("p (k t) -> p k t", k=4), g, ALU.mult).then_inc(h2T_ready, 1)

                def logits(n):
                    dve.wait_ge(rl_turned, n // 4 + 1)
                    dve.tensor_tensor(rl[:, n, :], PS[:, 7, (n % 4) * (NG + NE):(n % 4 + 1) * (NG + NE)], prm[:, PC["b_rg"][0]:PC["b_re"][1]], ALU.add).then_inc(rl_ready, 1)

                for n in range(NT):
                    residual(n)
                    if n >= 1:
                        norm(n - 1)
                    if n == 6:
                        for m in range(4):
                            logits(m)
                norm(NT - 1)
                for m in range(4, NT):
                    logits(m)

        dest_i = sb("dest_i", [P, NT, 2], I32)
        gates = sb("gates", [P, NT, 2])
        plan = sb("plan", [1, 2 + 16], I32)
        slots_i = sb("slots_i", [P, LST], I32)
        with ExitStack() as c, nc.Block() as block:
            new_phase(c)
            def rt(name, *shape, dt=F32):
                return sb(name, [P, *shape], dt, c=c)
            glp, g8, gi8 = rt("glp", NT, 8), rt("g8", NT, 8), rt("gi8", NT, 8, dt=U32)
            gidx, oh_g, gd, gs = rt("gidx", NT), rt("oh_g", NT, NG), rt("gd", NT, NG), rt("gs", NT)
            eall, esel = rt("eall", NT, NG, EPG), rt("esel", NT, EPG)
            e8, ei8, eid, rr = rt("e8", NT, 8), rt("ei8", NT, 8, dt=U32), rt("eid", NT, 2), rt("rr3", NT)
            Mk, Mb, onesb = rt("Mk", 2, NT, NE), rt("Mb", NT, NE, dt=BF16), rt("onesb", P, dt=BF16)
            pre, rank, ov, cum, big = rt("pre", NT, NE), rt("rank", NT, NE), rt("ov", NE), rt("cum", 2, NE), rt("big", NT, NE)
            cnt, ia, ib = rt("cnt", NE), rt("ia", NE), rt("ib", NE)
            tmpd, dest_f, nb_f, cmp_, tok = rt("tmpd", NT, NE), rt("dest_f", NT, 2), rt("nb_f", 18), rt("cmp", 16, NE), rt("tok", NT)
            zl = sb("zl", [LST, P], c=c)
            lrow = sb("lrow", [LST, P], c=c)
            g_exp, g_act, Mb_ready, rank_mm, dest_ready, zl_ready = (sem(n_) for n_ in (
                "g_exp", "g_act", "Mb_ready", "rank_mm", "dest_ready", "zl_ready"))
            zl_stored, listed, lrow_loaded, l_turned = sem("zl_stored"), sem("listed"), sem("lrow_loaded"), sem("l_turned")
            dstep = sem("r_dve_step")

            @block.sync
            def _(sp):
                for j, e in ((0, 0), (1, 0), (0, 1), (1, 1)):
                    if e == 1:
                        sp.wait_ge(raw_loaded[j], 16)
                    load_raw(sp, j, e, e)
                sp.wait_ge(zl_ready, 1)
                sp.dma_start(list_dram.rearrange("(a b) o -> a (b o)", b=P), zl[:, :]).then_inc(zl_stored, 16)
                sp.wait_ge(listed, 16 * 2 * NT)
                sp.dma_start(lrow[:, :], list_dram.rearrange("(a b) o -> a (b o)", b=P)).then_inc(lrow_loaded, 16)

            @block.gpsimd
            def _(pool):
                pool.wait_ge(zl_stored, 16)
                pool.wait_ge(dest_ready, 1)
                for n in range(NT):
                    for k in range(2):
                        pool.indirect_dma_start(list_dram, bass.IndirectOffsetOnAxis(ap=dest_i[:, n, k:k + 1], axis=0),
                                                tok[:, n:n + 1], None).then_inc(listed, 16)

            @block.tensor
            def _(pe):
                pe.wait_ge(Mb_ready, 1)
                m = Mb[:, :, :].rearrange("p n e -> p (n e)")
                pe.matmul(PS[:, 0, 0:NT * NE], before, m, start=True, stop=True)
                pe.matmul(PS[:, 1, 0:NT * NE], onesb[:, :], m, start=True, stop=True).then_inc(rank_mm, 1)
                pe.wait_ge(lrow_loaded, 16)
                pe.transpose(PS[:, 2, 0:LST], lrow[:, :], ident[0:LST, 0:LST]).then_inc(l_turned, 1)

            @block.scalar
            def _(act):
                act.wait_ge(g_exp, 1)
                act.activation(gd[:, :, :], gd[:, :, :], ACT.Exp).then_inc(g_act, 1)
                act.wait_ge(g_exp, 2)
                act.activation(rr[:, :], rr[:, :], ACT.Exp).then_inc(g_act, 1)

            @block.vector
            def _(dve):
                st = Steps(dve, dstep)
                dve.memset(zl[:, :], 0.0).then_inc(zl_ready, 1)
                st.done(dve.memset(onesb[:, :], 1.0))
                st.done(dve.memset(glp[:, :, :], NEG))
                st.done(dve.tensor_copy(glp[:, :, 0:NG], rl[:, :, 0:NG]))
                for n in range(NT):
                    st.done(dve.max(g8[:, n, :], glp[:, n, :]))
                    st.done(dve.max_index(gi8[:, n, :], g8[:, n, :], glp[:, n, :]))
                st.done(dve.tensor_copy(gidx[:, :], gi8[:, :, 0]))
                iota = kc[:, K_IOTA, :]
                st.done(dve.tensor_tensor(oh_g[:, :, :], iota[:, 0:NG].unsqueeze(1).to_broadcast([P, NT, NG]),
                                          gidx[:, :].unsqueeze(2).to_broadcast([P, NT, NG]), ALU.is_equal))
                dve.tensor_tensor(gd[:, :, :], rl[:, :, 0:NG], g8[:, :, 0:1].to_broadcast([P, NT, NG]), ALU.subtract).then_inc(g_exp, 1)
                for n in range(NT):
                    st.done(dve.tensor_tensor(eall[:, n, :, :], rl[:, n, NG:].rearrange("p (g e) -> p g e", g=NG),
                                              oh_g[:, n, :].unsqueeze(2).to_broadcast([P, NG, EPG]), ALU.mult))
                    st.done(dve.tensor_reduce(esel[:, n, :], eall[:, n, :, :].rearrange("p g e -> p e g"), AX.X, ALU.add))
                    st.done(dve.max(e8[:, n, :], esel[:, n, :]))
                    st.done(dve.max_index(ei8[:, n, :], e8[:, n, :], esel[:, n, :]))
                dve.tensor_tensor(rr[:, :], e8[:, :, 1], e8[:, :, 0], ALU.subtract).then_inc(g_exp, 1)
                st.done(dve.tensor_copy(eid[:, :, :], ei8[:, :, 0:2]))
                st.done(dve.tensor_scalar(gidx[:, :], gidx[:, :], float(EPG), None, ALU.mult))
                st.done(dve.tensor_tensor(eid[:, :, :], eid[:, :, :], gidx[:, :].unsqueeze(2).to_broadcast([P, NT, 2]), ALU.add))
                for k in range(2):
                    st.done(dve.tensor_tensor(Mk[:, k, :, :], iota[:, 0:NE].unsqueeze(1).to_broadcast([P, NT, NE]),
                                              eid[:, :, k:k + 1].to_broadcast([P, NT, NE]), ALU.is_equal))
                dve.tensor_tensor(Mb[:, :, :], Mk[:, 0, :, :], Mk[:, 1, :, :], ALU.add).then_inc(Mb_ready, 1)
                dve.wait_ge(g_act, 2)
                st.done(dve.tensor_reduce(gs[:, :], gd[:, :, :], AX.X, ALU.add))
                st.done(dve.reciprocal(gs[:, :], gs[:, :]))
                st.done(dve.tensor_scalar(gates[:, :, 1], rr[:, :], 1.0, None, ALU.add))
                st.done(dve.reciprocal(gates[:, :, 1], gates[:, :, 1]))
                st.done(dve.tensor_tensor(gates[:, :, 0], gates[:, :, 1], gs[:, :], ALU.mult))
                st.done(dve.tensor_tensor(gates[:, :, 1], gates[:, :, 0], rr[:, :], ALU.mult))
                dve.wait_ge(rank_mm, 1)
                st.done(dve.memset(pre[:, 0, :], 0.0))
                tot = PS[:, 1, 0:NT * NE].rearrange("p (n e) -> p n e", n=NT)
                for n in range(1, NT):
                    st.done(dve.tensor_tensor(pre[:, n, :], pre[:, n - 1, :], tot[:, n - 1, :], ALU.add))
                st.done(dve.tensor_tensor(cnt[:, :], pre[:, NT - 1, :], tot[:, NT - 1, :], ALU.add))
                st.done(dve.tensor_tensor(rank[:, :, :], pre[:, :, :], PS[:, 0, 0:NT * NE].rearrange("p (n e) -> p n e", n=NT), ALU.add))
                st.done(dve.tensor_scalar(ov[:, :], cnt[:, :], float(P), None, ALU.is_gt))
                for m in range(2, NT):
                    st.done(dve.scalar_tensor_tensor(out=ov[:, :], in0=cnt[:, :], scalar=float(P * m), in1=ov[:, :], op0=ALU.is_gt, op1=ALU.add))
                st.done(dve.tensor_copy(cum[:, 0, :], ov[:, :]))
                a = 0
                for sh in (1, 2, 4, 8, 16):
                    st.done(dve.tensor_copy(cum[:, 1 - a, 0:sh], cum[:, a, 0:sh]))
                    st.done(dve.tensor_tensor(cum[:, 1 - a, sh:NE], cum[:, a, sh:NE], cum[:, a, 0:NE - sh], ALU.add))
                    a = 1 - a
                incl = cum[:, a, :]
                st.done(dve.tensor_scalar(ia[:, :], iota[:, 0:NE], float(P), None, ALU.mult))
                st.done(dve.tensor_tensor(ib[:, :], incl, ov[:, :], ALU.subtract))
                st.done(dve.tensor_scalar(ib[:, :], ib[:, :], float(NE - 1), float(P), ALU.add, ALU.mult))
                st.done(dve.tensor_tensor(ib[:, :], ib[:, :], ia[:, :], ALU.subtract))
                st.done(dve.tensor_scalar(big[:, :, :], rank[:, :, :], float(P), None, ALU.is_ge))
                st.done(dve.tensor_tensor(big[:, :, :], big[:, :, :], ib[:, :].unsqueeze(1).to_broadcast([P, NT, NE]), ALU.mult))
                st.done(dve.tensor_tensor(rank[:, :, :], rank[:, :, :], big[:, :, :], ALU.add))
                st.done(dve.tensor_tensor(rank[:, :, :], rank[:, :, :], ia[:, :].unsqueeze(1).to_broadcast([P, NT, NE]), ALU.add))
                for k in range(2):
                    st.done(dve.tensor_tensor(tmpd[:, :, :], rank[:, :, :], Mk[:, k, :, :], ALU.mult))
                    st.done(dve.tensor_reduce(dest_f[:, :, k], tmpd[:, :, :], AX.X, ALU.add))
                for n in range(NT):
                    st.done(dve.tensor_scalar(tok[:, n:n + 1], kc[:, K_HO, 2:3], float(n * P), None, ALU.add))
                dve.tensor_copy(dest_i[:, :, :], dest_f[:, :, :]).then_inc(dest_ready, 1)
                st.done(dve.tensor_scalar(nb_f[:, 0:1], incl[:, NE - 1:NE], float(NE - 2), None, ALU.add))
                st.done(dve.memset(nb_f[:, 1:2], float(NE - 1)))
                st.done(dve.tensor_tensor(cmp_[:, :, :], incl.unsqueeze(1).to_broadcast([P, 16, NE]),
                                          iota[:, 0:16].unsqueeze(2).to_broadcast([P, 16, NE]), ALU.is_le))
                st.done(dve.tensor_reduce(nb_f[:, 2:18], cmp_[:, :, :], AX.X, ALU.add))
                st.done(dve.tensor_scalar(nb_f[:, 2:18], nb_f[:, 2:18], float(NE - 1), None, ALU.min))
                st.done(dve.tensor_copy(plan[:, :], nb_f[0:1, :]))
                dve.wait_ge(l_turned, 1)
                st.done(dve.tensor_copy(slots_i[:, :], PS[:, 2, 0:LST]))

        with ExitStack() as c, nc.Block() as block:
            new_phase(c)
            F32R = mybir.dt.float32r
            w_split = [sb(f"w_split{r}", [P, 2, 4, 512], c=c) for r in range(3)]
            xg, ysb, xf = sb("xg", [P, D], c=c), sb("ysb", [P, D], c=c), sb("xf", [P, KD, P], c=c)
            x_hi, x_lo = sb("x_hi", [P, KD, P], c=c), sb("x_lo", [P, KD, P], c=c)
            sg, ac = sb("sg", [P, DE], c=c), sb("ac", [P, DE], c=c)
            a_hi, a_lo = sb("a_hi", [P, KH, P], c=c), sb("a_lo", [P, KH, P], c=c)
            idxb = sb("idxb", [P, 1], I32, c=c)
            settle, settled = sb("settle", [P, 1], c=c), sb("settled", [P, 1], c=c)
            idx_ready, x_gathered, x_turned, x_scaled, xhi_ready, xlo_ready = (sem(n_) for n_ in (
                "idx_ready", "x_gathered", "x_turned", "x_scaled", "xhi_ready", "xlo_ready"))
            hi_ready, lo_ready, used = sem("whi_ready"), sem("wlo_ready"), sem("half_used")
            silu_ready, ac_ready, a_turned, ahi_ready, alo_ready = (sem(n_) for n_ in (
                "e_silu_ready", "ac_ready", "a_turned", "ahi_ready", "alo_ready"))
            y_copied, y_stored, slot_free = sem("y_copied"), sem("y_stored"), sem("raw_slot_free")
            GATE, UP, DOWN = range(3)

            def blocks(eng):
                return eng.value_load(plan[0:1, 0:1], min_val=NE - 2, max_val=MAXB - 2) + 2

            def same(i, v):
                return isinstance(i, int) and i == v

            def halves_of(i, tail=False):
                seq = [(UP, i - 1, 0), (UP, i - 1, 1)]
                seq += [] if tail else [(GATE, i, 0), (GATE, i, 1)]
                seq += [(DOWN, i - 1, 0), (DOWN, i - 1, 1)]
                return [(j, blk, b, 6 * i - 4 + o) for o, (j, blk, b) in enumerate(seq)]

            def slot(j, b, tail=False):
                return {(UP, 0): 2, (UP, 1): 0, (GATE, 0): 1, (GATE, 1): 2, (DOWN, 0): 0 + tail, (DOWN, 1): 1 + tail}[j, b]

            def w_hi(r):
                return w_split[r][:, 0, :, :]

            def w_lo(r):
                return w_split[r][:, 1, :, :]

            def raw_half(j, blk, b):
                if j == DOWN:
                    return raw_d.rearrange("p (k n) -> p k n", k=KH)[:, :, 512 * b:512 * b + 512]
                return raw_gate_up(j, blk).rearrange("p (k n) -> p k n", k=KD)[:, 4 * b:4 * b + 4, :]

            @block.sync
            def _(sp):
                def load(j, e, i):
                    sp.wait_ge(lo_ready, {GATE: 6 * i - 7, UP: 6 * i - 3, DOWN: 6 * i + 2}[j])
                    sp.nop().then_inc(slot_free, 1)
                    load_raw(sp, j, e, i)

                def expert(i):
                    return sp.value_load(plan[0:1, bass.ds(i - (NE - 2), 1)], min_val=0, max_val=NE - 1)

                for j, split in ((GATE, 2), (UP, 4)):
                    sp.wait_ge(raw_loaded[j], 32)
                    sp.wait_ge(lo_ready, split)
                    load_raw(sp, j, 2, 2)
                load(DOWN, 1, 1)
                with sp.Fori(3, NE) as i:
                    load(GATE, i, i)
                    load(DOWN, i - 1, i - 1)
                    load(UP, i, i)
                nb = blocks(sp)
                with sp.If(nb > NE):
                    with sp.Fori(NE, nb) as i:
                        e = expert(i)
                        load(GATE, e, i)
                        load(DOWN, expert(i - 1), i - 1)
                        load(UP, e, i)
                load(DOWN, expert(nb - 1), nb - 1)

            @block.gpsimd
            def _(pool):
                def gather(i):
                    if not same(i, 0):
                        pool.wait_ge(x_turned, 2 * i)
                    src = slots_i[:, i:i + 1] if isinstance(i, int) else slots_i[:, bass.ds(i, 1)]
                    pool.tensor_copy(idxb[:, :], src).then_inc(idx_ready, 1)
                    pool.wait_ge(idx_ready, i + 1)
                    pool.tensor_tensor(settle[:, :], eps[:, :], eps[:, :], ALU.add)
                    pool.indirect_dma_start(xg[:, :], None, h2_dram, bass.IndirectOffsetOnAxis(ap=idxb[:, 0:1], axis=0))\
                        .then_inc(x_gathered, 16)

                def rest_of_x(i):
                    for b in range(2):
                        pool.wait_ge(xhi_ready, 2 * i + b + 1)
                        k = slice(4 * b, 4 * b + 4)
                        pool.tensor_tensor(x_lo[:, k, :].bitcast(F32R), xf[:, k, :], x_hi[:, k, :], ALU.subtract).then_inc(xlo_ready, 1)

                gather(0)
                rest_of_x(0)
                nb = blocks(pool)
                with pool.Fori(1, nb) as i:
                    gather(i)
                    rest_of_x(i)

            @block.tensor
            def _(pe):
                def turn_x(b, i):
                    if b == 0:
                        pe.wait_ge(x_gathered, 16 * i + 16)
                    if not same(i, 0):
                        pe.wait_ge(x_scaled, 2 * i + b - 1)
                    for k in range(4):
                        mm = pe.transpose(PS[:, b, k * P:(k + 1) * P], xg[:, (4 * b + k) * P:(4 * b + k + 1) * P], ident)
                    mm.then_inc(x_turned, 1)

                def product(bank, hi, lo, r, first, last):
                    for k in range(4):
                        w1, w2 = w_hi(r)[:, k, :].bitcast(F32R), w_lo(r)[:, k, :].bitcast(F32R)
                        x1, x2 = hi[:, k, :].bitcast(F32R), lo[:, k, :].bitcast(F32R)
                        pe.matmul(PS[:, bank, :], x1, w1, start=(first and k == 0), stop=False)
                        pe.matmul(PS[:, bank, :], x1, w2, start=False, stop=False)
                        mm = pe.matmul(PS[:, bank, :], x2, w1, start=False, stop=(last and k == 3))
                    mm.then_inc(used, 1)

                def gate_up(j, b, i, q, r):
                    pe.wait_ge(lo_ready, q + 1)
                    if j == GATE:
                        pe.wait_ge(xlo_ready, 2 * i + b + 1)
                    if b == 0 and not same(i, 0):
                        pe.wait_ge(silu_ready if j == GATE else ac_ready, i)
                    k = slice(4 * b, 4 * b + 4)
                    product(2 + j, x_hi[:, k, :], x_lo[:, k, :], r, b == 0, b == 1)

                def turn_a(i):
                    pe.wait_ge(ac_ready, i + 1)
                    if not same(i, 0):
                        pe.wait_ge(alo_ready, i)
                    for k in range(KH):
                        mm = pe.transpose(PS[:, 4, k * P:(k + 1) * P], ac[:, k * P:(k + 1) * P], ident)
                    mm.then_inc(a_turned, 1)

                def down(b, i, q, r):
                    pe.wait_ge(lo_ready, q + 1)
                    if b == 0:
                        pe.wait_ge(alo_ready, i + 1)
                    if not same(i, 0):
                        pe.wait_ge(y_copied, 2 * i + b - 1)
                    product(5 + b, a_hi, a_lo, r, True, True)

                def iteration(i, p):
                    u0, u1, g0, g1, d0, d1 = halves_of(i)
                    gate_up(UP, 0, p, u0[3], slot(UP, 0))
                    turn_x(0, i)
                    gate_up(UP, 1, p, u1[3], slot(UP, 1))
                    turn_x(1, i)
                    gate_up(GATE, 0, i, g0[3], slot(GATE, 0))
                    turn_a(p)
                    gate_up(GATE, 1, i, g1[3], slot(GATE, 1))
                    down(0, p, d0[3], slot(DOWN, 0))
                    down(1, p, d1[3], slot(DOWN, 1))

                for b in range(2):
                    turn_x(b, 0)
                for b in range(2):
                    gate_up(GATE, b, 0, b, b)
                iteration(1, 0)
                nb = blocks(pe)
                with pe.Fori(2, nb) as i:
                    iteration(i, i - 1)
                u0, u1, d0, d1 = halves_of(nb, tail=True)
                gate_up(UP, 0, nb - 1, u0[3], slot(UP, 0))
                gate_up(UP, 1, nb - 1, u1[3], slot(UP, 1))
                turn_a(nb - 1)
                down(0, nb - 1, d0[3], slot(DOWN, 0, True))
                down(1, nb - 1, d1[3], slot(DOWN, 1, True))

            @block.scalar
            def _(act):
                def split_hi(h, r):
                    j, blk, b, q = h
                    act.wait_ge(raw_loaded[j], 16 * blk + 16)
                    if not (isinstance(q, int) and q < 3):
                        act.wait_ge(used, q - 2)
                    act.activation(w_hi(r).bitcast(F32R), raw_half(j, blk, b), ACT.Copy).then_inc(hi_ready, 1)

                def x_part(b, i):
                    act.wait_ge(x_scaled, 2 * i + b + 1)
                    k = slice(4 * b, 4 * b + 4)
                    act.activation(x_hi[:, k, :].bitcast(F32R), xf[:, k, :], ACT.Copy).then_inc(xhi_ready, 1)

                def silu(i):
                    act.wait_ge(used, 6 * i if not same(i, 0) else 2)
                    if not same(i, 0):
                        act.wait_ge(ac_ready, i)
                    act.activation(sg[:, :], PS[:, 2, :], ACT.Silu).then_inc(silu_ready, 1)

                def a_part(i):
                    act.wait_ge(a_turned, i + 1)
                    act.activation(a_hi[:, :, :].bitcast(F32R), PS[:, 4, :].rearrange("p (k t) -> p k t", k=KH), ACT.Copy).then_inc(ahi_ready, 1)

                def y_half0(i, q):
                    act.wait_ge(used, q + 1)
                    if not same(i, 0):
                        act.wait_ge(y_stored, 16 * i)
                    act.activation(ysb[:, 0:512], PS[:, 5, :], ACT.Copy).then_inc(y_copied, 1)

                def y_half1(i, q):
                    act.wait_ge(used, q + 1)
                    act.activation(ysb[:, 512:D], PS[:, 6, :], ACT.Copy).then_inc(y_copied, 1)
                    act.wait_ge(y_copied, 2 * i + 2)
                    dst = y_dram[i * P:(i + 1) * P, :] if isinstance(i, int) else y_dram[bass.ds(i * P, P), :]
                    act.dma_start(dst, ysb[:, :]).then_inc(y_stored, 16)

                def iteration(i, p):
                    u0, u1, g0, g1, d0, d1 = halves_of(i)
                    if not same(i, 1):
                        split_hi(u0, slot(UP, 0))
                    split_hi(u1, slot(UP, 1))
                    if not same(i, 1):
                        y_half0(p - 1, 6 * p)
                        y_half1(p - 1, 6 * p + 1)
                    split_hi(g0, slot(GATE, 0))
                    x_part(0, i)
                    split_hi(g1, slot(GATE, 1))
                    x_part(1, i)
                    split_hi(d0, slot(DOWN, 0))
                    a_part(p)
                    split_hi(d1, slot(DOWN, 1))
                    silu(i)

                act.preload_act_table_set("silu_and_others")
                for b in range(2):
                    split_hi((GATE, 0, b, b), b)
                split_hi(halves_of(1)[0], slot(UP, 0))
                for b in range(2):
                    x_part(b, 0)
                silu(0)
                iteration(1, 0)
                nb = blocks(act)
                with act.Fori(2, nb) as i:
                    iteration(i, i - 1)
                u0, u1, d0, d1 = halves_of(nb, tail=True)
                split_hi(u0, slot(UP, 0))
                split_hi(u1, slot(UP, 1))
                y_half0(nb - 2, 6 * nb - 6)
                y_half1(nb - 2, 6 * nb - 5)
                split_hi(d0, slot(DOWN, 0, True))
                a_part(nb - 1)
                split_hi(d1, slot(DOWN, 1, True))
                y_half0(nb - 1, 6 * nb - 2)
                y_half1(nb - 1, 6 * nb - 1)
                act.wait_ge(y_stored, 16 * nb)
                act.activation(settled[:, :], eps[:, :], ACT.Copy)

            @block.vector
            def _(dve):
                def split_lo(h, r):
                    j, blk, b, q = h
                    dve.wait_ge(hi_ready, q + 1)
                    dve.tensor_tensor(w_lo(r).bitcast(F32R), raw_half(j, blk, b), w_hi(r), ALU.subtract).then_inc(lo_ready, 1)

                def rows(b, i):
                    dve.wait_ge(x_turned, 2 * i + b + 1)
                    g = par("ffn_gain")[:, 4 * b:4 * b + 4].unsqueeze(2).to_broadcast([P, 4, P])
                    dve.tensor_tensor(xf[:, 4 * b:4 * b + 4, :], PS[:, b, :].rearrange("p (k t) -> p k t", k=4), g, ALU.mult)\
                       .then_inc(x_scaled, 1)

                def act_mul(i, q):
                    dve.wait_ge(used, q + 1)
                    dve.wait_ge(silu_ready, i + 1)
                    dve.tensor_tensor(ac[:, :], sg[:, :], PS[:, 3, :], ALU.mult).then_inc(ac_ready, 1)

                def rest_of_a(i):
                    dve.wait_ge(ahi_ready, i + 1)
                    dve.tensor_tensor(a_lo[:, :, :].bitcast(F32R), PS[:, 4, :].rearrange("p (k t) -> p k t", k=KH), a_hi[:, :, :], ALU.subtract)\
                       .then_inc(alo_ready, 1)

                def iteration(i, p):
                    u0, u1, g0, g1, d0, d1 = halves_of(i)
                    split_lo(u0, slot(UP, 0))
                    split_lo(u1, slot(UP, 1))
                    rows(0, i)
                    split_lo(g0, slot(GATE, 0))
                    rows(1, i)
                    act_mul(p, u1[3])
                    split_lo(g1, slot(GATE, 1))
                    split_lo(d0, slot(DOWN, 0))
                    rest_of_a(p)
                    split_lo(d1, slot(DOWN, 1))

                for b in range(2):
                    split_lo((GATE, 0, b, b), b)
                for b in range(2):
                    rows(b, 0)
                iteration(1, 0)
                nb = blocks(dve)
                with dve.Fori(2, nb) as i:
                    iteration(i, i - 1)
                u0, u1, d0, d1 = halves_of(nb, tail=True)
                split_lo(u0, slot(UP, 0))
                split_lo(u1, slot(UP, 1))
                act_mul(nb - 1, u1[3])
                split_lo(d0, slot(DOWN, 0, True))
                rest_of_a(nb - 1)
                split_lo(d1, slot(DOWN, 1, True))

        with ExitStack() as c, nc.Block() as block:
            new_phase(c)
            yg = wslots[:, :, :, :].rearrange("p a k n -> p (a k n)").rearrange("p (n k d) -> p n k d", n=6, k=2)
            y_gathered = [sem(f"y_gathered{n}") for n in range(NT)]
            sum_ready, out_stored, cstep = sem("sum_ready"), sem("out_stored"), sem("c_step")

            @block.gpsimd
            def _(pool):
                for n in range(NT):
                    if n >= 6:
                        pool.wait_ge(sum_ready, n - 5)
                    for k in range(2):
                        pool.indirect_dma_start(yg[:, n % 6, k, :], None, y_dram,
                                                bass.IndirectOffsetOnAxis(ap=dest_i[:, n, k:k + 1], axis=0)).then_inc(y_gathered[n], 16)

            @block.vector
            def _(dve):
                st = Steps(dve, cstep)
                for n in range(NT):
                    dve.wait_ge(y_gathered[n], 32)
                    st.done(dve.scalar_tensor_tensor(out=mix[:, n, :], in0=yg[:, n % 6, 0, :], scalar=gates[:, n, 0:1], in1=mix[:, n, :],
                                                     op0=ALU.mult, op1=ALU.add))
                    dve.scalar_tensor_tensor(out=mix[:, n, :], in0=yg[:, n % 6, 1, :], scalar=gates[:, n, 1:2], in1=mix[:, n, :],
                                             op0=ALU.mult, op1=ALU.add).then_inc(sum_ready, 1)

            @block.sync
            def _(sp):
                for n in range(NT):
                    sp.wait_ge(sum_ready, n + 1)
                    sp.dma_start(out[n * P:(n + 1) * P, :], mix[:, n, :]).then_inc(out_stored, 16)
                sp.wait_ge(out_stored, 16 * NT)
    return nc


def shape_constants(np, bf16):
    kc = np.zeros((P, NKC, P), np.float32)
    i = np.arange(P)
    kc[:, K_ID] = np.eye(P)
    kc[:, K_U] = i[:, None] <= i[None, :]
    kc[:, K_L] = i[:, None] > i[None, :]
    kc[:, K_ONE] = 1
    for l in range(7):
        same = (i[:, None] >> (l + 1)) == (i[None, :] >> (l + 1))
        kc[:, K_LM + l] = same & (((i[:, None] >> l) & 1) == 0) & (((i[None, :] >> l) & 1) == 1)
    for h in range(H_GLA):
        kc[:, K_BD + h // 2, (h % 2) * HD:(h % 2 + 1) * HD] = (i[:, None] // DK) == h
    kc[0:HD, K_HO, 0] = 1
    kc[HD:P, K_HO, 1] = 1
    kc[:, K_HO, K_PAIR:K_PAIR + 2] = kc[:, K_HO, 0:2]
    kc[:, K_IOTA] = i[None, :]
    kc[:, K_HO, 2] = i
    km = np.zeros((P, 5, P), np.float32)
    km[:, 0] = np.eye(P)
    km[:, 1] = np.where(i[None, :] > i[:, None], NEG, 0)
    km[:, 2] = np.where(i[:, None] > i[None, :], NEG, 0)
    km[:, 3] = np.where(i[:, None] >= i[None, :], NEG, 0)
    km[:, 4] = i[:, None] < i[None, :]
    return kc, km.astype(bf16)


def layout(np, inputs):
    a = {k: np.asarray(v)[0] if k != "x" else np.asarray(v)[0] for k, v in inputs.items()}

    def cols(v):
        return np.ascontiguousarray(v.reshape(-1, P).T)

    def rows(v):
        return np.broadcast_to(v[None, :], (P, v.shape[0]))

    prm = np.concatenate([cols(a["attn_norm"]), cols(a["ffn_norm"]), rows(a["fox_q_norm"]), rows(a["fox_k_norm"]),
                          rows(a["fox_o_norm"]), rows(a["gdn_o_norm"]), rows(a["gla_o_norm"]), rows(a["fox_f_bias"]),
                          rows(a["gdn_dt_bias"]), rows(a["gdn_a_log"]),
                          a["gdn_conv"].reshape(4, 9, P).transpose(2, 1, 0).reshape(P, 36),
                          rows(a["b_router_group"]), rows(a["b_router_expert"]), rows(a["gla_b_a"])], axis=1)
    return {
        "x": a["x"], "w_in": a["w_in"], "w_out": a["w_out"],
        "w_router": np.concatenate([a["w_router_group"], a["w_router_expert"]], axis=1),
        "w_a2": a["gla_w_a2"], "w_g": a["w_expert_gate"], "w_u": a["w_expert_up"], "w_d": a["w_expert_down"],
        "params": np.ascontiguousarray(prm),
    }


def kernel(**inputs):
    import numpy as np
    import ml_dtypes
    import concourse.bacc as bacc
    from concourse.bass_utils import run_bass_kernel_spmd

    nc = bacc.Bacc("TRN2", target_bir_lowering=False, num_devices=1)
    data = layout(np, inputs)
    data["consts"], data["masks"] = shape_constants(np, ml_dtypes.bfloat16)
    arrays, args = {}, {}
    for name, v in data.items():
        v = np.ascontiguousarray(v)
        arrays["in_" + name] = v
        args[name] = nc.dram_tensor("in_" + name, v.shape, mybir.dt.from_np(v.dtype), kind="ExternalInput").ap()
    out = nc.dram_tensor("out_0", (S, D), F32, kind="ExternalOutput").ap()
    trunk_kernel(nc, out=out, **args)
    r = run_bass_kernel_spmd(nc, [arrays], core_ids=[0])
    return r.results[0]["out_0"].reshape(1, S, D)
```
